# Optimizing a Trainium2 kernel written in Bass

```python
import math
import jax, jax.numpy as jnp
from jax import lax
import numpy as np

D_MODEL = 1024
BATCH = 1
SEQ = 512
DEPTH = 2

N_BRANCH = 3
BRANCH_DIM = D_MODEL
CONV_DIM = BRANCH_DIM
CONV_WIDTH = 3
MLSTM_HEADS = 8
MLSTM_DV = BRANCH_DIM // MLSTM_HEADS
MLSTM_DK = MLSTM_DV // 2
MLSTM_CHUNK = 128
GATE_CAP = 15.0
MLA_NOPE = 128
MLA_ROPE = 64
MLA_V = 128
MLA_HEADS = BRANCH_DIM // MLA_V
Q_LORA = D_MODEL // 4
KV_LORA = D_MODEL // 8
ROPE_BASE = 10000.0
ATTN_BLOCK = 128
D_FF = 4 * D_MODEL
NORM_EPS = 1e-6

IN_SPLITS = (
    CONV_DIM, CONV_DIM, CONV_DIM,
    MLSTM_HEADS * MLSTM_DK, MLSTM_HEADS * MLSTM_DK,
    MLSTM_HEADS * MLSTM_DV, MLSTM_HEADS * MLSTM_DV,
    MLSTM_HEADS, MLSTM_HEADS,
    Q_LORA, KV_LORA, MLA_ROPE,
    N_BRANCH * D_MODEL,
)
IN_DIM = (3 * CONV_DIM + 2 * MLSTM_HEADS * MLSTM_DK + 2 * MLSTM_HEADS * MLSTM_DV + 2 * MLSTM_HEADS
          + Q_LORA + KV_LORA + MLA_ROPE + N_BRANCH * D_MODEL)

kernel_name = 'hybrid_conv_mlstm_mla_gated_block'

def rms_norm(x, g):
    xf = x.astype(jnp.float32)
    y = xf * lax.rsqrt(jnp.mean(xf * xf, axis=-1, keepdims=True) + NORM_EPS)
    return (y * g.astype(jnp.float32)).astype(x.dtype)

def rope_tables(positions):
    inv_freq = ROPE_BASE ** (-jnp.arange(0, MLA_ROPE, 2, dtype=jnp.float32) / MLA_ROPE)
    ang = positions.astype(jnp.float32)[..., None] * inv_freq
    return jnp.cos(ang), jnp.sin(ang)

def apply_rope(x, cos, sin):
    half = MLA_ROPE // 2
    xf = x.astype(jnp.float32)
    x1, x2 = xf[..., :half], xf[..., half:]
    out = jnp.concatenate([x1 * cos - x2 * sin, x1 * sin + x2 * cos], axis=-1)
    return out.astype(x.dtype)

def split_columns(proj):
    idx = np.cumsum(np.array(IN_SPLITS))[:-1].tolist()
    return jnp.split(proj, idx, axis=-1)

def soft_cap(z):
    return GATE_CAP * jnp.tanh(z / GATE_CAP)

def short_conv_mixer(gate_b, gate_c, u, conv_w):
    z = gate_c * u
    zc = lax.conv_general_dilated(
        z, conv_w[:, None, :].astype(z.dtype), window_strides=(1,),
        padding=[(CONV_WIDTH - 1, 0)],
        dimension_numbers=('NWC', 'WIO', 'NWC'),
        feature_group_count=CONV_DIM)
    return gate_b * zc

def mlstm_mixer(q, k, v, o_pre, i_pre, f_pre, b_i, b_f, head_norm):
    bsz, seq = q.shape[:2]
    nc, L = seq // MLSTM_CHUNK, MLSTM_CHUNK
    f32 = jnp.float32

    def heads(t, d):
        return t.astype(f32).reshape(bsz, nc, L, MLSTM_HEADS, d).transpose(0, 3, 1, 2, 4)

    qh = heads(q, MLSTM_DK) * (MLSTM_DK ** -0.5)
    kh = heads(k, MLSTM_DK)
    vh = heads(v, MLSTM_DV)
    log_i = soft_cap(i_pre.astype(f32) + b_i.astype(f32))
    log_f = jax.nn.log_sigmoid(soft_cap(f_pre.astype(f32) + b_f.astype(f32)))
    log_i = log_i.reshape(bsz, nc, L, MLSTM_HEADS).transpose(0, 3, 1, 2)
    log_f = log_f.reshape(bsz, nc, L, MLSTM_HEADS).transpose(0, 3, 1, 2)

    b = jnp.cumsum(log_f, axis=-1)
    b_last = b[..., -1]
    a = b_last[..., None] - b + log_i
    m_loc = jnp.max(a, axis=-1)
    w = jnp.exp(a - m_loc[..., None])
    c_loc = jnp.einsum('bhcs,bhcsk,bhcsv->bhckv', w, kh, vh)
    n_loc = jnp.einsum('bhcs,bhcsk->bhck', w, kh)

    def step(carry, xs):
        c_st, n_st, m_st = carry
        bl, ml, cl, nl = xs
        m_new = jnp.maximum(bl + m_st, ml)
        s_old = jnp.exp(bl + m_st - m_new)
        s_loc = jnp.exp(ml - m_new)
        c_new = s_old[..., None, None] * c_st + s_loc[..., None, None] * cl
        n_new = s_old[..., None] * n_st + s_loc[..., None] * nl
        return (c_new, n_new, m_new), (c_st, n_st, m_st)

    init = (jnp.zeros((bsz, MLSTM_HEADS, MLSTM_DK, MLSTM_DV), f32),
            jnp.zeros((bsz, MLSTM_HEADS, MLSTM_DK), f32),
            jnp.zeros((bsz, MLSTM_HEADS), f32))
    xs = (jnp.moveaxis(b_last, 2, 0), jnp.moveaxis(m_loc, 2, 0),
          jnp.moveaxis(c_loc, 2, 0), jnp.moveaxis(n_loc, 2, 0))
    _, (c_prev, n_prev, m_prev) = lax.scan(step, init, xs)
    c_prev = jnp.moveaxis(c_prev, 0, 2)
    n_prev = jnp.moveaxis(n_prev, 0, 2)
    m_prev = jnp.moveaxis(m_prev, 0, 2)

    g = b + m_prev[..., None]
    d = b[..., :, None] - b[..., None, :] + log_i[..., None, :]
    causal = jnp.tril(jnp.ones((L, L), dtype=bool))
    d = jnp.where(causal, d, -jnp.inf)
    m_t = jnp.maximum(g, jnp.max(d, axis=-1))
    inter = jnp.exp(g - m_t)
    s = jnp.einsum('bhctk,bhcsk->bhcts', qh, kh) * jnp.exp(d - m_t[..., None])
    num = inter[..., None] * jnp.einsum('bhctk,bhckv->bhctv', qh, c_prev) + jnp.einsum('bhcts,bhcsv->bhctv', s, vh)
    den = inter * jnp.einsum('bhctk,bhck->bhct', qh, n_prev) + jnp.sum(s, axis=-1)
    h = num / jnp.maximum(jnp.abs(den), jnp.exp(-m_t))[..., None]
    h = h.transpose(0, 2, 3, 1, 4).reshape(bsz, seq, MLSTM_HEADS, MLSTM_DV)
    h = rms_norm(h, head_norm.reshape(MLSTM_HEADS, MLSTM_DV))
    h = h.reshape(bsz, seq, MLSTM_HEADS * MLSTM_DV) * jax.nn.sigmoid(o_pre.astype(f32))
    return h.astype(q.dtype)

def blocked_causal_attention(q, k, v):
    bsz, nh, seq, dh = q.shape
    nb = seq // ATTN_BLOCK
    scale = dh ** -0.5
    qb = q.reshape(bsz, nh, nb, ATTN_BLOCK, dh).transpose(2, 0, 1, 3, 4)
    key_idx = jnp.arange(seq)

    def one_block(args):
        qi, bi = args
        sc = jnp.einsum('bhqd,bhkd->bhqk', qi, k).astype(jnp.float32) * scale
        q_idx = bi * ATTN_BLOCK + jnp.arange(ATTN_BLOCK)
        sc = jnp.where(key_idx[None, :] <= q_idx[:, None], sc, -jnp.inf)
        p = jax.nn.softmax(sc, axis=-1)
        return jnp.einsum('bhqk,bhkd->bhqd', p.astype(v.dtype), v)

    out = lax.map(one_block, (qb, jnp.arange(nb)))
    return out.transpose(1, 2, 0, 3, 4).reshape(bsz, nh, seq, v.shape[-1])

def mla_mixer(c_q, c_kv, k_rope, q_a_norm, w_uq, kv_a_norm, w_ukv, q_norm, k_norm, cos, sin):
    bsz, seq = c_q.shape[:2]
    q = (rms_norm(c_q, q_a_norm) @ w_uq).reshape(bsz, seq, MLA_HEADS, MLA_NOPE + MLA_ROPE)
    kv = (rms_norm(c_kv, kv_a_norm) @ w_ukv).reshape(bsz, seq, MLA_HEADS, MLA_NOPE + MLA_V)
    q_nope = rms_norm(q[..., :MLA_NOPE], q_norm[:MLA_NOPE])
    q_pe = apply_rope(rms_norm(q[..., MLA_NOPE:], q_norm[MLA_NOPE:]), cos[:, :, None, :], sin[:, :, None, :])
    k_nope = rms_norm(kv[..., :MLA_NOPE], k_norm[:MLA_NOPE])
    v = kv[..., MLA_NOPE:]
    k_pe = apply_rope(rms_norm(k_rope, k_norm[MLA_NOPE:]), cos, sin)
    k_pe = jnp.broadcast_to(k_pe[:, :, None, :], (bsz, seq, MLA_HEADS, MLA_ROPE))
    qh = jnp.concatenate([q_nope, q_pe], axis=-1).transpose(0, 2, 1, 3)
    kh = jnp.concatenate([k_nope, k_pe], axis=-1).transpose(0, 2, 1, 3)
    vh = v.transpose(0, 2, 1, 3)
    o = blocked_causal_attention(qh, kh, vh)
    return o.transpose(0, 2, 1, 3).reshape(bsz, seq, MLA_HEADS * MLA_V)

def hybrid_layer(x, cos, sin, mix_norm, w_in, conv_w, b_i, b_f, head_norm,
                 q_a_norm, w_uq, kv_a_norm, w_ukv, q_norm, k_norm,
                 w_branch, w_out, mlp_norm, w_up, w_down):
    bsz, seq = x.shape[:2]
    xn = rms_norm(x, mix_norm)
    (cb, cc, cu, mq, mk, mv, mo, mi, mf, cq, ckv, krope, gate_pre) = split_columns(xn @ w_in)
    y_a = short_conv_mixer(cb, cc, cu, conv_w)
    y_b = mlstm_mixer(mq, mk, mv, mo, mi, mf, b_i, b_f, head_norm)
    y_c = mla_mixer(cq, ckv, krope, q_a_norm, w_uq, kv_a_norm, w_ukv, q_norm, k_norm, cos, sin)
    ys = jnp.stack([y_a, y_b, y_c], axis=0)
    branch = jnp.einsum('nbsc,ncd->nbsd', ys, w_branch)
    gates = jax.nn.sigmoid(gate_pre.reshape(bsz, seq, N_BRANCH, D_MODEL))
    merged = jnp.einsum('bsnd,nbsd->bsd', gates, branch)
    x = x + merged @ w_out
    h = rms_norm(x, mlp_norm)
    x = x + jnp.square(jax.nn.relu(h @ w_up)) @ w_down
    return x

def setup_inputs(seed: int = 0) -> dict:
    key = jax.random.key(seed)
    ks = jax.random.split(key, 24)
    f32 = jnp.float32

    def nrm(k, shape, scale):
        return jax.random.normal(k, shape, f32) * scale

    def gain(k, shape):
        return 1.0 + 0.1 * jax.random.normal(k, shape, f32)

    x = jax.random.normal(ks[0], (BATCH, SEQ, D_MODEL), f32)
    offsets = jax.random.randint(ks[1], (BATCH, 1), 0, 4096, dtype=jnp.int32)
    positions = (offsets + jnp.arange(SEQ, dtype=jnp.int32)[None, :]).astype(jnp.int32)
    f_bias = jnp.linspace(3.0, 6.0, MLSTM_HEADS, dtype=f32)[None, :] + 0.1 * jax.random.normal(ks[5], (DEPTH, MLSTM_HEADS), f32)
    return {
        'x': x,
        'positions': positions,
        'mix_norm': gain(ks[2], (DEPTH, D_MODEL)),
        'w_in': nrm(ks[3], (DEPTH, D_MODEL, IN_DIM), D_MODEL ** -0.5),
        'conv_w': nrm(ks[4], (DEPTH, CONV_WIDTH, CONV_DIM), CONV_WIDTH ** -0.5),
        'mlstm_igate_bias': nrm(ks[6], (DEPTH, MLSTM_HEADS), 0.1),
        'mlstm_fgate_bias': f_bias,
        'mlstm_head_norm': gain(ks[7], (DEPTH, MLSTM_HEADS * MLSTM_DV)),
        'mla_q_a_norm': gain(ks[8], (DEPTH, Q_LORA)),
        'mla_w_uq': nrm(ks[9], (DEPTH, Q_LORA, MLA_HEADS * (MLA_NOPE + MLA_ROPE)), Q_LORA ** -0.5),
        'mla_kv_a_norm': gain(ks[10], (DEPTH, KV_LORA)),
        'mla_w_ukv': nrm(ks[11], (DEPTH, KV_LORA, MLA_HEADS * (MLA_NOPE + MLA_V)), KV_LORA ** -0.5),
        'mla_q_norm': gain(ks[12], (DEPTH, MLA_NOPE + MLA_ROPE)),
        'mla_k_norm': gain(ks[13], (DEPTH, MLA_NOPE + MLA_ROPE)),
        'w_branch': nrm(ks[14], (DEPTH, N_BRANCH, BRANCH_DIM, D_MODEL), BRANCH_DIM ** -0.5),
        'w_out': nrm(ks[15], (DEPTH, D_MODEL, D_MODEL), D_MODEL ** -0.5),
        'mlp_norm': gain(ks[16], (DEPTH, D_MODEL)),
        'w_up': nrm(ks[17], (DEPTH, D_MODEL, D_FF), D_MODEL ** -0.5),
        'w_down': nrm(ks[18], (DEPTH, D_FF, D_MODEL), D_FF ** -0.5),
    }

def reference(x, positions, mix_norm, w_in, conv_w, mlstm_igate_bias, mlstm_fgate_bias,
              mlstm_head_norm, mla_q_a_norm, mla_w_uq, mla_kv_a_norm, mla_w_ukv,
              mla_q_norm, mla_k_norm, w_branch, w_out, mlp_norm, w_up, w_down):
    cos, sin = rope_tables(positions)
    for l in range(DEPTH):
        x = hybrid_layer(x, cos, sin, mix_norm[l], w_in[l], conv_w[l],
                         mlstm_igate_bias[l], mlstm_fgate_bias[l], mlstm_head_norm[l],
                         mla_q_a_norm[l], mla_w_uq[l], mla_kv_a_norm[l], mla_w_ukv[l],
                         mla_q_norm[l], mla_k_norm[l], w_branch[l], w_out[l],
                         mlp_norm[l], w_up[l], w_down[l])
    return x


_drawn_inputs = setup_inputs


def setup_inputs(seed=0):
    import zlib

    import numpy as np

    out = dict(_drawn_inputs(seed))
    spreads = {}
    factors = {'mlstm_igate_bias': 64.0,
     'mla_q_a_norm': 5.599,
     'mla_kv_a_norm': 2.986,
     'mla_q_norm': 5.677,
     'mla_k_norm': 5.512}
    for name, (base, spread) in spreads.items():
        noise = np.random.default_rng([zlib.crc32(name.encode()), seed]).standard_normal(out[name].shape)
        drawn = base * np.exp(spread * noise) if base else spread * noise
        out[name] = __import__('jax').numpy.asarray(drawn.astype(out[name].dtype))
    for name, factor in factors.items():
        out[name] = (out[name] * factor).astype(out[name].dtype)
    return out
```

```python
import math
from contextlib import ExitStack

import numpy as np
import concourse.bass as bass
from concourse import mybir

D_MODEL, SEQ, DEPTH = 1024, 512, 2
P = 128
KT = D_MODEL // P
TC = SEQ // P
HEADS = 8
DK, DV = 64, 128
NOPE, ROPE = 128, 64
Q_LORA, KV_LORA = 256, 128
D_FF = 4096
FG = D_FF // D_MODEL
EPS = 1e-6
GATE_CAP = 15.0
BIG = 1e30

C_CB, C_CC, C_CU = 0, 1024, 2048
C_MQ, C_MK, C_MV, C_MO = 3072, 3584, 4096, 5120
C_MI, C_MF, C_CQ, C_CKV, C_KR, C_GATE = 6144, 6152, 6160, 6416, 6544, 6608

U_PRE, U_HEAD, U_MERGE, U_OUT, U_MLP = 4, 8, 16, 8, 16
UNITS = U_PRE + HEADS * U_HEAD + 3 * U_MERGE + U_OUT + FG * U_MLP
B_HEAD = U_PRE
B_MERGE = B_HEAD + HEADS * U_HEAD
B_OUT = B_MERGE + 3 * U_MERGE
B_MLP = B_OUT + U_OUT
STAGES, WSLOTS = 2, 4

PAR = {}
_at = 0
for _n, _w in (("mix_next", KT), ("mlp", KT), ("conv", KT * 3), ("head", KT), ("qa", 2), ("kva", 1),
               ("q_nope", 1), ("k_nope", 1), ("q_rope", 1), ("k_rope", 1), ("b_i", 1), ("b_f", 1)):
    PAR[_n] = _at
    _at += _w
NPAR = _at
CST = {}
_at = 0
for _n, _w in (("ident", P), ("after", P), ("future", P), ("swap", P), ("onehot", HEADS), ("freq", 1),
               ("sign", 1), ("mix0", KT)):
    CST[_n] = _at
    _at += _w
NCST = _at

USES = {
    "q_nope": (2, 0), "score0": (2, 1), "pt0": (2, 2),
    "k_nope": (3, 0), "score1": (3, 1), "pt1": (3, 2),
    "q_rope": (4, 0), "score2": (4, 1), "pt2": (4, 2),
    "v_t": (5, 0), "stat_q": (5, 1), "stat_r": (5, 2), "score3": (5, 3), "pv": (5, 4),
    "m_bc": (6, 0), "k_tr": (6, 1), "vm_tr": (6, 2), "stat_k": (6, 3), "num1": (6, 4), "v_tr": (6, 5),
    "i_bc": (7, 0), "s_t": (7, 1), "c_loc": (7, 2), "num0": (7, 3), "h_tr": (7, 4),
}
BY_UNIT = ("q_rope", "v_t")
PRE_USE = {"stat_x": 2, "stat_kv": 3, "stat_cq": 4, "stat_kr": 5, "rot_kr": 6, "rows_tr": 7}
POST_USE = {"stat_h": 2}


def _per(bank, fills=False):
    return sum(1 for n, (b, _) in USES.items() if b == bank and not (fills and n in BY_UNIT))


def _nth(name, fills=False):
    b, k = USES[name]
    return k - (sum(1 for n in BY_UNIT if USES[n][0] == b and USES[n][1] < k) if fills else 0)


def _layer(bank, fills=False):
    return (HEADS * _per(bank, fills) + (bank in PRE_USE.values()) + (bank in POST_USE.values()))


def build_trunk(nc, x_in, pos_in, wstream, par_in, cst_in, out):
    f32, f32r, i32 = mybir.dt.float32, mybir.dt.float32r, mybir.dt.int32
    ALU, ACT, AX = mybir.AluOpType, mybir.ActivationFunctionType, mybir.AxisListType
    ctx = ExitStack()
    V, S, T, G = nc.vector, nc.scalar, nc.tensor, nc.gpsimd

    top = [16512]
    names = {}

    def place(name, shape, dt=f32, at=None):
        size = 4 * int(np.prod(shape[1:]))
        if at is None:
            at = top[0]
            top[0] += (size + 31) // 32 * 32
        names[name] = at
        return nc.alloc_sbuf_tensor_at(name, shape, dt, offset=at)

    xT = place("xT", [P, KT, SEQ])
    xg_hi = place("xg_hi", [P, KT, SEQ], f32r)
    xg_lo = place("xg_lo", [P, KT, SEQ], f32r)
    ysA = place("ysA", [P, KT, SEQ])
    ysB = place("ysB", [P, KT, SEQ])
    ysC = place("ysC", [P, KT, SEQ])
    merged = place("merged", [P, KT, SEQ], at=names["ysA"])
    mg_hi = place("mg_hi", [P, KT, SEQ], f32r, at=names["ysB"])
    mg_lo = place("mg_lo", [P, KT, SEQ], f32r, at=names["ysC"])
    x_tok = place("x_tok", [P, TC, D_MODEL], at=names["ysA"])
    out_tok = place("out_tok", [P, TC, D_MODEL], at=names["ysB"])
    stage = place("stage", [P, STAGES, 1024])
    whi = place("whi", [P, WSLOTS, 1024], f32r)
    wlo = place("wlo", [P, WSLOTS, 1024], f32r)

    cst = place("cst", [P, NCST])
    par = place("par", [P, NPAR])
    ones = place("ones", [P, P])
    after_r = place("after_r", [P, SEQ], f32r)
    ident_r = place("ident_r", [P, P], f32r)
    cs = place("cs", [P, SEQ])
    gcs = place("gcs", [P, SEQ])
    eps = place("eps", [P, 1])
    halfpi = place("halfpi", [P, 1])
    cq_hi = place("cq_hi", [P, 2, SEQ], f32r)
    cq_lo = place("cq_lo", [P, 2, SEQ], f32r)
    ckv_hi = place("ckv_hi", [P, SEQ], f32r)
    ckv_lo = place("ckv_lo", [P, SEQ], f32r)
    kpe = place("kpe", [ROPE, SEQ])
    rows_mi = place("rows_mi", [40, SEQ])
    acol = place("acol", [P, TC, HEADS])
    emt = place("emt", [P, TC, HEADS])
    rstd = place("rstd", [P, SEQ])
    ssum = place("ssum", [P, SEQ])
    tmp0 = top[0]
    sqx = place("sqx", [P, SEQ])
    ev_t = place("ev_t", [P, SEQ])
    ev_r = place("ev_r", [P, SEQ])
    ev_n = place("ev_n", [P, SEQ])
    gsig = [ev_t, ev_r]
    tmp_end = top[0]
    act_hi = place("act_hi", [P, KT, SEQ], f32r)
    act_lo = place("act_lo", [P, KT, SEQ], f32r)
    act0 = names["act_hi"]
    end = top[0]

    top[0] = tmp0
    prob = place("prob", [P, 1280])
    so = place("so", [P, SEQ])
    kw = place("kw", [P, TC, DK])
    assert top[0] <= tmp_end
    top[0] = act0
    nq = place("nq", [P, SEQ])
    nk = place("nk", [P, SEQ])
    nr = place("nr", [ROPE, SEQ])
    prob_t = place("prob_t", [P, 1280], at=names["nq"])
    qsb = place("qsb", [DK, SEQ])
    ksb = place("ksb", [DK, SEQ])
    v_ch = place("v_ch", [P, SEQ])
    vm_ch = place("vm_ch", [P, SEQ])
    htok = place("htok", [P, TC, DV], at=names["vm_ch"])
    mi = place("mi", [40, SEQ])
    qs = place("qs", [DK, SEQ])
    dec = place("dec", [P, TC, P])
    qpe = place("qpe", [ROPE, SEQ])
    cb = place("cb", [P, SEQ])
    cc = place("cc", [P, SEQ])
    vmt = place("vmt", [P, TC, DV + 1])
    v_tok = place("v_tok", [P, TC, DV])
    assert top[0] <= end, (top[0], end)
    top[0] = end
    zp = place("zp", [P, SEQ + 2])
    csb = place("csb", [DK, TC - 1, DV + 1], at=names["ssum"])
    sold = place("sold", [DK, TC], at=names["ssum"] + 1568)
    sm = place("sm", [P, 16, TC], at=names["ssum"] + 1600)
    end = top[0]
    assert end <= 229368, end
    MX, NM, SUM, RINV, SS, DEN, ADEN, DD, RR, R2, TT, LN, HR, FF = range(14)

    top[0] = act0
    cq_raw = place("cq_raw", [P, 2, SEQ])
    ckv_raw = place("ckv_raw", [P, SEQ])
    kr_raw = place("kr_raw", [ROPE, SEQ])
    sq_cq = place("sq_cq", [P, 2, SEQ])
    sq_ckv = place("sq_ckv", [P, SEQ])
    sq_kr = place("sq_kr", [ROPE, SEQ])
    r_i = place("r_i", [HEADS, SEQ])
    r_f = place("r_f", [HEADS, SEQ])
    r_nb = place("r_nb", [HEADS, SEQ])
    r_a = place("r_a", [HEADS, SEQ])
    r_d = place("r_d", [HEADS, SEQ])
    m_prev = place("m_prev", [HEADS, TC + 1])
    assert top[0] <= act0 + 2 * KT * SEQ * 4
    top[0] = act0
    pos_i = place("pos_i", [P, SEQ], i32)
    ang = place("ang", [P, SEQ])
    turns = place("turns", [P, SEQ])
    red = place("red", [P, SEQ])

    bank = [ctx.enter_context(nc.psum_tensor(f"bank{b}", [P, 512], f32)) for b in range(8)]

    def col(name, k=0, w=1):
        return cst[:, CST[name] + k:CST[name] + k + w]

    def gain(name, k=0, rows=slice(0, P)):
        return par[rows, PAR[name] + k:PAR[name] + k + 1]

    ident = cst[:, CST["ident"]:CST["ident"] + P]

    def sem(name):
        return ctx.enter_context(nc.semaphore(name))

    stage_in = [sem(f"stage_in{s}") for s in range(STAGES)]
    hi_ready = sem("hi_ready")
    w_ready = sem("w_ready")
    unit_done = sem("unit_done")
    taken = [sem(f"bank{b}_taken") for b in range(8)]
    filled = [sem(f"bank{b}_filled") for b in range(8)]
    cst_in_s, x_in_s, pos_in_s, par_in_s = sem("cst_in"), sem("x_in"), sem("pos_in"), sem("par_in")
    out_s = sem("out_stored")
    consts = sem("consts_ready")
    trig = sem("trig_step")
    trig_done = sem("trig_done")
    xt_filled, xt_taken = sem("x_transposed"), sem("x_transpose_taken")
    x_sq = sem("x_squared")
    ss_add = sem("ssum_added")
    xg_hi_s = sem("xg_hi_ready")
    xg_ready = sem("xg_ready")
    rs_step = sem("rstd_step")
    nw = sem("newton_step")
    pre_raw = sem("pre_raw")
    pre_sq = sem("pre_squared")
    pre_rs = sem("pre_rstd")
    pre_n = sem("pre_normed")
    row_v, row_s = sem("rows_vector"), sem("rows_scalar")
    head_in = sem("head_inputs")
    mi_s = sem("mi_ready")
    q_s = sem("mlstm_q_ready")
    qs_s = sem("qs_ready")
    kw_s = sem("kw_step")
    dec_s = sem("dec_step")
    vt_s = sem("num_half_read")
    sq_s = sem("mla_squared")
    rs_s = sem("mla_rstd")
    c_s = sem("c_state_step")
    rope_s = sem("rope_step")
    mx_s, nm_s, rinv_s, p_s = sem("score_max"), sem("neg_max"), sem("prob_sum_inv"), sem("prob_ready")
    ex_s = sem("prob_exp")
    ss_s, fin_s, hr_s = sem("num_squared"), sem("num_step"), sem("head_rstd")
    h_s = sem("htok_step")
    so_s = sem("o_gate_ready")
    conv_s = sem("conv_step")
    act_a = sem("act_value")
    act_h = sem("act_hi_ready")
    act_s = sem("act_ready")
    g_s = sem("gate_ready")
    mg_a = sem("merge_sum")
    mg_h = sem("mg_hi_ready")
    mg_s = sem("merged_ready")

    block = ctx.enter_context(nc.Block())

    N_CONSTS = 5 + 1 + TC
    N_TRIG = 12
    PRE_N, ROW_V = 12, 20

    ACC_L = (U_PRE + HEADS * 6 + 3 * U_MERGE + U_OUT + FG * U_MLP) // 2
    A_HEAD = U_PRE // 2
    A_MERGE = A_HEAD + HEADS * 3
    A_OUT = A_MERGE + 3 * U_MERGE // 2
    A_MLP = A_OUT + U_OUT // 2

    def unit(l, base, i=0, per=0, j=0):
        return l * UNITS + i * per + (base + j)

    def used(l, i, name):
        b, _ = USES[name]
        return l * _layer(b) + i * _per(b) + (1 + _nth(name))

    def w_filled(e, l, i, name):
        b, _ = USES[name]
        e.wait_ge(filled[b], l * _layer(b, True) + i * _per(b, True) + (1 + _nth(name, True)) + 1)

    def w_taken(e, l, i, name):
        e.wait_ge(taken[USES[name][0]], used(l, i, name) + 2)

    def w_free(e, l, i, name):
        e.wait_ge(taken[USES[name][0]], used(l, i, name) + 1)

    def w_unit(e, u):
        e.wait_ge(unit_done, u + (1 + WSLOTS))

    def w_acc(e, b, n):
        e.wait_ge(taken[b], n + 2)

    @block.sync
    def _(sp):
        sp.dma_start(cst[:, :], cst_in).then_inc(cst_in_s, 16)
        sp.dma_start(x_tok[:, :, :], x_in.rearrange("(c p) d -> p c d", p=P)).then_inc(x_in_s, 16)
        with sp.Fori(0, DEPTH * UNITS // STAGES) as i:
            for s in range(STAGES):
                sp.wait_ge(w_ready, i * STAGES + (s + 1))
                sp.dma_start(stage[:, s, :], wstream[i * STAGES + s, :, :]).then_inc(stage_in[s], 16)
        sp.wait_ge(xt_taken, 2 * KT)
        sp.dma_start(out.rearrange("(c p) d -> p c d", p=P), out_tok[:, :, :]).then_inc(out_s, 16)
        sp.wait_ge(out_s, 16)

    @block.gpsimd
    def _(pool):
        pool.sem_inc(w_ready, STAGES)
        pool.sem_inc(unit_done, WSLOTS)
        for b in range(8):
            pool.sem_inc(taken[b], 1)
        G.memset(ones[:, :], 1.0).then_inc(consts, 1)
        G.memset(eps[:, :], EPS).then_inc(consts, 1)
        G.memset(halfpi[:, :], math.pi / 2).then_inc(consts, 1)
        G.memset(rows_mi[:, :], 0.0).then_inc(consts, 1)
        G.memset(zp[:, 0:2], 0.0).then_inc(consts, 1)
        with pool.Fori(0, DEPTH * UNITS // WSLOTS) as i:
            for j in range(WSLOTS):
                pool.wait_ge(hi_ready, i * WSLOTS + (j + 1))
                G.tensor_tensor(wlo[:, j, :], stage[:, j % STAGES, :], whi[:, j, :].bitcast(f32),
                                ALU.subtract).then_inc(w_ready, 1)

    @block.tensor
    def _(pe):
        def split_mm(acc, w, hi, lo, first, last):
            T.matmul(acc, w[0], hi, start=first, stop=False)
            T.matmul(acc, w[0], lo, start=False, stop=False)
            return T.matmul(acc, w[1], hi, start=False, stop=last)

        def project(u, slot, b, n, hi, lo, tile_ready=None):
            pe.wait_ge(w_ready, u + (1 + STAGES))
            pe.wait_ge(taken[b], n + 1)
            for k in range(KT):
                if tile_ready is not None:
                    pe.wait_ge(tile_ready[0], tile_ready[1] + (k + 1))
                w = (whi[:, slot, k * P:(k + 1) * P], wlo[:, slot, k * P:(k + 1) * P])
                last = split_mm(bank[b][:, :], w, hi[:, k, :], lo[:, k, :], k == 0, k == KT - 1)
            last.then_inc(unit_done, 1)

        pe.wait_ge(cst_in_s, 16)
        pe.wait_ge(x_in_s, 16)
        for k in range(KT):
            if k >= 2:
                pe.wait_ge(xt_taken, k - 1)
            for c in range(TC):
                last = T.transpose(bank[k % 2][:, c * P:(c + 1) * P], x_tok[:, c, k * P:(k + 1) * P], ident)
            last.then_inc(xt_filled, 1)
        pe.wait_ge(consts, N_CONSTS)
        pe.wait_ge(xt_taken, KT)

        with pe.Fori(0, DEPTH) as l:
            for j in range(U_PRE):
                project(unit(l, 0, j=j), j % WSLOTS, j % 2, l * ACC_L + j // 2, xg_hi, xg_lo,
                        (xg_ready, l * 2 * KT) if j == 0 else None)
                if j == 0:
                    pe.wait_ge(ss_add, l * 2 * (KT - 1) + (KT - 1))
                    pe.wait_ge(taken[2], l * _layer(2) + 1)
                    T.matmul(bank[2][:, :], ones[:, :], ssum[:, :], start=True, stop=True).then_inc(filled[2], 1)
            pe.wait_ge(pre_sq, l * 4 + 1)
            pe.wait_ge(taken[5], l * _layer(5) + 1)
            T.matmul(bank[5][:, :], ones[0:ROPE, :], sq_kr[:, :], start=True, stop=True).then_inc(filled[5], 1)
            pe.wait_ge(pre_sq, l * 4 + 2)
            pe.wait_ge(taken[3], l * _layer(3) + 1)
            T.matmul(bank[3][:, :], ones[:, :], sq_ckv[:, :], start=True, stop=True).then_inc(filled[3], 1)
            pe.wait_ge(pre_sq, l * 4 + 4)
            pe.wait_ge(taken[4], l * _layer(4) + 1)
            T.matmul(bank[4][:, :], ones[:, :], sq_cq[:, 0, :], start=True, stop=False)
            T.matmul(bank[4][:, :], ones[:, :], sq_cq[:, 1, :], start=False, stop=True).then_inc(filled[4], 1)
            pe.wait_ge(row_v, l * ROW_V + ROW_V)
            pe.wait_ge(taken[7], l * _layer(7) + 1)
            pe.wait_ge(pre_n, l * PRE_N + 2)
            pe.wait_ge(taken[6], l * _layer(6) + 1)
            T.matmul(bank[6][:, :], col("swap", 0, P)[0:ROPE, :], kr_raw[:, :], start=True, stop=True).then_inc(filled[6], 1)
            for c in range(TC):
                T.transpose(bank[7][:, c * 8:c * 8 + 8], r_a[:, c * P:(c + 1) * P], ident[0:8, 0:8])
            for c in range(TC):
                last = T.transpose(bank[7][:, 32 + c * 8:40 + c * 8], r_d[:, c * P:(c + 1) * P], ident[0:8, 0:8])
            last.then_inc(filled[7], 1)

            with pe.Fori(0, HEADS) as i:
                def free(name):
                    w_free(pe, l, i, name)

                def fill(name, ins):
                    ins.then_inc(filled[USES[name][0]], 1)

                def head_unit(j, slot, b, n):
                    project(unit(l, B_HEAD, i, U_HEAD, j), slot, b, l * ACC_L + i * 3 + (A_HEAD + n), xg_hi, xg_lo)

                head_unit(0, 0, 0, 0)
                pe.wait_ge(mi_s, l * HEADS + i + 1)
                free("m_bc")
                T.matmul(bank[6][:, :], ones[0:8, :], mi[0:8, :], start=True, stop=False)
                fill("m_bc", T.matmul(bank[6][:, :], ident_r[:, :], after_r[:, :], start=False, stop=True))
                free("i_bc")
                fill("i_bc", T.matmul(bank[7][0:DK, :], ones[32:40, 0:DK], mi[32:40, :], start=True, stop=True))
                head_unit(1, 1, 1, 0)
                w_acc(pe, 0, l * ACC_L + i * 3 + A_HEAD)
                free("k_tr")
                free("s_t")
                for c in range(TC):
                    last = T.matmul(bank[7][:, c * P:(c + 1) * P], ksb[:, c * P:(c + 1) * P], qsb[:, c * P:(c + 1) * P],
                                    start=True, stop=True)
                fill("s_t", last)
                for c in range(TC):
                    last = T.transpose(bank[6][:, c * DK:(c + 1) * DK], ksb[:, c * P:(c + 1) * P], ident[0:DK, 0:DK])
                fill("k_tr", last)
                pe.wait_ge(w_ready, unit(l, B_HEAD, i, U_HEAD, 2) + (1 + STAGES))
                pe.wait_ge(pre_n, l * PRE_N + PRE_N)
                free("q_nope")
                for name, b, off in (("q_nope", 2, 0), ("q_rope", 4, P)):
                    if b == 4:
                        free("q_rope")
                    for k in range(2):
                        o = k * 2 * P + off
                        last = split_mm(bank[b][:, :], (whi[:, 2, o:o + P], wlo[:, 2, o:o + P]),
                                        cq_hi[:, k, :], cq_lo[:, k, :], k == 0, k == 1)
                    if b == 2:
                        fill("q_nope", last)
                last.then_inc(unit_done, 1)
                pe.wait_ge(w_ready, unit(l, B_HEAD, i, U_HEAD, 3) + (1 + STAGES))
                free("k_nope")
                fill("k_nope", split_mm(bank[3][:, :], (whi[:, 3, 0:P], wlo[:, 3, 0:P]), ckv_hi[:, :], ckv_lo[:, :], True, True))
                free("v_t")
                split_mm(bank[5][:, :], (whi[:, 3, P:2 * P], wlo[:, 3, P:2 * P]), ckv_hi[:, :], ckv_lo[:, :], True, True)\
                    .then_inc(unit_done, 1)
                w_acc(pe, 1, l * ACC_L + i * 3 + A_HEAD)
                free("vm_tr")
                for c in range(TC):
                    last = T.transpose(bank[6][:, c * P:(c + 1) * P], vm_ch[:, c * P:(c + 1) * P], ident)
                fill("vm_tr", last)
                head_unit(4, 0, 0, 1)
                w_taken(pe, l, i, "k_tr")
                w_taken(pe, l, i, "vm_tr")
                free("c_loc")
                for c in range(TC - 1):
                    last = T.matmul(bank[7][0:DK, c * 129:(c + 1) * 129], kw[:, c, :], vmt[:, c, :], start=True, stop=True)
                fill("c_loc", last)
                pe.wait_ge(sq_s, (l * HEADS + i) * 3 + 3)
                free("stat_q")
                fill("stat_q", T.matmul(bank[5][:, :], ones[:, :], nq[:, :], start=True, stop=True))
                free("stat_k")
                fill("stat_k", T.matmul(bank[6][:, :], ones[:, :], nk[:, :], start=True, stop=True))
                free("stat_r")
                fill("stat_r", T.matmul(bank[5][:, :], ones[0:ROPE, :], nr[:, :], start=True, stop=True))
                head_unit(5, 1, 1, 1)
                w_taken(pe, l, i, "s_t")
                pe.wait_ge(qs_s, l * HEADS + i + 1)
                for half, name in ((0, "num0"), (1, "num1")):
                    free(name)
                    for c in (2 * half, 2 * half + 1):
                        o = bank[7 - half][:, (c % 2) * 129:(c % 2) * 129 + 129]
                        last = T.matmul(o, dec[:, c, :], vmt[:, c, :], start=True, stop=(c == 0))
                        if c:
                            last = T.matmul(o, qs[:, c * P:(c + 1) * P], csb[:, c - 1, :], start=False, stop=True)
                    fill(name, last)
                w_taken(pe, l, i, "q_nope")
                w_taken(pe, l, i, "k_nope")
                pe.wait_ge(rope_s, (l * HEADS + i) * 3 + 3)
                for qb in range(TC):
                    b, w = bank[2 + qb], (qb + 1) * P
                    free(f"score{qb}")
                    T.matmul(b[:, 0:w], nq[:, qb * P:w], nk[:, 0:w], start=True, stop=False)
                    T.matmul(b[:, 0:w], qpe[:, qb * P:w], kpe[:, 0:w], start=False, stop=False)
                    fill(f"score{qb}", T.matmul(b[:, qb * P:w], ident, col("future", 0, P), start=False, stop=True))
                head_unit(6, 2, 0, 2)
                pe.wait_ge(p_s, (l * HEADS + i) * TC + TC)
                at = {0: (2, 0), 1: (3, 0), 2: (4, 0), 3: (4, 2 * P)}
                for kb in range(TC):
                    b, o = at[kb]
                    if kb < 3:
                        free(f"pt{kb}")
                    for qb in range(kb, TC):
                        src = (qb * (qb + 1) // 2 + kb) * P
                        last = T.transpose(bank[b][:, o + (qb - kb) * P:o + (qb - kb + 1) * P], prob[:, src:src + P], ident)
                    if kb != 2:
                        fill(f"pt{min(kb, 2)}", last)
                free("v_tr")
                for c in range(TC):
                    last = T.transpose(bank[6][:, c * P:(c + 1) * P], v_ch[:, c * P:(c + 1) * P], ident)
                fill("v_tr", last)
                free("h_tr")
                for c in range(TC):
                    last = T.transpose(bank[7][:, c * P:(c + 1) * P], htok[:, c, :], ident)
                fill("h_tr", last)
                head_unit(7, 3, 1, 2)
                for kb in range(3):
                    w_taken(pe, l, i, f"pt{kb}")
                w_taken(pe, l, i, "v_tr")
                free("pv")
                at = 0
                for kb in range(TC):
                    w = (TC - kb) * P
                    last = T.matmul(bank[5][:, kb * P:SEQ], v_tok[:, kb, :], prob_t[:, at:at + w],
                                    start=(kb == 0), stop=(kb == TC - 1))
                    at += w
                fill("pv", last)

            for n in range(3):
                with pe.Fori(0, 4) as i:
                    for j in range(4):
                        u = unit(l, B_MERGE + n * U_MERGE, i, 4, j)
                        a = l * ACC_L + i * 2 + (A_MERGE + n * 8 + j // 2)
                        if j % 2 == 0:
                            project(u, j, 0, a, xg_hi, xg_lo)
                        else:
                            project(u, j, 1, a, act_hi, act_lo, (act_s, (l * 7 + n) * KT) if j == 1 else None)
            with pe.Fori(0, 2) as i:
                for j in range(4):
                    project(unit(l, B_OUT, i, 4, j), j, j % 2, l * ACC_L + i * 2 + (A_OUT + j // 2), mg_hi, mg_lo,
                            (mg_s, l * KT) if j == 0 else None)
            pe.wait_ge(ss_add, l * 2 * (KT - 1) + 2 * (KT - 1))
            pe.wait_ge(taken[2], l * _layer(2) + (_layer(2) - 1) + 1)
            T.matmul(bank[2][:, :], ones[:, :], ssum[:, :], start=True, stop=True).then_inc(filled[2], 1)
            with pe.Fori(0, FG) as g:
                with pe.Fori(0, 2) as i:
                    for j in range(4):
                        project(unit(l, B_MLP, g, U_MLP, j) + i * 4, j, j % 2,
                                l * ACC_L + g * 8 + i * 2 + (A_MLP + j // 2), xg_hi, xg_lo,
                                (xg_ready, l * 2 * KT + KT) if j == 0 else None)
                with pe.Fori(0, 2) as i:
                    for j in range(4):
                        project(unit(l, B_MLP + 8, g, U_MLP, j) + i * 4, j, j % 2,
                                l * ACC_L + g * 8 + i * 2 + (A_MLP + 4 + j // 2), act_hi, act_lo,
                                (act_s, l * 7 * KT + g * KT + 3 * KT) if j == 0 else None)

        for b in range(2):
            pe.wait_ge(taken[b], DEPTH * ACC_L + 1)
        for k in range(KT):
            if k >= 2:
                pe.wait_ge(xt_taken, KT + k - 1)
            for c in range(TC):
                last = T.transpose(bank[k % 2][:, c * P:(c + 1) * P], xT[:, k, c * P:(c + 1) * P], ident)
            last.then_inc(xt_filled, 1)

    @block.scalar
    def _(act):
        def hi(l, base, i, per, j):
            slot = (base + j) % WSLOTS
            act.wait_ge(stage_in[slot % STAGES], (l * (UNITS // 2) + i * (per // 2) + (base + j) // 2) * 16 + 16)
            act.wait_ge(unit_done, unit(l, base, i, per, j) + 1)
            S.activation(whi[:, slot, :], stage[:, slot % STAGES, :], ACT.Copy).then_inc(hi_ready, 1)

        def main_rstd(l, norm):
            act.wait_ge(filled[2], l * _layer(2, True) + (_layer(2, True) if norm else 1))
            S.activation(rstd[:, :], bank[2][:, :], ACT.Ln, scale=1.0 / D_MODEL, bias=eps[:, :]).then_inc(rs_step, 1)
            act.wait_ge(rs_step, l * 4 + (norm * 2 + 1))
            S.activation(rstd[:, :], rstd[:, :], ACT.Exp, scale=-0.5).then_inc(rs_step, 1)

        def squares(norm, k):
            if k >= 2:
                act.wait_ge(ss_add, norm * (KT - 1) + (k - 1))
            S.activation(ssum[:, :] if k == 0 else sqx[:, :], xT[:, k, :], ACT.Square).then_inc(x_sq, 1)

        act.dma_start(pos_i[:, :], pos_in.partition_broadcast(P)).then_inc(pos_in_s, 16)
        act.wait_ge(consts, N_CONSTS)
        for k in range(KT):
            act.wait_ge(xt_taken, k + 1)
            squares(0, k)
        act.wait_ge(trig, N_TRIG)
        S.activation(cs[0:64, :], red[0:64, :], ACT.Sin, scale=-1.0, bias=halfpi[0:64, :]).then_inc(trig_done, 1)
        S.activation(cs[64:P, :], red[64:P, :], ACT.Sin, scale=col("sign")[64:P, :]).then_inc(trig_done, 1)

        with act.Fori(0, DEPTH) as l:
            S.preload_act_table_set("natural_log_exp_and_others")
            for j in range(4):
                hi(l, 0, 0, 0, j)
            act.wait_ge(xg_ready, l * 2 * KT + KT)
            act.dma_start(par[:, :], par_in[l, :, :]).then_inc(par_in_s, 16)
            main_rstd(l, 0)
            hi(l, 0, 0, 0, 4)
            act.wait_ge(pre_raw, l * 2 + 1)
            S.activation(sq_kr[:, :], kr_raw[:, :], ACT.Square).then_inc(pre_sq, 1)
            act.wait_ge(row_v, l * ROW_V + 2)
            S.activation(r_i[:, :], r_i[:, :], ACT.Tanh).then_inc(row_s, 1)
            S.activation(r_f[:, :], r_f[:, :], ACT.Tanh).then_inc(row_s, 1)
            S.preload_act_table_set("natural_log_exp_and_others")
            act.wait_ge(row_s, l * 8 + 2)
            S.activation(r_f[:, :], r_f[:, :], ACT.Exp, scale=-GATE_CAP).then_inc(row_s, 1)
            act.wait_ge(row_s, l * 8 + 3)
            S.activation(r_f[:, :], r_f[:, :], ACT.Ln, bias=ones[0:HEADS, 0:1]).then_inc(row_s, 1)
            hi(l, 0, 0, 0, 5)
            w_acc(act, 1, l * ACC_L)
            S.activation(sq_ckv[:, :], ckv_raw[:, :], ACT.Square).then_inc(pre_sq, 1)
            for k in range(2):
                w_acc(act, k, l * ACC_L + 1)
                S.activation(sq_cq[:, k, :], cq_raw[:, k, :], ACT.Square).then_inc(pre_sq, 1)
            for n, (b, dst, width, rows) in enumerate(((5, sq_kr[:, :], ROPE, ROPE), (3, sq_ckv[:, :], KV_LORA, P),
                                                       (4, sq_cq[:, 0, :], Q_LORA, P))):
                act.wait_ge(filled[b], l * _layer(b, True) + 1)
                S.activation(dst, bank[b][0:rows, :], ACT.Ln, scale=1.0 / width, bias=eps[0:rows, :]).then_inc(taken[b], 1)
                act.wait_ge(taken[b], l * _layer(b) + 2)
                S.activation(dst, dst, ACT.Exp, scale=-0.5).then_inc(pre_rs, 1)
            for c in range(TC):
                act.wait_ge(row_v, l * ROW_V + (9 + 3 * c))
                S.activation(rows_mi[32:40, c * P:(c + 1) * P], rows_mi[0:HEADS, c * P:(c + 1) * P], ACT.Exp,
                             scale=-1.0, bias=m_prev[:, c:c + 1]).then_inc(row_s, 1)
            act.wait_ge(filled[7], l * _layer(7, True) + 1)
            S.activation(acol[:, :, :], bank[7][:, 0:32].rearrange("p (c h) -> p c h", h=8), ACT.Copy).then_inc(head_in, 1)
            S.activation(emt[:, :, :], bank[7][:, 32:64].rearrange("p (c h) -> p c h", h=8), ACT.Exp).then_inc(taken[7], 1)

            with act.Fori(0, HEADS) as i:
                def head_hi(j):
                    hi(l, B_HEAD, i, U_HEAD, j)

                it = l * HEADS + i
                head_hi(2)
                act.wait_ge(head_in, l + 1)
                w_filled(act, l, i, "m_bc")
                for c in range(TC):
                    ins = S.activation(dec[:, c, :], bank[6][:, c * P:(c + 1) * P], ACT.Exp, scale=-1.0,
                                       bias=acol[:, c, bass.ds(i, 1)])
                    ins.then_inc(taken[6] if c == TC - 1 else dec_s, 1)
                head_hi(3)
                head_hi(4)
                head_hi(5)
                w_filled(act, l, i, "q_nope")
                S.activation(nq[:, :], bank[2][:, :], ACT.Square).then_inc(sq_s, 1)
                w_unit(act, unit(l, B_HEAD, i, U_HEAD, 2))
                S.activation(nr[:, :], bank[4][0:ROPE, :], ACT.Square).then_inc(sq_s, 1)
                head_hi(6)
                w_filled(act, l, i, "k_nope")
                S.activation(nk[:, :], bank[3][:, :], ACT.Square).then_inc(sq_s, 1)
                head_hi(7)
                for n, (name, dst, rows) in enumerate((("stat_q", nq, P), ("stat_k", nk, P), ("stat_r", nr, ROPE))):
                    w_filled(act, l, i, name)
                    b = USES[name][0]
                    S.activation(dst[:, :], bank[b][0:rows, :], ACT.Ln, scale=1.0 / rows, bias=eps[0:rows, :])\
                        .then_inc(taken[b], 1)
                    w_taken(act, l, i, name)
                    S.activation(dst[:, :], dst[:, :], ACT.Exp, scale=-0.5).then_inc(rs_s, 1)
                head_hi(8)
                w_acc(act, 0, l * ACC_L + i * 3 + (A_HEAD + 1))
                S.activation(so[:, :], so[:, :], ACT.Sigmoid).then_inc(so_s, 1)
                S.preload_act_table_set("natural_log_exp_and_others")
                for c in range(TC):
                    if c % 2 == 0:
                        act.wait_ge(fin_s, it * 8 + c // 2 + 1)
                    S.activation(htok[:, c, :], bank[7 - c // 2][:, (c % 2) * 129:(c % 2) * 129 + DV], ACT.Square,
                                 accum_out=sm[:, SS, c:c + 1]).then_inc(ss_s, 1)
                act.wait_ge(nm_s, it + 1)
                for qb in range(TC):
                    o = qb * (qb + 1) // 2 * P
                    S.activation(prob[:, o:o + (qb + 1) * P], bank[2 + qb][:, 0:(qb + 1) * P], ACT.Exp,
                                 scale=(NOPE + ROPE) ** -0.5, bias=sm[:, NM, qb:qb + 1],
                                 accum_out=sm[:, SUM, qb:qb + 1]).then_inc(taken[2 + qb], 1)
                head_hi(9)
                act.wait_ge(fin_s, it * 8 + 7)
                S.activation(sm[:, LN, :], sm[:, TT, :], ACT.Ln, scale=1.0 / DV, bias=eps[:, :]).then_inc(hr_s, 1)
                act.wait_ge(hr_s, it * 2 + 1)
                S.activation(sm[:, HR, :], sm[:, LN, :], ACT.Exp, scale=-0.5).then_inc(hr_s, 1)
                w_filled(act, l, i, "pt0")
                S.activation(prob_t[:, 0:512], bank[2][:, :], ACT.Copy).then_inc(taken[2], 1)
                w_filled(act, l, i, "v_tr")
                S.activation(v_tok[:, :, :], bank[6][:, :].rearrange("p (c d) -> p c d", d=DV), ACT.Copy)\
                    .then_inc(taken[6], 1)
                w_filled(act, l, i, "pv")
                S.activation(ysC[:, i, :], bank[5][:, :], ACT.Copy).then_inc(taken[5], 1)

            S.preload_act_table_set("sigmoid_and_others")
            for n in range(3):
                with act.Fori(0, 4) as i:
                    for j in range(4):
                        hi(l, B_MERGE + n * U_MERGE, i, 4, j + 2)
                        if j % 2 == 0:
                            w_acc(act, 0, l * ACC_L + i * 2 + (A_MERGE + n * 8 + j // 2))
                            g = gsig[j // 2]
                            S.activation(g[:, :], g[:, :], ACT.Sigmoid).then_inc(g_s, 1)
            S.preload_act_table_set("natural_log_exp_and_others")
            for k in range(KT):
                hi(l, B_OUT, 0, 0, k + 2)
                w_acc(act, k % 2, l * ACC_L + (A_OUT + k // 2))
                squares(l * 2 + 1, k)
            main_rstd(l, 1)
            with act.Fori(0, FG * U_MLP // 4 - 2) as i:
                for j in range(4):
                    hi(l, B_MLP, i, 4, j + 2)
            for k in range(KT):
                if k < KT - 2:
                    hi(l, B_MLP + FG * U_MLP - KT, 0, 0, k + 2)
                w_acc(act, k % 2, l * ACC_L + (ACC_L - KT // 2 + k // 2))
                squares(l * 2 + 2, k)

    @block.vector
    def _(dve):
        def split_x(norm, k, g):
            V.tensor_scalar(xg_hi[:, k, :], xT[:, k, :], g, None, ALU.mult).then_inc(xg_hi_s, 1)
            dve.wait_ge(xg_hi_s, norm * KT + (k + 1))
            V.scalar_tensor_tensor(out=xg_lo[:, k, :], in0=xT[:, k, :], scalar=g, in1=xg_hi[:, k, :].bitcast(f32),
                                   op0=ALU.mult, op1=ALU.subtract).then_inc(xg_ready, 1)
            dve.wait_ge(x_sq, norm * KT + (k + 1))
            if k:
                if k > 1:
                    dve.wait_ge(ss_add, norm * (KT - 1) + (k - 1))
                V.tensor_tensor(ssum[:, :], ssum[:, :], sqx[:, :], ALU.add).then_inc(ss_add, 1)

        def newton(l, norm):
            base = norm * 4
            dve.wait_ge(filled[2], l * _layer(2, True) + (_layer(2, True) if norm else 1))
            dve.wait_ge(rs_step, l * 4 + (norm * 2 + 1))
            V.tensor_scalar(ev_n[:, :], bank[2][:, :], 1.0 / D_MODEL, EPS, ALU.mult, ALU.add).then_inc(taken[2], 1)
            dve.wait_ge(rs_step, l * 4 + (norm * 2 + 2))
            V.tensor_tensor(ev_t[:, :], rstd[:, :], rstd[:, :], ALU.mult).then_inc(nw, 1)
            dve.wait_ge(nw, l * 8 + (base + 1))
            dve.wait_ge(taken[2], l * _layer(2) + ((_layer(2) if norm else 1) + 1))
            V.tensor_tensor(ev_t[:, :], ev_t[:, :], ev_n[:, :], ALU.mult).then_inc(nw, 1)
            dve.wait_ge(nw, l * 8 + (base + 2))
            V.tensor_scalar(ev_t[:, :], ev_t[:, :], -0.5, 1.5, ALU.mult, ALU.add).then_inc(nw, 1)
            dve.wait_ge(nw, l * 8 + (base + 3))
            V.tensor_tensor(rstd[:, :], rstd[:, :], ev_t[:, :], ALU.mult).then_inc(nw, 1)

        dve.wait_ge(cst_in_s, 16)
        V.tensor_copy(ident_r[:, :], ident).then_inc(consts, 1)
        for c in range(TC):
            V.tensor_copy(after_r[:, c * P:(c + 1) * P], col("after", 0, P)).then_inc(consts, 1)
        dve.wait_ge(consts, N_CONSTS)
        for k in range(KT):
            dve.wait_ge(xt_filled, k + 1)
            V.tensor_copy(xT[:, k, :], bank[k % 2][:, :]).then_inc(xt_taken, 1)
            dve.wait_ge(xt_taken, k + 1)
            split_x(0, k, col("mix0", k))
        dve.wait_ge(pos_in_s, 16)
        step = 0

        def link(ins):
            nonlocal step
            step += 1
            ins.then_inc(trig, 1)
            dve.wait_ge(trig, step)

        link(V.tensor_copy(ang[:, :], pos_i[:, :]))
        link(V.tensor_scalar(ang[:, :], ang[:, :], col("freq"), None, ALU.mult))
        link(V.tensor_scalar(turns[:, :], ang[:, :], 1.0 / (2 * math.pi), None, ALU.mult))
        link(V.tensor_scalar(turns[:, :], turns[:, :], 12582912.0, None, ALU.add))
        link(V.tensor_scalar(turns[:, :], turns[:, :], 12582912.0, None, ALU.subtract))
        left, parts = 2 * math.pi, []
        for bits in (5, 13, 21):
            parts.append(math.floor(left * 2 ** bits) / 2 ** bits)
            left -= parts[-1]
        for part in (*parts, left):
            link(V.scalar_tensor_tensor(out=ang[:, :], in0=turns[:, :], scalar=-part, in1=ang[:, :],
                                        op0=ALU.mult, op1=ALU.add))
        link(V.tensor_scalar(red[:, :], ang[:, :], 3.1415925, -3.1415925, ALU.min, ALU.max))
        link(V.tensor_scalar(ang[0:64, :], red[0:64, :], -1.0, None, ALU.mult))
        link(V.tensor_tensor(red[0:64, :], red[0:64, :], ang[0:64, :], ALU.max))
        assert step == N_TRIG

        with dve.Fori(0, DEPTH) as l:
            newton(l, 0)
            dve.wait_ge(nw, l * 8 + 4)
            w_unit(dve, unit(l, 0))
            V.tensor_tensor(kr_raw[:, :], bank[0][0:64, :], rstd[0:64, :], ALU.mult).then_inc(pre_raw, 1)
            V.tensor_tensor(r_i[:, :], bank[0][64:72, :], rstd[64:72, :], ALU.mult).then_inc(pre_raw, 1)
            V.tensor_tensor(r_f[:, :], bank[0][96:104, :], rstd[96:104, :], ALU.mult).then_inc(taken[0], 1)
            dve.wait_ge(par_in_s, l * 16 + 16)
            dve.wait_ge(pre_raw, l * 2 + 2)
            V.tensor_scalar(r_i[:, :], r_i[:, :], gain("b_i", 0, slice(0, 8)), 1.0 / GATE_CAP, ALU.add, ALU.mult).then_inc(row_v, 1)
            w_acc(dve, 0, l * ACC_L)
            V.tensor_scalar(r_f[:, :], r_f[:, :], gain("b_f", 0, slice(0, 8)), 1.0 / GATE_CAP, ALU.add, ALU.mult).then_inc(row_v, 1)
            w_unit(dve, unit(l, 0, j=1))
            V.tensor_tensor(ckv_raw[:, :], bank[1][:, :], rstd[:, :], ALU.mult).then_inc(taken[1], 1)
            dve.wait_ge(trig_done, 2)
            V.tensor_scalar(gcs[:, :], cs[:, :], gain("q_rope"), None, ALU.mult).then_inc(pre_n, 1)
            dve.wait_ge(row_s, l * 8 + 4)
            for c in range(TC):
                V.tensor_tensor_scan(r_nb[:, c * P:(c + 1) * P], ones[0:HEADS, :], r_f[:, c * P:(c + 1) * P], 0.0,
                                     ALU.mult, ALU.add).then_inc(row_v, 1)
            dve.wait_ge(row_v, l * ROW_V + 6)
            V.scalar_tensor_tensor(out=r_a[:, :], in0=r_i[:, :], scalar=GATE_CAP, in1=r_nb[:, :], op0=ALU.mult,
                                   op1=ALU.add).then_inc(row_v, 1)
            V.memset(m_prev[:, 0:1], 0.0).then_inc(row_v, 1)
            dve.wait_ge(row_v, l * ROW_V + 8)
            for c in range(TC):
                s = slice(c * P, (c + 1) * P)
                V.tensor_tensor_scan(rows_mi[0:HEADS, s], r_a[:, s], r_a[:, s], m_prev[:, c:c + 1], ALU.max, ALU.max)\
                    .then_inc(row_v, 1)
                dve.wait_ge(row_v, l * ROW_V + (9 + 3 * c))
                V.tensor_tensor(m_prev[:, c + 1:c + 2], rows_mi[0:HEADS, (c + 1) * P - 1:(c + 1) * P],
                                r_nb[:, (c + 1) * P - 1:(c + 1) * P], ALU.subtract).then_inc(row_v, 1)
                V.tensor_tensor(r_d[:, s], r_nb[:, s], rows_mi[0:HEADS, s], ALU.subtract).then_inc(row_v, 1)
                dve.wait_ge(row_v, l * ROW_V + (11 + 3 * c))
            for k in range(2):
                w_unit(dve, unit(l, 0, j=2 + k))
                V.tensor_tensor(cq_raw[:, k, :], bank[k][:, :], rstd[:, :], ALU.mult).then_inc(taken[k], 1)
            dve.wait_ge(pre_rs, l * 3 + 1)
            V.scalar_tensor_tensor(out=kr_raw[:, :], in0=kr_raw[:, :], scalar=gain("k_rope", 0, slice(0, 64)), in1=sq_kr[:, :],
                                   op0=ALU.mult, op1=ALU.mult).then_inc(pre_n, 1)
            dve.wait_ge(pre_rs, l * 3 + 3)
            V.scalar_tensor_tensor(out=ckv_raw[:, :], in0=ckv_raw[:, :], scalar=gain("kva"), in1=sq_ckv[:, :],
                                   op0=ALU.mult, op1=ALU.mult).then_inc(pre_n, 1)
            for k in range(2):
                V.scalar_tensor_tensor(out=cq_raw[:, k, :], in0=cq_raw[:, k, :], scalar=gain("qa", k), in1=sq_cq[:, 0, :],
                                       op0=ALU.mult, op1=ALU.mult).then_inc(pre_n, 1)
            dve.wait_ge(pre_n, l * PRE_N + 5)
            V.tensor_copy(ckv_hi[:, :], ckv_raw[:, :]).then_inc(pre_n, 1)
            V.tensor_copy(cq_hi[:, :, :], cq_raw[:, :, :]).then_inc(pre_n, 1)
            dve.wait_ge(pre_n, l * PRE_N + 7)
            V.tensor_tensor(ckv_lo[:, :], ckv_raw[:, :], ckv_hi[:, :].bitcast(f32), ALU.subtract).then_inc(pre_n, 1)
            V.tensor_tensor(cq_lo[:, :, :], cq_raw[:, :, :], cq_hi[:, :, :].bitcast(f32), ALU.subtract).then_inc(pre_n, 1)
            dve.wait_ge(filled[6], l * _layer(6, True) + 1)
            V.tensor_tensor(kpe[:, :], bank[6][64:P, :], cs[64:P, :], ALU.mult).then_inc(taken[6], 1)
            V.tensor_tensor(sq_kr[:, :], kr_raw[:, :], cs[0:64, :], ALU.mult).then_inc(pre_n, 1)
            dve.wait_ge(taken[6], l * _layer(6) + 2)
            dve.wait_ge(pre_n, l * PRE_N + 10)
            V.tensor_tensor(kpe[:, :], kpe[:, :], sq_kr[:, :], ALU.add).then_inc(pre_n, 1)
            dve.wait_ge(row_s, l * 8 + 8)
            dve.wait_ge(taken[7], l * _layer(7) + 2)
            V.memset(vmt[:, :, DV:DV + 1], 1.0).then_inc(pre_n, 1)

            with dve.Fori(0, HEADS) as i:
                dve.wait_ge(pre_n, l * PRE_N + PRE_N)
                it = l * HEADS + i
                A = l * ACC_L + i * 3 + A_HEAD

                def w_head_unit(j):
                    w_unit(dve, unit(l, B_HEAD, i, U_HEAD, j))

                V.tensor_scalar(mi[:, :], rows_mi[:, :], cst[0:40, bass.ds(i + CST["onehot"], 1)], None, ALU.mult)\
                    .then_inc(mi_s, 1)
                w_head_unit(0)
                V.scalar_tensor_tensor(out=qsb[:, :], in0=bank[0][0:DK, :], scalar=DK ** -0.5, in1=rstd[0:DK, :],
                                       op0=ALU.mult, op1=ALU.mult).then_inc(q_s, 1)
                V.tensor_tensor(ksb[:, :], bank[0][DK:P, :], rstd[DK:P, :], ALU.mult).then_inc(taken[0], 1)
                w_filled(dve, l, i, "i_bc")
                dve.wait_ge(q_s, it + 1)
                V.tensor_tensor(qs[:, :], bank[7][0:DK, :], qsb[:, :], ALU.mult).then_inc(qs_s, 1)
                V.tensor_copy(sold[:, :], bank[7][0:DK, P - 1:SEQ:P]).then_inc(taken[7], 1)
                w_head_unit(1)
                V.tensor_tensor(vm_ch[:, :], bank[1][:, :], rstd[:, :], ALU.mult).then_inc(taken[1], 1)
                w_filled(dve, l, i, "k_tr")
                w_taken(dve, l, i, "m_bc")
                for c in range(TC):
                    V.tensor_scalar(kw[:, c, :], bank[6][:, c * DK:(c + 1) * DK], dec[:, c, P - 1:P], None, ALU.mult)\
                        .then_inc(taken[6] if c == TC - 1 else kw_s, 1)
                w_filled(dve, l, i, "s_t")
                w_taken(dve, l, i, "k_tr")
                V.tensor_tensor(dec[:, :, :], bank[7][:, :].rearrange("p (c t) -> p c t", t=P), dec[:, :, :], ALU.mult)\
                    .then_inc(taken[7], 1)
                w_head_unit(3)
                V.tensor_copy(v_ch[:, :], bank[5][:, :]).then_inc(taken[5], 1)
                w_filled(dve, l, i, "vm_tr")
                V.tensor_copy(vmt[:, :, 0:DV], bank[6][:, :].rearrange("p (c d) -> p c d", d=DV)).then_inc(taken[6], 1)
                w_head_unit(4)
                V.tensor_tensor(so[:, :], bank[0][:, :], rstd[:, :], ALU.mult).then_inc(taken[0], 1)
                w_filled(dve, l, i, "c_loc")
                V.tensor_copy(csb[:, 0, :], bank[7][0:DK, 0:129]).then_inc(c_s, 1)
                for c in (1, 2):
                    dve.wait_ge(c_s, it * 2 + c)
                    V.scalar_tensor_tensor(out=csb[:, c, :], in0=csb[:, c - 1, :], scalar=sold[:, c:c + 1],
                                           in1=bank[7][0:DK, c * 129:(c + 1) * 129], op0=ALU.mult, op1=ALU.add)\
                        .then_inc(c_s if c == 1 else taken[7], 1)
                for n, (b, dst, name) in enumerate(((2, nq, "q_nope"), (3, nk, "k_nope"))):
                    dve.wait_ge(rs_s, it * 3 + n + 1)
                    V.scalar_tensor_tensor(out=dst[:, :], in0=bank[b][:, :], scalar=gain(name), in1=dst[:, :],
                                           op0=ALU.mult, op1=ALU.mult).then_inc(taken[b], 1)
                V.tensor_tensor(qpe[:, :], bank[4][0:ROPE, :], gcs[0:ROPE, :], ALU.mult).then_inc(rope_s, 1)
                V.tensor_tensor(ksb[:, :], bank[4][ROPE:P, :], gcs[ROPE:P, :], ALU.mult).then_inc(taken[4], 1)
                dve.wait_ge(rope_s, it * 3 + 1)
                w_taken(dve, l, i, "q_rope")
                V.tensor_tensor(qpe[:, :], qpe[:, :], ksb[:, :], ALU.add).then_inc(rope_s, 1)
                dve.wait_ge(rope_s, it * 3 + 2)
                dve.wait_ge(rs_s, it * 3 + 3)
                V.tensor_tensor(qpe[:, :], qpe[:, :], nr[:, :], ALU.mult).then_inc(rope_s, 1)
                w_head_unit(5)
                V.tensor_tensor(cb[:, :], bank[1][:, :], rstd[:, :], ALU.mult).then_inc(taken[1], 1)
                w_filled(dve, l, i, "num0")
                V.tensor_copy(sm[:, DEN, 0:2], bank[7][:, 128:258:129]).then_inc(fin_s, 1)
                w_filled(dve, l, i, "num1")
                V.tensor_copy(sm[:, DEN, 2:4], bank[6][:, 128:258:129]).then_inc(fin_s, 1)
                dve.wait_ge(fin_s, it * 8 + 2)
                V.scalar_tensor_tensor(out=sm[:, ADEN, :], in0=sm[:, DEN, :], scalar=-1.0, in1=sm[:, DEN, :],
                                       op0=ALU.mult, op1=ALU.max).then_inc(fin_s, 1)
                dve.wait_ge(fin_s, it * 8 + 3)
                V.tensor_tensor(sm[:, DD, :], sm[:, ADEN, :], emt[:, :, i], ALU.max).then_inc(fin_s, 1)
                dve.wait_ge(fin_s, it * 8 + 4)
                V.reciprocal(sm[:, RR, :], sm[:, DD, :]).then_inc(fin_s, 1)
                dve.wait_ge(fin_s, it * 8 + 5)
                V.tensor_tensor(sm[:, R2, :], sm[:, RR, :], sm[:, RR, :], ALU.mult).then_inc(fin_s, 1)
                dve.wait_ge(fin_s, it * 8 + 6)
                dve.wait_ge(ss_s, it * 4 + 4)
                V.tensor_tensor(sm[:, TT, :], sm[:, R2, :], sm[:, SS, :], ALU.mult).then_inc(fin_s, 1)
                for qb in range(TC):
                    w_filled(dve, l, i, f"score{qb}")
                    V.reduce_max(sm[:, MX, qb:qb + 1], bank[2 + qb][:, 0:(qb + 1) * P], axis=AX.X).then_inc(mx_s, 1)
                dve.wait_ge(mx_s, it * 4 + 4)
                V.tensor_scalar(sm[:, NM, :], sm[:, MX, :], -(NOPE + ROPE) ** -0.5, None, ALU.mult).then_inc(nm_s, 1)
                for qb in range(TC):
                    w_taken(dve, l, i, f"score{qb}")
                V.reciprocal(sm[:, RINV, :], sm[:, SUM, :]).then_inc(rinv_s, 1)
                dve.wait_ge(rinv_s, it + 1)
                for qb in range(TC):
                    o = qb * (qb + 1) // 2 * P
                    V.tensor_scalar(prob[:, o:o + (qb + 1) * P], prob[:, o:o + (qb + 1) * P], sm[:, RINV, qb:qb + 1], None,
                                    ALU.mult).then_inc(p_s, 1)
                dve.wait_ge(hr_s, it * 2 + 2)
                V.tensor_tensor(sm[:, FF, :], sm[:, RR, :], sm[:, HR, :], ALU.mult).then_inc(fin_s, 1)
                dve.wait_ge(fin_s, it * 8 + 8)
                for c in range(TC):
                    b = 7 - c // 2
                    V.tensor_scalar(htok[:, c, :], bank[b][:, (c % 2) * 129:(c % 2) * 129 + DV], sm[:, FF, c:c + 1], None,
                                    ALU.mult).then_inc(taken[b] if c % 2 else h_s, 1)
                w_head_unit(6)
                V.tensor_tensor(cc[:, :], bank[0][:, :], rstd[:, :], ALU.mult).then_inc(taken[0], 1)
                w_filled(dve, l, i, "pt1")
                V.tensor_copy(prob_t[:, 512:896], bank[3][:, 0:384]).then_inc(taken[3], 1)
                w_filled(dve, l, i, "pt2")
                V.tensor_copy(prob_t[:, 896:1280], bank[4][:, 0:384]).then_inc(taken[4], 1)
                w_filled(dve, l, i, "h_tr")
                dve.wait_ge(so_s, it + 1)
                V.scalar_tensor_tensor(out=ysB[:, i, :], in0=bank[7][:, :], scalar=par[:, bass.ds(i + PAR["head"], 1)],
                                       in1=so[:, :], op0=ALU.mult, op1=ALU.mult).then_inc(taken[7], 1)
                w_head_unit(7)
                V.tensor_tensor(zp[:, 2:SEQ + 2], bank[1][:, :], rstd[:, :], ALU.mult).then_inc(taken[1], 1)
                w_acc(dve, 1, A + 2)
                w_acc(dve, 0, A + 2)
                V.tensor_tensor(zp[:, 2:SEQ + 2], zp[:, 2:SEQ + 2], cc[:, :], ALU.mult).then_inc(conv_s, 1)
                dve.wait_ge(conv_s, it * 5 + 1)
                for j in range(3):
                    w = par[:, bass.ds(i * 3 + (PAR["conv"] + j), 1)]
                    if j == 0:
                        V.tensor_scalar(cc[:, :], zp[:, 0:SEQ], w, None, ALU.mult).then_inc(conv_s, 1)
                    else:
                        V.scalar_tensor_tensor(out=cc[:, :], in0=zp[:, j:j + SEQ], scalar=w, in1=cc[:, :],
                                               op0=ALU.mult, op1=ALU.add).then_inc(conv_s, 1)
                    dve.wait_ge(conv_s, it * 5 + 2 + j)
                V.tensor_tensor(ysA[:, i, :], cb[:, :], cc[:, :], ALU.mult).then_inc(conv_s, 1)

            dve.wait_ge(conv_s, (l + 1) * HEADS * 5)
            dve.wait_ge(taken[5], (l + 1) * _layer(5) + 1)
            for n, ys in enumerate((ysA, ysB, ysC)):
                if n:
                    w_unit(dve, unit(l, B_MERGE + n * U_MERGE - 1))
                for k in range(KT):
                    V.tensor_copy(act_hi[:, k, :], ys[:, k, :]).then_inc(act_h, 1)
                    dve.wait_ge(act_h, (l * 7 + n) * KT + k + 1)
                    V.tensor_tensor(act_lo[:, k, :], ys[:, k, :], act_hi[:, k, :].bitcast(f32), ALU.subtract).then_inc(act_s, 1)
                with dve.Fori(0, 4) as i:
                    dve.wait_ge(act_s, (l * 7 + n + 1) * KT)
                    for j in range(2):
                        a = l * ACC_L + i * 2 + (A_MERGE + n * 8 + j)
                        m = l * 3 * KT + i * 2 + (n * KT + j)
                        g = gsig[j]
                        mk = merged[:, i * 2 + j, :]
                        w_unit(dve, unit(l, B_MERGE + n * U_MERGE, i, 4, 2 * j))
                        V.tensor_tensor(g[:, :], bank[0][:, :], rstd[:, :], ALU.mult).then_inc(taken[0], 1)
                        w_unit(dve, unit(l, B_MERGE + n * U_MERGE, i, 4, 2 * j + 1))
                        dve.wait_ge(g_s, m + 1)
                        V.tensor_tensor(mk if n == 0 else ev_n[:, :], bank[1][:, :], g[:, :], ALU.mult).then_inc(taken[1], 1)
                        if n:
                            w_acc(dve, 1, a)
                            V.tensor_tensor(mk, mk, ev_n[:, :], ALU.add).then_inc(mg_a, 1)
                        if n == 2:
                            dve.wait_ge(mg_a, l * 2 * KT + i * 2 + (KT + j + 1))
                            V.tensor_copy(mg_hi[:, i * 2 + j, :], mk).then_inc(mg_h, 1)
                            dve.wait_ge(mg_h, l * KT + i * 2 + (j + 1))
                            V.tensor_tensor(mg_lo[:, i * 2 + j, :], mk, mg_hi[:, i * 2 + j, :].bitcast(f32), ALU.subtract)\
                                .then_inc(mg_s, 1)
            for k in range(KT):
                w_unit(dve, unit(l, B_OUT, j=k))
                V.tensor_tensor(xT[:, k, :], xT[:, k, :], bank[k % 2][:, :], ALU.add).then_inc(taken[k % 2], 1)
                w_acc(dve, k % 2, l * ACC_L + (A_OUT + k // 2))
                split_x(l * 2 + 1, k, gain("mlp", k))
            newton(l, 1)
            def up(g):
                dve.wait_ge(nw, l * 8 + 8)
                for k in range(KT):
                    a = l * ACC_L + g * 8 + (A_MLP + k // 2)
                    m = l * 4 * KT + g * KT + (k + 1)
                    w_unit(dve, unit(l, B_MLP, g, U_MLP, k))
                    V.tensor_tensor(ev_t[:, :], bank[k % 2][:, :], rstd[:, :], ALU.mult).then_inc(taken[k % 2], 1)
                    w_acc(dve, k % 2, a)
                    V.scalar_tensor_tensor(out=ev_r[:, :], in0=ev_t[:, :], scalar=0.0, in1=ev_t[:, :],
                                           op0=ALU.max, op1=ALU.mult).then_inc(act_a, 1)
                    dve.wait_ge(act_a, m)
                    V.tensor_copy(act_hi[:, k, :], ev_r[:, :]).then_inc(act_h, 1)
                    dve.wait_ge(act_h, l * 7 * KT + g * KT + (3 * KT + k + 1))
                    V.tensor_tensor(act_lo[:, k, :], ev_r[:, :], act_hi[:, k, :].bitcast(f32), ALU.subtract).then_inc(act_s, 1)

            with dve.Fori(0, FG - 1) as g:
                up(g)
                for k in range(KT):
                    w_unit(dve, unit(l, B_MLP, g, U_MLP, KT + k))
                    V.tensor_tensor(xT[:, k, :], xT[:, k, :], bank[k % 2][:, :], ALU.add).then_inc(taken[k % 2], 1)
            up(FG - 1)
            for k in range(KT):
                w_unit(dve, unit(l, B_MLP, FG - 1, U_MLP, KT + k))
                V.tensor_tensor(xT[:, k, :], xT[:, k, :], bank[k % 2][:, :], ALU.add).then_inc(taken[k % 2], 1)
                w_acc(dve, k % 2, l * ACC_L + (ACC_L - KT // 2 + k // 2))
                split_x(l * 2 + 2, k, gain("mix_next", k))

        for k in range(KT):
            dve.wait_ge(xt_filled, KT + k + 1)
            V.tensor_copy(out_tok[:, :, k * P:(k + 1) * P], bank[k % 2][:, :].rearrange("p (c d) -> p c d", d=P))\
                .then_inc(xt_taken, 1)

    ctx.close()


def unit_columns(w, c0, width=P):
    rows = w.shape[0]
    return w[:, c0:c0 + width].reshape(rows // P, P, width).transpose(1, 0, 2).reshape(P, rows // P * width)


def weight_stream(w_in, w_uq, w_ukv, w_branch, w_out, w_up, w_down):
    stream = np.zeros((DEPTH * UNITS, P, 1024), np.float32)
    at = 0

    def put(*blocks):
        nonlocal at
        o = 0
        for b in blocks:
            stream[at, :, o:o + b.shape[1]] = b
            o += b.shape[1]
        at += 1

    for l in range(DEPTH):
        kif = np.concatenate([w_in[l][:, C_KR:C_KR + 64], w_in[l][:, C_MI:C_MI + 32], w_in[l][:, C_MF:C_MF + 32]], axis=1)
        put(unit_columns(kif, 0))
        put(unit_columns(w_in[l], C_CKV))
        for k in range(2):
            put(unit_columns(w_in[l], C_CQ + k * P))
        for h in range(HEADS):
            qk = np.concatenate([w_in[l][:, C_MQ + h * DK:C_MQ + (h + 1) * DK], w_in[l][:, C_MK + h * DK:C_MK + (h + 1) * DK]],
                                axis=1)
            put(unit_columns(qk, 0))
            put(unit_columns(w_in[l], C_MV + h * P))
            q0 = h * (NOPE + ROPE)
            r0 = q0 + NOPE
            rows = [w_uq[l][k * P:(k + 1) * P] for k in range(2)]
            put(*[np.concatenate([r[:, q0:r0 + ROPE], r[:, r0 + ROPE // 2:r0 + ROPE], r[:, r0:r0 + ROPE // 2]], axis=1)
                  for r in rows])
            put(w_ukv[l][:, h * 2 * P:(h + 1) * 2 * P])
            put(unit_columns(w_in[l], C_MO + h * P))
            for c in (C_CB, C_CC, C_CU):
                put(unit_columns(w_in[l], c + h * P))
        for n in range(3):
            for d in range(KT):
                put(unit_columns(w_in[l], C_GATE + n * D_MODEL + d * P))
                put(unit_columns(w_branch[l, n], d * P))
        for d in range(KT):
            put(unit_columns(w_out[l], d * P))
        for g in range(FG):
            for j in range(KT):
                put(unit_columns(w_up[l], (g * KT + j) * P))
            for d in range(KT):
                put(unit_columns(w_down[l][g * D_MODEL:(g + 1) * D_MODEL], d * P))
    assert at == DEPTH * UNITS
    return stream


def tiles(v):
    return v.reshape(-1, P).T


def kernel(x, positions, mix_norm, w_in, conv_w, mlstm_igate_bias, mlstm_fgate_bias, mlstm_head_norm,
           mla_q_a_norm, mla_w_uq, mla_kv_a_norm, mla_w_ukv, mla_q_norm, mla_k_norm, w_branch, w_out,
           mlp_norm, w_up, w_down):
    import concourse.bacc as bacc
    from concourse.bass_utils import run_bass_kernel_spmd

    par = np.zeros((DEPTH, P, NPAR), np.float32)
    for l in range(DEPTH):
        def put(name, block, row=0):
            par[l, row:row + block.shape[0], PAR[name]:PAR[name] + block.shape[1]] = block

        put("mix_next", tiles(mix_norm[min(l + 1, DEPTH - 1)]))
        put("mlp", tiles(mlp_norm[l]))
        put("conv", conv_w[l].reshape(3, KT, P).transpose(2, 1, 0).reshape(P, KT * 3))
        put("head", tiles(mlstm_head_norm[l]))
        put("qa", tiles(mla_q_a_norm[l]))
        put("kva", tiles(mla_kv_a_norm[l]))
        put("q_nope", mla_q_norm[l][:NOPE, None])
        put("k_nope", mla_k_norm[l][:NOPE, None])
        put("q_rope", mla_q_norm[l][NOPE:, None])
        put("q_rope", mla_q_norm[l][NOPE + ROPE // 2:, None], 64)
        put("q_rope", mla_q_norm[l][NOPE:NOPE + ROPE // 2, None], 96)
        put("k_rope", mla_k_norm[l][NOPE:, None])
        put("b_i", mlstm_igate_bias[l][:, None])
        put("b_f", mlstm_fgate_bias[l][:, None])

    cst = np.zeros((P, NCST), np.float32)
    r = np.arange(P)
    cst[:, CST["ident"]:CST["ident"] + P] = np.eye(P)
    cst[:, CST["after"]:CST["after"] + P] = np.where(r[:, None] > r[None, :], BIG, 0)
    cst[:, CST["future"]:CST["future"] + P] = np.where(r[None, :] > r[:, None], -BIG, 0)
    for d in range(ROPE):
        cst[(d + ROPE // 2) % ROPE, CST["swap"] + ROPE + d] = 1
    for h in range(HEADS):
        cst[h, CST["onehot"] + h] = cst[32 + h, CST["onehot"] + h] = 1
    freq = (10000.0 ** (-np.arange(0, ROPE, 2) / ROPE)).astype(np.float32)
    cst[:, CST["freq"]] = freq[r % (ROPE // 2)]
    cst[:, CST["sign"]] = np.where(r % ROPE < ROPE // 2, -1, 1)
    cst[:, CST["mix0"]:CST["mix0"] + KT] = tiles(mix_norm[0])

    arrays = {
        "x": np.ascontiguousarray(x[0]),
        "positions": np.ascontiguousarray(positions[0]),
        "wstream": weight_stream(w_in, mla_w_uq, mla_w_ukv, w_branch, w_out, w_up, w_down),
        "par": par,
        "cst": cst,
    }
    nc = bacc.Bacc("TRN2", target_bir_lowering=False, num_devices=1)
    args = [nc.dram_tensor(n, a.shape, mybir.dt.from_np(a.dtype), kind="ExternalInput").ap() for n, a in arrays.items()]
    out = nc.dram_tensor("out", (SEQ, D_MODEL), mybir.dt.float32, kind="ExternalOutput").ap()
    build_trunk(nc, *args, out)
    result = run_bass_kernel_spmd(nc, [arrays], core_ids=[0])
    return result.results[0]["out"].reshape(1, SEQ, D_MODEL)
```

```python
import math
from contextlib import ExitStack

import numpy as np
import concourse.bass as bass
from concourse import mybir

D_MODEL, SEQ, DEPTH = 1024, 512, 2
P = 128
KT = D_MODEL // P
TC = SEQ // P
HEADS = 8
DK, DV = 64, 128
NOPE, ROPE = 128, 64
Q_LORA, KV_LORA = 256, 128
D_FF = 4096
FG = D_FF // D_MODEL
EPS = 1e-6
GATE_CAP = 15.0
BIG = 1e30

C_CB, C_CC, C_CU = 0, 1024, 2048
C_MQ, C_MK, C_MV, C_MO = 3072, 3584, 4096, 5120
C_MI, C_MF, C_CQ, C_CKV, C_KR, C_GATE = 6144, 6152, 6160, 6416, 6544, 6608

U_PRE, U_HEAD, U_MERGE, U_OUT, U_MLP = 4, 8, 16, 8, 16
UNITS = U_PRE + HEADS * U_HEAD + 3 * U_MERGE + U_OUT + FG * U_MLP
B_HEAD = U_PRE
B_MERGE = B_HEAD + HEADS * U_HEAD
B_OUT = B_MERGE + 3 * U_MERGE
B_MLP = B_OUT + U_OUT
STAGES, WSLOTS = 2, 4

PAR = {}
_at = 0
for _n, _w in (("mix_next", KT), ("mlp", KT), ("conv", KT * 3), ("head", KT), ("qa", 2), ("kva", 1),
               ("q_nope", 1), ("k_nope", 1), ("q_rope", 1), ("k_rope", 1), ("b_i", 1), ("b_f", 1)):
    PAR[_n] = _at
    _at += _w
NPAR = _at
CST = {}
_at = 0
for _n, _w in (("ident", P), ("swap", P), ("onehot", HEADS), ("freq", 1),
               ("sign", 1), ("mix0", KT)):
    CST[_n] = _at
    _at += _w
NCST = _at

USES = {
    "q_nope": (2, 0), "score0": (2, 1), "pt0": (2, 2),
    "k_nope": (3, 0), "score1": (3, 1), "pt1": (3, 2),
    "q_rope": (4, 0), "score2": (4, 1), "pt2": (4, 2),
    "v_t": (5, 0), "stat_q": (5, 1), "stat_r": (5, 2), "score3": (5, 3), "pv": (5, 4),
    "m_bc": (6, 0), "k_tr": (6, 1), "vm_tr": (6, 2), "stat_k": (6, 3), "num1": (6, 4), "v_tr": (6, 5),
    "i_bc": (7, 0), "s_t": (7, 1), "c_loc": (7, 2), "num0": (7, 3), "h_tr": (7, 4),
}
BY_UNIT = ("q_rope", "v_t")
PRE_USE = {"stat_x": 2, "stat_kv": 3, "stat_cq": 4, "stat_kr": 5, "rot_kr": 6, "rows_tr": 7}
POST_USE = {"stat_h": 2}


def _per(bank, fills=False):
    return sum(1 for n, (b, _) in USES.items() if b == bank and not (fills and n in BY_UNIT))


def _nth(name, fills=False):
    b, k = USES[name]
    return k - (sum(1 for n in BY_UNIT if USES[n][0] == b and USES[n][1] < k) if fills else 0)


def _layer(bank, fills=False):
    return (HEADS * _per(bank, fills) + (bank in PRE_USE.values()) + (bank in POST_USE.values()))


def build_trunk(nc, x_in, pos_in, wstream, par_in, cst_in, masks_in, out):
    f32, f32r, bf16, i32 = mybir.dt.float32, mybir.dt.float32r, mybir.dt.bfloat16, mybir.dt.int32
    ALU, ACT, AX = mybir.AluOpType, mybir.ActivationFunctionType, mybir.AxisListType
    ctx = ExitStack()
    V, S, T, G = nc.vector, nc.scalar, nc.tensor, nc.gpsimd

    top = [16512]
    names = {}

    def place(name, shape, dt=f32, at=None):
        size = (2 if dt == bf16 else 4) * int(np.prod(shape[1:]))
        if at is None:
            at = top[0]
            top[0] += (size + 31) // 32 * 32
        names[name] = at
        return nc.alloc_sbuf_tensor_at(name, shape, dt, offset=at)

    xT = place("xT", [P, KT, SEQ])
    xg_hi = place("xg_hi", [P, KT, SEQ], f32r)
    xg_lo = place("xg_lo", [P, KT, SEQ], f32r)
    ysA = place("ysA", [P, KT, SEQ])
    ysB = place("ysB", [P, KT, SEQ])
    ysC = place("ysC", [P, KT, SEQ])
    merged = place("merged", [P, KT, SEQ], at=names["ysA"])
    mg_hi = place("mg_hi", [P, KT, SEQ], f32r, at=names["ysB"])
    mg_lo = place("mg_lo", [P, KT, SEQ], f32r, at=names["ysC"])
    x_tok = place("x_tok", [P, TC, D_MODEL], at=names["ysA"])
    out_tok = place("out_tok", [P, TC, D_MODEL], at=names["ysB"])
    stage = place("stage", [P, STAGES, 1024])
    whi = place("whi", [P, WSLOTS, 1024], f32r)
    wlo = place("wlo", [P, WSLOTS, 1024], f32r)

    cst = place("cst", [P, NCST])
    par = place("par", [P, NPAR])
    after_b = place("after_b", [P, SEQ], bf16)
    ones_r = place("ones_r", [P, P], f32r)
    ones = ones_r[:, :].bitcast(f32)
    ident_b = place("ident_b", [P, P], bf16)
    future_b = place("future_b", [P, P], bf16)
    cs = place("cs", [P, SEQ])
    gcs = place("gcs", [P, SEQ])
    eps = place("eps", [P, 1])
    halfpi = place("halfpi", [P, 1])
    cq_hi = place("cq_hi", [P, 2, SEQ], f32r)
    cq_lo = place("cq_lo", [P, 2, SEQ], f32r)
    ckv_hi = place("ckv_hi", [P, SEQ], f32r)
    ckv_lo = place("ckv_lo", [P, SEQ], f32r)
    kpe_h = place("kpe_h", [P, SEQ], f32r)
    kpe_l = place("kpe_l", [P, SEQ], f32r)
    rows_mi = place("rows_mi", [P, SEQ], f32r)
    acol = place("acol", [P, TC, HEADS])
    emt = place("emt", [P, TC, HEADS])
    rstd = place("rstd", [P, SEQ])
    ssum = place("ssum", [P, SEQ])
    tmp0 = top[0]
    sqx = place("sqx", [P, SEQ])
    ev_t = place("ev_t", [P, SEQ])
    ev_r = place("ev_r", [P, SEQ])
    ev_n = place("ev_n", [P, SEQ])
    gsig = [ev_t, ev_r]
    tmp_end = top[0]
    act_hi = place("act_hi", [P, KT, SEQ], f32r)
    act_lo = place("act_lo", [P, KT, SEQ], f32r)
    act0 = names["act_hi"]
    end = top[0]

    top[0] = tmp0
    prob = place("prob", [P, 1280])
    so = place("so", [P, SEQ])
    kw = place("kw", [P, TC, DK])
    assert top[0] <= tmp_end
    top[0] = act0
    nq = place("nq", [P, SEQ])
    nk = place("nk", [P, SEQ])
    nr = place("nr", [ROPE, SEQ])
    q_pe = place("q_pe", [P, SEQ], f32r)
    prob_t = place("prob_t", [P, 1280], at=names["nq"])
    qsb = place("qsb", [DK, SEQ])
    ksb = place("ksb", [DK, SEQ])
    v_ch = place("v_ch", [P, SEQ])
    vm_ch = place("vm_ch", [P, SEQ])
    htok = place("htok", [P, TC, DV], at=names["vm_ch"])
    mi = place("mi", [P, SEQ], f32r)
    tmp_n = place("tmp_n", [P, SEQ], at=names["mi"])
    qs = place("qs", [DK, SEQ])
    dec = place("dec", [P, TC, P])
    cb = place("cb", [P, SEQ])
    cc = place("cc", [P, SEQ])
    vmt = place("vmt", [P, TC, DV + 1])
    v_tok = place("v_tok", [P, TC, DV])
    sq_hi = [place("sqq_hi", [P, SEQ], f32r, at=names["cb"]), place("sqk_hi", [P, SEQ], f32r, at=names["vm_ch"])]
    sq_lo = [place("sqq_lo", [P, SEQ], f32r, at=names["cc"]), place("sqk_lo", [P, SEQ], f32r, at=names["prob"] + 2048)]
    nq_hi = place("nq_hi", [P, SEQ], f32r, at=names["prob"])
    nq_lo = place("nq_lo", [P, SEQ], f32r, at=names["v_tok"])
    nk_hi = place("nk_hi", [P, SEQ], f32r, at=names["vm_ch"])
    nk_lo = place("nk_lo", [P, SEQ], f32r, at=names["prob"] + 2048)
    assert top[0] <= end, (top[0], end)
    top[0] = end
    zp = place("zp", [P, SEQ + 2])
    csb = place("csb", [DK, TC - 1, DV + 1], at=names["ssum"])
    sold = place("sold", [DK, TC], at=names["ssum"] + 1568)
    sm = place("sm", [P, 16, TC], at=names["ssum"] + 1600)
    end = top[0]
    assert end <= 229368, end
    MX, NM, SUM, RINV, SS, DEN, ADEN, DD, RR, R2, TT, LN, HR, FF = range(14)

    top[0] = act0
    cq_raw = place("cq_raw", [P, 2, SEQ])
    ckv_raw = place("ckv_raw", [P, SEQ])
    kr_raw = place("kr_raw", [ROPE, SEQ])
    sq_cq = place("sq_cq", [P, 2, SEQ])
    sq_ckv = place("sq_ckv", [P, SEQ])
    sq_kr = place("sq_kr", [ROPE, SEQ])
    r_i = place("r_i", [HEADS, SEQ])
    r_f = place("r_f", [HEADS, SEQ])
    r_nb = place("r_nb", [HEADS, SEQ])
    r_a = place("r_a", [HEADS, SEQ])
    r_d = place("r_d", [HEADS, SEQ])
    r_m = place("r_m", [HEADS, SEQ])
    r_e = place("r_e", [HEADS, SEQ])
    kpe = place("kpe", [ROPE, SEQ], at=names["sq_ckv"])
    m_prev = place("m_prev", [HEADS, TC + 1])
    masks = place("masks", [P, 2, P])
    assert top[0] <= act0 + 2 * KT * SEQ * 4
    top[0] = act0
    pos_i = place("pos_i", [P, SEQ], i32)
    ang = place("ang", [P, SEQ])
    turns = place("turns", [P, SEQ])
    red = place("red", [P, SEQ])

    bank = [ctx.enter_context(nc.psum_tensor(f"bank{b}", [P, 512], f32)) for b in range(8)]

    def col(name, k=0, w=1):
        return cst[:, CST[name] + k:CST[name] + k + w]

    def gain(name, k=0, rows=slice(0, P)):
        return par[rows, PAR[name] + k:PAR[name] + k + 1]

    ident = cst[:, CST["ident"]:CST["ident"] + P]

    def sem(name):
        return ctx.enter_context(nc.semaphore(name))

    stage_in = [sem(f"stage_in{s}") for s in range(STAGES)]
    hi_ready = sem("hi_ready")
    w_ready = sem("w_ready")
    unit_done = sem("unit_done")
    taken = [sem(f"bank{b}_taken") for b in range(8)]
    filled = [sem(f"bank{b}_filled") for b in range(8)]
    cst_in_s, pos_in_s, par_in_s = sem("cst_in"), sem("pos_in"), sem("par_in")
    x_in_s = [sem(f"x_in{g}") for g in range(4)]
    out_s = sem("out_stored")
    consts = sem("consts_ready")
    trig = sem("trig_step")
    trig_done = sem("trig_done")
    xt_filled, xt_taken = sem("x_transposed"), sem("x_transpose_taken")
    x_sq = sem("x_squared")
    ss_add = sem("ssum_added")
    xg_hi_s = sem("xg_hi_ready")
    xg_ready = sem("xg_ready")
    rs_step = sem("rstd_step")
    nw = sem("newton_step")
    pre_raw = sem("pre_raw")
    pre_sq = sem("pre_squared")
    pre_rs = sem("pre_rstd")
    pre_n = sem("pre_normed")
    row_v, row_s = sem("rows_vector"), sem("rows_scalar")
    head_in = sem("head_inputs")
    mi_s = sem("mi_ready")
    q_s = sem("mlstm_q_ready")
    qs_s = sem("qs_ready")
    kw_s = sem("kw_step")
    dec_s = sem("dec_step")
    vt_s = sem("num_half_read")
    sq_s = sem("mla_squared")
    rs_s = sem("mla_rstd")
    c_s = sem("c_state_step")
    qpe_s = sem("rotary_query_ready")
    nrm_s = sem("query_key_split")
    sql_s = sem("squares_split")
    chain = sem("head_step")
    mx_s, nm_s, rinv_s, p_s = sem("score_max"), sem("neg_max"), sem("prob_sum_inv"), sem("prob_ready")
    ex_s = sem("prob_exp")
    ss_s, fin_s, hr_s = sem("num_squared"), sem("num_step"), sem("head_rstd")
    h_s = sem("htok_step")
    so_s = sem("o_gate_ready")
    conv_s = sem("conv_step")
    act_a = sem("act_value")
    act_h = sem("act_hi_ready")
    act_s = sem("act_ready")
    g_s = sem("gate_ready")
    mg_a = sem("merge_sum")
    mg_h = sem("mg_hi_ready")
    mg_s = sem("merged_ready")

    block = ctx.enter_context(nc.Block())

    CH = 12
    N_CONSTS = 4 + 3 + TC
    N_TRIG = 12
    PRE_N, ROW_V, ROWS_AT = 16, 24, 20

    ACC_L = (U_PRE + HEADS * 6 + 3 * U_MERGE + U_OUT + FG * U_MLP) // 2
    A_HEAD = U_PRE // 2
    A_MERGE = A_HEAD + HEADS * 3
    A_OUT = A_MERGE + 3 * U_MERGE // 2
    A_MLP = A_OUT + U_OUT // 2

    def unit(l, base, i=0, per=0, j=0):
        return l * UNITS + i * per + (base + j)

    def used(l, i, name):
        b, _ = USES[name]
        return l * _layer(b) + i * _per(b) + (1 + _nth(name))

    def w_filled(e, l, i, name):
        b, _ = USES[name]
        e.wait_ge(filled[b], l * _layer(b, True) + i * _per(b, True) + (1 + _nth(name, True)) + 1)

    def w_taken(e, l, i, name):
        e.wait_ge(taken[USES[name][0]], used(l, i, name) + 2)

    def w_free(e, l, i, name):
        e.wait_ge(taken[USES[name][0]], used(l, i, name) + 1)

    def w_unit(e, u):
        e.wait_ge(unit_done, u + (1 + WSLOTS))

    def w_acc(e, b, n):
        e.wait_ge(taken[b], n + 2)

    @block.sync
    def _(sp):
        sp.dma_start(cst[:, :], cst_in).then_inc(cst_in_s, 16)
        for g in range(4):
            sp.dma_start(x_tok[:, :, g * 256:(g + 1) * 256], x_in.rearrange("(c p) d -> p c d", p=P)[:, :, g * 256:(g + 1) * 256])\
                .then_inc(x_in_s[g], 16)
        sp.dma_start(masks[:, :, :], masks_in).then_inc(cst_in_s, 16)
        with sp.Fori(0, DEPTH * UNITS // STAGES) as i:
            for s in range(STAGES):
                sp.wait_ge(w_ready, i * STAGES + (s + 1))
                sp.dma_start(stage[:, s, :], wstream[i * STAGES + s, :, :]).then_inc(stage_in[s], 16)
        sp.wait_ge(xt_taken, 2 * KT)
        sp.dma_start(out.rearrange("(c p) d -> p c d", p=P), out_tok[:, :, :]).then_inc(out_s, 16)
        sp.wait_ge(out_s, 16)

    @block.gpsimd
    def _(pool):
        pool.sem_inc(w_ready, STAGES)
        pool.sem_inc(unit_done, WSLOTS)
        for b in range(8):
            pool.sem_inc(taken[b], 1)
        G.memset(eps[:, :], EPS).then_inc(consts, 1)
        G.memset(halfpi[:, :], math.pi / 2).then_inc(consts, 1)
        G.memset(rows_mi[:, :].bitcast(f32), 0.0).then_inc(consts, 1)
        G.memset(zp[:, 0:2], 0.0).then_inc(consts, 1)
        with pool.Fori(0, DEPTH * UNITS // WSLOTS) as i:
            for j in range(WSLOTS):
                pool.wait_ge(hi_ready, i * WSLOTS + (j + 1))
                G.tensor_tensor(wlo[:, j, :], stage[:, j % STAGES, :], whi[:, j, :].bitcast(f32),
                                ALU.subtract).then_inc(w_ready, 1)

    @block.tensor
    def _(pe):
        def split_mm(acc, w, hi, lo, first, last):
            T.matmul(acc, w[0], hi, start=first, stop=False)
            T.matmul(acc, w[0], lo, start=False, stop=False)
            return T.matmul(acc, w[1], hi, start=False, stop=last)

        def project(u, slot, b, n, hi, lo, tile_ready=None):
            pe.wait_ge(w_ready, u + (1 + STAGES))
            pe.wait_ge(taken[b], n + 1)
            for k in range(KT):
                if tile_ready is not None:
                    pe.wait_ge(tile_ready[0], tile_ready[1] + (k + 1))
                w = (whi[:, slot, k * P:(k + 1) * P], wlo[:, slot, k * P:(k + 1) * P])
                last = split_mm(bank[b][:, :], w, hi[:, k, :], lo[:, k, :], k == 0, k == KT - 1)
            last.then_inc(unit_done, 1)

        pe.wait_ge(cst_in_s, 32)
        for k in range(KT):
            pe.wait_ge(x_in_s[k // 2], 16)
            if k >= 2:
                pe.wait_ge(xt_taken, k - 1)
            for c in range(TC):
                last = T.transpose(bank[k % 2][:, c * P:(c + 1) * P], x_tok[:, c, k * P:(k + 1) * P], ident)
            last.then_inc(xt_filled, 1)
        pe.wait_ge(consts, N_CONSTS)
        pe.wait_ge(xt_taken, KT)

        with pe.Fori(0, DEPTH) as l:
            for j in range(U_PRE):
                project(unit(l, 0, j=j), j % WSLOTS, j % 2, l * ACC_L + j // 2, xg_hi, xg_lo,
                        (xg_ready, l * 2 * KT) if j == 0 else None)
                if j == 0:
                    pe.wait_ge(ss_add, l * 2 * (KT - 1) + (KT - 1))
                    pe.wait_ge(taken[2], l * _layer(2) + 1)
                    T.matmul(bank[2][:, :], ones[:, :], ssum[:, :], start=True, stop=True).then_inc(filled[2], 1)
            pe.wait_ge(pre_sq, l * 4 + 1)
            pe.wait_ge(taken[5], l * _layer(5) + 1)
            T.matmul(bank[5][:, :], ones[0:ROPE, :], sq_kr[:, :], start=True, stop=True).then_inc(filled[5], 1)
            pe.wait_ge(pre_sq, l * 4 + 2)
            pe.wait_ge(taken[3], l * _layer(3) + 1)
            T.matmul(bank[3][:, :], ones[:, :], sq_ckv[:, :], start=True, stop=True).then_inc(filled[3], 1)
            pe.wait_ge(pre_sq, l * 4 + 4)
            pe.wait_ge(taken[4], l * _layer(4) + 1)
            T.matmul(bank[4][:, :], ones[:, :], sq_cq[:, 0, :], start=True, stop=False)
            T.matmul(bank[4][:, :], ones[:, :], sq_cq[:, 1, :], start=False, stop=True).then_inc(filled[4], 1)
            pe.wait_ge(row_v, l * ROW_V + ROWS_AT)
            pe.wait_ge(taken[7], l * _layer(7) + 1)
            pe.wait_ge(pre_n, l * PRE_N + 2)
            pe.wait_ge(taken[6], l * _layer(6) + 1)
            T.matmul(bank[6][:, :], col("swap", 0, P)[0:ROPE, :], kr_raw[:, :], start=True, stop=True).then_inc(filled[6], 1)
            for c in range(TC):
                T.transpose(bank[7][:, c * 8:c * 8 + 8], r_a[:, c * P:(c + 1) * P], ident[0:8, 0:8])
            for c in range(TC):
                last = T.transpose(bank[7][:, 32 + c * 8:40 + c * 8], r_d[:, c * P:(c + 1) * P], ident[0:8, 0:8])
            last.then_inc(filled[7], 1)

            with pe.Fori(0, HEADS) as i:
                def free(name):
                    w_free(pe, l, i, name)

                def fill(name, ins):
                    ins.then_inc(filled[USES[name][0]], 1)

                def head_unit(j, slot, b, n):
                    project(unit(l, B_HEAD, i, U_HEAD, j), slot, b, l * ACC_L + i * 3 + (A_HEAD + n), xg_hi, xg_lo)

                head_unit(0, 0, 0, 0)
                pe.wait_ge(mi_s, l * HEADS + i + 1)
                free("m_bc")
                T.matmul(bank[6][:, :], ones_r[0:64, :], mi[0:64, :], start=True, stop=False)
                fill("m_bc", T.matmul(bank[6][:, :], ident_b[:, :], after_b[:, :], start=False, stop=True))
                free("i_bc")
                fill("i_bc", T.matmul(bank[7][:, :], ones_r[64:P, :], mi[64:P, :], start=True, stop=True))
                head_unit(1, 1, 1, 0)
                w_acc(pe, 0, l * ACC_L + i * 3 + A_HEAD)
                free("k_tr")
                free("s_t")
                for c in range(TC):
                    last = T.matmul(bank[7][:, c * P:(c + 1) * P], ksb[:, c * P:(c + 1) * P], qsb[:, c * P:(c + 1) * P],
                                    start=True, stop=True)
                fill("s_t", last)
                for c in range(TC):
                    last = T.transpose(bank[6][:, c * DK:(c + 1) * DK], ksb[:, c * P:(c + 1) * P], ident[0:DK, 0:DK])
                fill("k_tr", last)
                pe.wait_ge(w_ready, unit(l, B_HEAD, i, U_HEAD, 2) + (1 + STAGES))
                pe.wait_ge(pre_n, l * PRE_N + PRE_N)
                free("q_nope")
                for name, b, off in (("q_nope", 2, 0), ("q_rope", 4, P)):
                    if b == 4:
                        free("q_rope")
                    for k in range(2):
                        o = k * 2 * P + off
                        last = split_mm(bank[b][:, :], (whi[:, 2, o:o + P], wlo[:, 2, o:o + P]),
                                        cq_hi[:, k, :], cq_lo[:, k, :], k == 0, k == 1)
                    if b == 2:
                        fill("q_nope", last)
                last.then_inc(unit_done, 1)
                pe.wait_ge(w_ready, unit(l, B_HEAD, i, U_HEAD, 3) + (1 + STAGES))
                free("k_nope")
                fill("k_nope", split_mm(bank[3][:, :], (whi[:, 3, 0:P], wlo[:, 3, 0:P]), ckv_hi[:, :], ckv_lo[:, :], True, True))
                free("v_t")
                split_mm(bank[5][:, :], (whi[:, 3, P:2 * P], wlo[:, 3, P:2 * P]), ckv_hi[:, :], ckv_lo[:, :], True, True)\
                    .then_inc(unit_done, 1)
                w_acc(pe, 1, l * ACC_L + i * 3 + A_HEAD)
                free("vm_tr")
                for c in range(TC):
                    last = T.transpose(bank[6][:, c * P:(c + 1) * P], vm_ch[:, c * P:(c + 1) * P], ident)
                fill("vm_tr", last)
                head_unit(4, 0, 0, 1)
                w_taken(pe, l, i, "k_tr")
                w_taken(pe, l, i, "vm_tr")
                free("c_loc")
                for c in range(TC - 1):
                    last = T.matmul(bank[7][0:DK, c * 129:(c + 1) * 129], kw[:, c, :], vmt[:, c, :], start=True, stop=True)
                fill("c_loc", last)
                for n, name in enumerate(("stat_q", "stat_k")):
                    pe.wait_ge(sql_s, (l * HEADS + i) * 3 + (n + 1))
                    free(name)
                    b = bank[USES[name][0]]
                    T.matmul(b[:, :], ones_r[:, :], sq_hi[n][:, :], start=True, stop=False)
                    fill(name, T.matmul(b[:, :], ones_r[:, :], sq_lo[n][:, :], start=False, stop=True))
                head_unit(5, 1, 1, 1)
                pe.wait_ge(sql_s, (l * HEADS + i) * 3 + 3)
                free("stat_r")
                fill("stat_r", T.matmul(bank[5][:, :], ones_r[:, :], q_pe[:, :], start=True, stop=True))
                w_taken(pe, l, i, "s_t")
                pe.wait_ge(qs_s, l * HEADS + i + 1)
                for half, name in ((0, "num0"), (1, "num1")):
                    free(name)
                    for c in (2 * half, 2 * half + 1):
                        o = bank[7 - half][:, (c % 2) * 129:(c % 2) * 129 + 129]
                        last = T.matmul(o, dec[:, c, :], vmt[:, c, :], start=True, stop=(c == 0))
                        if c:
                            last = T.matmul(o, qs[:, c * P:(c + 1) * P], csb[:, c - 1, :], start=False, stop=True)
                    fill(name, last)
                head_unit(6, 2, 0, 2)
                pe.wait_ge(nrm_s, (l * HEADS + i) * 2 + 2)
                pe.wait_ge(qpe_s, l * HEADS + i + 1)
                for qb in range(TC):
                    b, w = bank[2 + qb], max(256, (qb + 1) * P)
                    q = slice(qb * P, (qb + 1) * P)
                    free(f"score{qb}")
                    split_mm(b[:, 0:w], (nq_hi[:, q], nq_lo[:, q]), nk_hi[:, 0:w], nk_lo[:, 0:w], True, False)
                    T.matmul(b[:, 0:w], q_pe[:, q], kpe_h[:, 0:w], start=False, stop=False)
                    T.matmul(b[:, 0:w], q_pe[:, q], kpe_l[:, 0:w], start=False, stop=False)
                    fill(f"score{qb}", T.matmul(b[:, q], ident_b[:, :], future_b[:, :], start=False, stop=True))
                head_unit(7, 3, 1, 2)
                pe.wait_ge(p_s, (l * HEADS + i) * TC + TC)
                at = {0: (2, 0), 1: (3, 0), 2: (4, 0), 3: (4, 2 * P)}
                for kb in range(TC):
                    b, o = at[kb]
                    if kb < 3:
                        free(f"pt{kb}")
                    for qb in range(kb, TC):
                        src = (qb * (qb + 1) // 2 + kb) * P
                        last = T.transpose(bank[b][:, o + (qb - kb) * P:o + (qb - kb + 1) * P], prob[:, src:src + P], ident)
                    if kb != 2:
                        fill(f"pt{min(kb, 2)}", last)
                free("v_tr")
                for c in range(TC):
                    last = T.transpose(bank[6][:, c * P:(c + 1) * P], v_ch[:, c * P:(c + 1) * P], ident)
                fill("v_tr", last)
                free("h_tr")
                for c in range(TC):
                    last = T.transpose(bank[7][:, c * P:(c + 1) * P], htok[:, c, :], ident)
                fill("h_tr", last)
                for kb in range(3):
                    w_taken(pe, l, i, f"pt{kb}")
                w_taken(pe, l, i, "v_tr")
                free("pv")
                at = 0
                for kb in range(TC):
                    w = (TC - kb) * P
                    last = T.matmul(bank[5][:, kb * P:SEQ], v_tok[:, kb, :], prob_t[:, at:at + w],
                                    start=(kb == 0), stop=(kb == TC - 1))
                    at += w
                fill("pv", last)

            for n in range(3):
                with pe.Fori(0, 4) as i:
                    for j in range(4):
                        u = unit(l, B_MERGE + n * U_MERGE, i, 4, j)
                        a = l * ACC_L + i * 2 + (A_MERGE + n * 8 + j // 2)
                        if j % 2 == 0:
                            project(u, j, 0, a, xg_hi, xg_lo)
                        else:
                            project(u, j, 1, a, act_hi, act_lo, (act_s, (l * 7 + n) * KT) if j == 1 else None)
            with pe.Fori(0, 2) as i:
                for j in range(4):
                    project(unit(l, B_OUT, i, 4, j), j, j % 2, l * ACC_L + i * 2 + (A_OUT + j // 2), mg_hi, mg_lo,
                            (mg_s, l * KT) if j == 0 else None)
            def mlp_quad(g, i, down, stat=False):
                for j in range(4):
                    base = B_MLP + (8 if down else 0)
                    hi, lo = (act_hi, act_lo) if down else (xg_hi, xg_lo)
                    ready = (act_s, l * 7 * KT + g * KT + 3 * KT) if down else (xg_ready, l * 2 * KT + KT)
                    project(unit(l, base, g, U_MLP, j) + i * 4, j, j % 2,
                            l * ACC_L + g * 8 + i * 2 + (A_MLP + (4 if down else 0) + j // 2), hi, lo,
                            ready if j == 0 else None)
                    if stat and j == 0:
                        pe.wait_ge(ss_add, l * 2 * (KT - 1) + 2 * (KT - 1))
                        pe.wait_ge(taken[2], l * _layer(2) + _layer(2))
                        T.matmul(bank[2][:, :], ones[:, :], ssum[:, :], start=True, stop=True).then_inc(filled[2], 1)

            mlp_quad(0, 0, False, stat=True)
            mlp_quad(0, 1, False)
            with pe.Fori(0, 2) as i:
                mlp_quad(0, i, True)
            with pe.Fori(1, FG) as g:
                with pe.Fori(0, 2) as i:
                    mlp_quad(g, i, False)
                with pe.Fori(0, 2) as i:
                    mlp_quad(g, i, True)

        for b in range(2):
            pe.wait_ge(taken[b], DEPTH * ACC_L + 1)
        for k in range(KT):
            if k >= 2:
                pe.wait_ge(xt_taken, KT + k - 1)
            for c in range(TC):
                last = T.transpose(bank[k % 2][:, c * P:(c + 1) * P], xT[:, k, c * P:(c + 1) * P], ident)
            last.then_inc(xt_filled, 1)

    @block.scalar
    def _(act):
        def hi(l, base, i, per, j):
            slot = (base + j) % WSLOTS
            act.wait_ge(stage_in[slot % STAGES], (l * (UNITS // 2) + i * (per // 2) + (base + j) // 2) * 16 + 16)
            act.wait_ge(unit_done, unit(l, base, i, per, j) + 1)
            S.activation(whi[:, slot, :], stage[:, slot % STAGES, :], ACT.Copy).then_inc(hi_ready, 1)

        def main_rstd(l, norm):
            act.wait_ge(filled[2], l * _layer(2, True) + (_layer(2, True) if norm else 1))
            S.activation(rstd[:, :], bank[2][:, :], ACT.Ln, scale=1.0 / D_MODEL, bias=eps[:, :]).then_inc(rs_step, 1)
            act.wait_ge(rs_step, l * 4 + (norm * 2 + 1))
            S.activation(rstd[:, :], rstd[:, :], ACT.Exp, scale=-0.5).then_inc(rs_step, 1)

        def squares(norm, k):
            if k >= 2:
                act.wait_ge(ss_add, norm * (KT - 1) + (k - 1))
            S.activation(ssum[:, :] if k == 0 else sqx[:, :], xT[:, k, :], ACT.Square).then_inc(x_sq, 1)

        act.dma_start(pos_i[:, :], pos_in.partition_broadcast(P)).then_inc(pos_in_s, 16)
        act.wait_ge(consts, N_CONSTS)
        for k in range(KT):
            act.wait_ge(xt_taken, k + 1)
            squares(0, k)
            if k < 4:
                hi(0, 0, 0, 0, k)
        act.wait_ge(trig, N_TRIG)
        S.activation(cs[0:64, :], red[0:64, :], ACT.Sin, scale=-1.0, bias=halfpi[0:64, :]).then_inc(trig_done, 1)
        S.activation(cs[64:P, :], red[64:P, :], ACT.Sin, scale=col("sign")[64:P, :]).then_inc(trig_done, 1)

        with act.Fori(0, DEPTH) as l:
            S.preload_act_table_set("natural_log_exp_and_others")
            act.wait_ge(xg_ready, l * 2 * KT + KT)
            act.dma_start(par[:, :], par_in[l, :, :]).then_inc(par_in_s, 16)
            main_rstd(l, 0)
            hi(l, 0, 0, 0, 4)
            act.wait_ge(pre_raw, l * 2 + 1)
            S.activation(sq_kr[:, :], kr_raw[:, :], ACT.Square).then_inc(pre_sq, 1)
            act.wait_ge(row_v, l * ROW_V + 2)
            S.activation(r_i[:, :], r_i[:, :], ACT.Tanh).then_inc(row_s, 1)
            S.activation(r_f[:, :], r_f[:, :], ACT.Tanh).then_inc(row_s, 1)
            S.preload_act_table_set("natural_log_exp_and_others")
            act.wait_ge(row_s, l * 8 + 2)
            S.activation(r_f[:, :], r_f[:, :], ACT.Exp, scale=-GATE_CAP).then_inc(row_s, 1)
            act.wait_ge(row_s, l * 8 + 3)
            S.activation(r_f[:, :], r_f[:, :], ACT.Ln, bias=ones[0:HEADS, 0:1]).then_inc(row_s, 1)
            hi(l, 0, 0, 0, 5)
            w_acc(act, 1, l * ACC_L)
            S.activation(sq_ckv[:, :], ckv_raw[:, :], ACT.Square).then_inc(pre_sq, 1)
            for k in range(2):
                w_acc(act, k, l * ACC_L + 1)
                S.activation(sq_cq[:, k, :], cq_raw[:, k, :], ACT.Square).then_inc(pre_sq, 1)
            for n, (b, dst, width, rows) in enumerate(((5, sq_kr[:, :], ROPE, ROPE), (3, sq_ckv[:, :], KV_LORA, P),
                                                       (4, sq_cq[:, 0, :], Q_LORA, P))):
                act.wait_ge(filled[b], l * _layer(b, True) + 1)
                S.activation(dst, bank[b][0:rows, :], ACT.Ln, scale=1.0 / width, bias=eps[0:rows, :]).then_inc(taken[b], 1)
                act.wait_ge(taken[b], l * _layer(b) + 2)
                S.activation(dst, dst, ACT.Exp, scale=-0.5).then_inc(pre_rs, 1)
            for c in range(TC):
                act.wait_ge(row_v, l * ROW_V + (9 + 3 * c))
                S.activation(r_e[:, c * P:(c + 1) * P], r_m[:, c * P:(c + 1) * P], ACT.Exp,
                             scale=-1.0, bias=m_prev[:, c:c + 1]).then_inc(row_s, 1)
            act.wait_ge(filled[7], l * _layer(7, True) + 1)
            S.activation(acol[:, :, :], bank[7][:, 0:32].rearrange("p (c h) -> p c h", h=8), ACT.Copy).then_inc(head_in, 1)
            S.activation(emt[:, :, :], bank[7][:, 32:64].rearrange("p (c h) -> p c h", h=8), ACT.Exp).then_inc(taken[7], 1)

            with act.Fori(0, HEADS) as i:
                def head_hi(j):
                    hi(l, B_HEAD, i, U_HEAD, j)

                it = l * HEADS + i
                head_hi(2)
                act.wait_ge(head_in, l + 1)
                w_filled(act, l, i, "m_bc")
                for c in range(TC):
                    ins = S.activation(dec[:, c, :], bank[6][:, c * P:(c + 1) * P], ACT.Exp, scale=-1.0,
                                       bias=acol[:, c, bass.ds(i, 1)])
                    ins.then_inc(taken[6] if c == TC - 1 else dec_s, 1)
                head_hi(3)
                head_hi(4)
                head_hi(5)
                w_filled(act, l, i, "q_nope")
                S.activation(sq_hi[0][:, :], bank[2][:, :], ACT.Square).then_inc(sq_s, 1)
                S.activation(nq[:, :], bank[2][:, :], ACT.Square).then_inc(sq_s, 1)
                head_hi(6)
                w_filled(act, l, i, "k_nope")
                w_filled(act, l, i, "vm_tr")
                S.activation(sq_hi[1][:, :], bank[3][:, :], ACT.Square).then_inc(sq_s, 1)
                S.activation(nk[:, :], bank[3][:, :], ACT.Square).then_inc(sq_s, 1)
                w_unit(act, unit(l, B_HEAD, i, U_HEAD, 2))
                S.activation(q_pe[0:ROPE, :], bank[4][0:ROPE, :], ACT.Square).then_inc(sq_s, 1)
                S.activation(nr[:, :], bank[4][0:ROPE, :], ACT.Square).then_inc(sq_s, 1)
                head_hi(7)
                for n, (name, dst, rows) in enumerate((("stat_q", nq, P), ("stat_k", nk, P), ("stat_r", nr, ROPE))):
                    if n == 2:
                        w_acc(act, 0, l * ACC_L + i * 3 + (A_HEAD + 1))
                        S.activation(so[:, :], so[:, :], ACT.Sigmoid).then_inc(so_s, 1)
                        S.preload_act_table_set("natural_log_exp_and_others")
                    w_filled(act, l, i, name)
                    b = USES[name][0]
                    S.activation(dst[:, :], bank[b][0:rows, :], ACT.Ln, scale=1.0 / rows).then_inc(rs_s, 1)
                    act.wait_ge(rs_s, it * 6 + (2 * n + 1))
                    S.activation(dst[:, :], dst[:, :], ACT.Exp, scale=-0.5).then_inc(rs_s, 1)
                head_hi(8)
                for c in range(TC):
                    if c % 2 == 0:
                        act.wait_ge(fin_s, it * 8 + c // 2 + 1)
                    S.activation(tmp_n[:, c * DV:(c + 1) * DV], bank[7 - c // 2][:, (c % 2) * 129:(c % 2) * 129 + DV], ACT.Square,
                                 accum_out=sm[:, SS, c:c + 1]).then_inc(ss_s, 1)
                head_hi(9)
                act.wait_ge(nm_s, it + 1)
                for qb in range(TC):
                    o = qb * (qb + 1) // 2 * P
                    S.activation(prob[:, o:o + (qb + 1) * P], bank[2 + qb][:, 0:(qb + 1) * P], ACT.Exp,
                                 scale=(NOPE + ROPE) ** -0.5, bias=sm[:, NM, qb:qb + 1],
                                 accum_out=sm[:, SUM, qb:qb + 1]).then_inc(taken[2 + qb], 1)
                act.wait_ge(fin_s, it * 8 + 7)
                S.activation(sm[:, LN, :], sm[:, TT, :], ACT.Ln, scale=1.0 / DV, bias=eps[:, :]).then_inc(hr_s, 1)
                act.wait_ge(hr_s, it * 2 + 1)
                S.activation(sm[:, HR, :], sm[:, LN, :], ACT.Exp, scale=-0.5).then_inc(hr_s, 1)
                w_filled(act, l, i, "pt0")
                S.activation(prob_t[:, 0:512], bank[2][:, :], ACT.Copy).then_inc(taken[2], 1)
                w_filled(act, l, i, "v_tr")
                S.activation(v_tok[:, :, :], bank[6][:, :].rearrange("p (c d) -> p c d", d=DV), ACT.Copy)\
                    .then_inc(taken[6], 1)
                w_filled(act, l, i, "pv")
                S.activation(ysC[:, i, :], bank[5][:, :], ACT.Copy).then_inc(taken[5], 1)

            S.preload_act_table_set("sigmoid_and_others")
            for n in range(3):
                with act.Fori(0, 4) as i:
                    for j in range(4):
                        hi(l, B_MERGE + n * U_MERGE, i, 4, j + 2)
                        if j % 2 == 0:
                            w_acc(act, 0, l * ACC_L + i * 2 + (A_MERGE + n * 8 + j // 2))
                            g = gsig[j // 2]
                            S.activation(g[:, :], g[:, :], ACT.Sigmoid).then_inc(g_s, 1)
            S.preload_act_table_set("natural_log_exp_and_others")
            for k in range(KT):
                hi(l, B_OUT, 0, 0, k + 2)
                w_acc(act, k % 2, l * ACC_L + (A_OUT + k // 2))
                squares(l * 2 + 1, k)
            main_rstd(l, 1)
            with act.Fori(0, FG * U_MLP // 4 - 2) as i:
                for j in range(4):
                    hi(l, B_MLP, i, 4, j + 2)
            for k in range(KT):
                if k < KT - 2:
                    hi(l, B_MLP + FG * U_MLP - KT, 0, 0, k + 2)
                else:
                    with act.If(l < DEPTH - 1):
                        hi(l, UNITS - KT, 0, 0, k + 2)
                w_acc(act, k % 2, l * ACC_L + (ACC_L - KT // 2 + k // 2))
                squares(l * 2 + 2, k)
            with act.If(l < DEPTH - 1):
                for k in range(2):
                    hi(l, UNITS, 0, 0, k + 2)

    @block.vector
    def _(dve):
        def split_x(norm, k, g):
            V.tensor_scalar(xg_hi[:, k, :], xT[:, k, :], g, None, ALU.mult).then_inc(xg_hi_s, 1)
            dve.wait_ge(xg_hi_s, norm * KT + (k + 1))
            V.scalar_tensor_tensor(out=xg_lo[:, k, :], in0=xT[:, k, :], scalar=g, in1=xg_hi[:, k, :].bitcast(f32),
                                   op0=ALU.mult, op1=ALU.subtract).then_inc(xg_ready, 1)
            dve.wait_ge(x_sq, norm * KT + (k + 1))
            if k:
                if k > 1:
                    dve.wait_ge(ss_add, norm * (KT - 1) + (k - 1))
                V.tensor_tensor(ssum[:, :], ssum[:, :], sqx[:, :], ALU.add).then_inc(ss_add, 1)

        def newton(l, norm):
            base = norm * 4
            dve.wait_ge(filled[2], l * _layer(2, True) + (_layer(2, True) if norm else 1))
            dve.wait_ge(rs_step, l * 4 + (norm * 2 + 1))
            V.tensor_scalar(ev_n[:, :], bank[2][:, :], 1.0 / D_MODEL, EPS, ALU.mult, ALU.add).then_inc(taken[2], 1)
            dve.wait_ge(rs_step, l * 4 + (norm * 2 + 2))
            V.tensor_tensor(ev_t[:, :], rstd[:, :], rstd[:, :], ALU.mult).then_inc(nw, 1)
            dve.wait_ge(nw, l * 8 + (base + 1))
            dve.wait_ge(taken[2], l * _layer(2) + ((_layer(2) if norm else 1) + 1))
            V.tensor_tensor(ev_t[:, :], ev_t[:, :], ev_n[:, :], ALU.mult).then_inc(nw, 1)
            dve.wait_ge(nw, l * 8 + (base + 2))
            V.tensor_scalar(ev_t[:, :], ev_t[:, :], -0.5, 1.5, ALU.mult, ALU.add).then_inc(nw, 1)
            dve.wait_ge(nw, l * 8 + (base + 3))
            V.tensor_tensor(rstd[:, :], rstd[:, :], ev_t[:, :], ALU.mult).then_inc(nw, 1)

        dve.wait_ge(cst_in_s, 32)
        V.tensor_copy(ident_b[:, :], ident).then_inc(consts, 1)
        V.tensor_copy(future_b[:, :], masks[:, 1, :]).then_inc(consts, 1)
        V.memset(ones[:, :], 1.0).then_inc(consts, 1)
        for c in range(TC):
            V.tensor_copy(after_b[:, c * P:(c + 1) * P], masks[:, 0, :]).then_inc(consts, 1)
        dve.wait_ge(consts, N_CONSTS)
        for k in range(KT):
            dve.wait_ge(xt_filled, k + 1)
            V.tensor_copy(xT[:, k, :], bank[k % 2][:, :]).then_inc(xt_taken, 1)
            dve.wait_ge(xt_taken, k + 1)
            split_x(0, k, col("mix0", k))
        dve.wait_ge(pos_in_s, 16)
        step = 0

        def link(ins):
            nonlocal step
            step += 1
            ins.then_inc(trig, 1)
            dve.wait_ge(trig, step)

        link(V.tensor_copy(ang[:, :], pos_i[:, :]))
        link(V.tensor_scalar(ang[:, :], ang[:, :], col("freq"), None, ALU.mult))
        link(V.tensor_scalar(turns[:, :], ang[:, :], 1.0 / (2 * math.pi), None, ALU.mult))
        link(V.tensor_scalar(turns[:, :], turns[:, :], 12582912.0, None, ALU.add))
        link(V.tensor_scalar(turns[:, :], turns[:, :], 12582912.0, None, ALU.subtract))
        left, parts = 2 * math.pi, []
        for bits in (5, 13, 21):
            parts.append(math.floor(left * 2 ** bits) / 2 ** bits)
            left -= parts[-1]
        for part in (*parts, left):
            link(V.scalar_tensor_tensor(out=ang[:, :], in0=turns[:, :], scalar=-part, in1=ang[:, :],
                                        op0=ALU.mult, op1=ALU.add))
        link(V.tensor_scalar(red[:, :], ang[:, :], 3.1415925, -3.1415925, ALU.min, ALU.max))
        link(V.tensor_scalar(ang[0:64, :], red[0:64, :], -1.0, None, ALU.mult))
        link(V.tensor_tensor(red[0:64, :], red[0:64, :], ang[0:64, :], ALU.max))
        assert step == N_TRIG

        with dve.Fori(0, DEPTH) as l:
            newton(l, 0)
            dve.wait_ge(nw, l * 8 + 4)
            w_unit(dve, unit(l, 0))
            V.tensor_tensor(kr_raw[:, :], bank[0][0:64, :], rstd[0:64, :], ALU.mult).then_inc(pre_raw, 1)
            V.tensor_tensor(r_i[:, :], bank[0][64:72, :], rstd[64:72, :], ALU.mult).then_inc(pre_raw, 1)
            V.tensor_tensor(r_f[:, :], bank[0][96:104, :], rstd[96:104, :], ALU.mult).then_inc(taken[0], 1)
            dve.wait_ge(par_in_s, l * 16 + 16)
            dve.wait_ge(pre_raw, l * 2 + 2)
            V.tensor_scalar(r_i[:, :], r_i[:, :], gain("b_i", 0, slice(0, 8)), 1.0 / GATE_CAP, ALU.add, ALU.mult).then_inc(row_v, 1)
            w_acc(dve, 0, l * ACC_L)
            V.tensor_scalar(r_f[:, :], r_f[:, :], gain("b_f", 0, slice(0, 8)), 1.0 / GATE_CAP, ALU.add, ALU.mult).then_inc(row_v, 1)
            w_unit(dve, unit(l, 0, j=1))
            V.tensor_tensor(ckv_raw[:, :], bank[1][:, :], rstd[:, :], ALU.mult).then_inc(taken[1], 1)
            dve.wait_ge(trig_done, 2)
            V.tensor_scalar(gcs[:, :], cs[:, :], gain("q_rope"), None, ALU.mult).then_inc(pre_n, 1)
            dve.wait_ge(row_s, l * 8 + 4)
            for c in range(TC):
                V.tensor_tensor_scan(r_nb[:, c * P:(c + 1) * P], ones[0:HEADS, :], r_f[:, c * P:(c + 1) * P], 0.0,
                                     ALU.mult, ALU.add).then_inc(row_v, 1)
            dve.wait_ge(row_v, l * ROW_V + 6)
            V.scalar_tensor_tensor(out=r_a[:, :], in0=r_i[:, :], scalar=GATE_CAP, in1=r_nb[:, :], op0=ALU.mult,
                                   op1=ALU.add).then_inc(row_v, 1)
            V.memset(m_prev[:, 0:1], 0.0).then_inc(row_v, 1)
            dve.wait_ge(row_v, l * ROW_V + 8)
            for c in range(TC):
                s = slice(c * P, (c + 1) * P)
                V.tensor_tensor_scan(r_m[:, s], r_a[:, s], r_a[:, s], m_prev[:, c:c + 1], ALU.max, ALU.max)\
                    .then_inc(row_v, 1)
                dve.wait_ge(row_v, l * ROW_V + (9 + 3 * c))
                V.tensor_tensor(m_prev[:, c + 1:c + 2], r_m[:, (c + 1) * P - 1:(c + 1) * P],
                                r_nb[:, (c + 1) * P - 1:(c + 1) * P], ALU.subtract).then_inc(row_v, 1)
                V.tensor_tensor(r_d[:, s], r_nb[:, s], r_m[:, s], ALU.subtract).then_inc(row_v, 1)
                dve.wait_ge(row_v, l * ROW_V + (11 + 3 * c))
            V.tensor_copy(rows_mi[0:8, :], r_m[:, :]).then_inc(row_v, 1)
            dve.wait_ge(row_v, l * ROW_V + 21)
            V.tensor_tensor(rows_mi[32:40, :], r_m[:, :], rows_mi[0:8, :].bitcast(f32), ALU.subtract).then_inc(row_v, 1)
            for k in range(2):
                w_unit(dve, unit(l, 0, j=2 + k))
                V.tensor_tensor(cq_raw[:, k, :], bank[k][:, :], rstd[:, :], ALU.mult).then_inc(taken[k], 1)
            dve.wait_ge(pre_rs, l * 3 + 1)
            V.scalar_tensor_tensor(out=kr_raw[:, :], in0=kr_raw[:, :], scalar=gain("k_rope", 0, slice(0, 64)), in1=sq_kr[:, :],
                                   op0=ALU.mult, op1=ALU.mult).then_inc(pre_n, 1)
            dve.wait_ge(pre_rs, l * 3 + 3)
            V.scalar_tensor_tensor(out=ckv_raw[:, :], in0=ckv_raw[:, :], scalar=gain("kva"), in1=sq_ckv[:, :],
                                   op0=ALU.mult, op1=ALU.mult).then_inc(pre_n, 1)
            for k in range(2):
                V.scalar_tensor_tensor(out=cq_raw[:, k, :], in0=cq_raw[:, k, :], scalar=gain("qa", k), in1=sq_cq[:, 0, :],
                                       op0=ALU.mult, op1=ALU.mult).then_inc(pre_n, 1)
            dve.wait_ge(pre_n, l * PRE_N + 5)
            V.tensor_copy(ckv_hi[:, :], ckv_raw[:, :]).then_inc(pre_n, 1)
            V.tensor_copy(cq_hi[:, :, :], cq_raw[:, :, :]).then_inc(pre_n, 1)
            dve.wait_ge(pre_n, l * PRE_N + 7)
            V.tensor_tensor(ckv_lo[:, :], ckv_raw[:, :], ckv_hi[:, :].bitcast(f32), ALU.subtract).then_inc(pre_n, 1)
            V.tensor_tensor(cq_lo[:, :, :], cq_raw[:, :, :], cq_hi[:, :, :].bitcast(f32), ALU.subtract).then_inc(pre_n, 1)
            dve.wait_ge(filled[6], l * _layer(6, True) + 1)
            V.tensor_tensor(kpe[:, :], bank[6][64:P, :], cs[64:P, :], ALU.mult).then_inc(taken[6], 1)
            V.tensor_tensor(sq_kr[:, :], kr_raw[:, :], cs[0:64, :], ALU.mult).then_inc(pre_n, 1)
            dve.wait_ge(taken[6], l * _layer(6) + 2)
            dve.wait_ge(pre_n, l * PRE_N + 10)
            V.tensor_tensor(kpe[:, :], kpe[:, :], sq_kr[:, :], ALU.add).then_inc(pre_n, 1)
            dve.wait_ge(pre_n, l * PRE_N + 11)
            for r0 in (0, 64):
                V.tensor_copy(kpe_h[r0:r0 + ROPE, :], kpe[:, :]).then_inc(pre_n, 1)
            dve.wait_ge(pre_n, l * PRE_N + 13)
            for r0 in (0, 64):
                V.tensor_tensor(kpe_l[r0:r0 + ROPE, :], kpe[:, :], kpe_h[0:ROPE, :].bitcast(f32), ALU.subtract).then_inc(
                    pre_n, 1)
            dve.wait_ge(row_s, l * 8 + 8)
            V.tensor_copy(rows_mi[64:72, :], r_e[:, :]).then_inc(row_v, 1)
            dve.wait_ge(row_v, l * ROW_V + 23)
            V.tensor_tensor(rows_mi[96:104, :], r_e[:, :], rows_mi[64:72, :].bitcast(f32), ALU.subtract).then_inc(row_v, 1)
            dve.wait_ge(taken[7], l * _layer(7) + 2)
            dve.wait_ge(row_v, l * ROW_V + ROW_V)
            V.memset(vmt[:, :, DV:DV + 1], 1.0).then_inc(pre_n, 1)

            with dve.Fori(0, HEADS) as i:
                dve.wait_ge(pre_n, l * PRE_N + PRE_N)
                dve.wait_ge(row_v, l * ROW_V + ROW_V)
                it = l * HEADS + i
                A = l * ACC_L + i * 3 + A_HEAD

                def w_head_unit(j):
                    w_unit(dve, unit(l, B_HEAD, i, U_HEAD, j))

                V.tensor_scalar(mi[:, :], rows_mi[:, :].bitcast(f32), cst[:, bass.ds(i + CST["onehot"], 1)], None, ALU.mult)\
                    .then_inc(mi_s, 1)
                w_head_unit(0)
                V.scalar_tensor_tensor(out=qsb[:, :], in0=bank[0][0:DK, :], scalar=DK ** -0.5, in1=rstd[0:DK, :],
                                       op0=ALU.mult, op1=ALU.mult).then_inc(q_s, 1)
                V.tensor_tensor(ksb[:, :], bank[0][DK:P, :], rstd[DK:P, :], ALU.mult).then_inc(taken[0], 1)
                w_filled(dve, l, i, "i_bc")
                dve.wait_ge(q_s, it + 1)
                V.tensor_tensor(qs[:, :], bank[7][0:DK, :], qsb[:, :], ALU.mult).then_inc(qs_s, 1)
                V.tensor_copy(sold[:, :], bank[7][0:DK, P - 1:SEQ:P]).then_inc(taken[7], 1)
                w_head_unit(1)
                V.tensor_tensor(vm_ch[:, :], bank[1][:, :], rstd[:, :], ALU.mult).then_inc(taken[1], 1)
                w_filled(dve, l, i, "k_tr")
                w_taken(dve, l, i, "m_bc")
                for c in range(TC):
                    V.tensor_scalar(kw[:, c, :], bank[6][:, c * DK:(c + 1) * DK], dec[:, c, P - 1:P], None, ALU.mult)\
                        .then_inc(taken[6] if c == TC - 1 else kw_s, 1)
                w_filled(dve, l, i, "s_t")
                w_taken(dve, l, i, "k_tr")
                V.tensor_tensor(dec[:, :, :], bank[7][:, :].rearrange("p (c t) -> p c t", t=P), dec[:, :, :], ALU.mult)\
                    .then_inc(taken[7], 1)
                w_head_unit(3)
                V.tensor_copy(v_ch[:, :], bank[5][:, :]).then_inc(taken[5], 1)
                w_filled(dve, l, i, "vm_tr")
                V.tensor_copy(vmt[:, :, 0:DV], bank[6][:, :].rearrange("p (c d) -> p c d", d=DV)).then_inc(taken[6], 1)
                for n, (sq, hi_, lo_) in enumerate(((nq[:, :], sq_hi[0][:, :], sq_lo[0][:, :]),
                                                    (nk[:, :], sq_hi[1][:, :], sq_lo[1][:, :]),
                                                    (nr[:, :], q_pe[0:ROPE, :], q_pe[ROPE:P, :]))):
                    dve.wait_ge(sq_s, it * 6 + (2 * n + 2))
                    V.scalar_tensor_tensor(out=lo_, in0=sq, scalar=EPS, in1=hi_.bitcast(f32), op0=ALU.add,
                                           op1=ALU.subtract).then_inc(sql_s, 1)
                V.tensor_tensor(ksb[:, :], bank[4][0:ROPE, :], gcs[0:ROPE, :], ALU.mult).then_inc(chain, 1)
                V.tensor_tensor(qsb[:, :], bank[4][ROPE:P, :], gcs[ROPE:P, :], ALU.mult).then_inc(taken[4], 1)
                dve.wait_ge(chain, it * CH + 1)
                w_taken(dve, l, i, "q_rope")
                V.tensor_tensor(ksb[:, :], ksb[:, :], qsb[:, :], ALU.add).then_inc(chain, 1)
                w_head_unit(4)
                V.tensor_tensor(so[:, :], bank[0][:, :], rstd[:, :], ALU.mult).then_inc(taken[0], 1)
                w_filled(dve, l, i, "c_loc")
                V.tensor_copy(csb[:, 0, :], bank[7][0:DK, 0:129]).then_inc(c_s, 1)
                for c in (1, 2):
                    dve.wait_ge(c_s, it * 2 + c)
                    V.scalar_tensor_tensor(out=csb[:, c, :], in0=csb[:, c - 1, :], scalar=sold[:, c:c + 1],
                                           in1=bank[7][0:DK, c * 129:(c + 1) * 129], op0=ALU.mult, op1=ALU.add)\
                        .then_inc(c_s if c == 1 else taken[7], 1)
                def refine(n, at, name, y):
                    rows = y.shape[0]
                    t = tmp_n[0:rows, :]
                    dve.wait_ge(rs_s, it * 6 + (2 * n + 2))
                    V.tensor_tensor(t, y, y, ALU.mult).then_inc(chain, 1)
                    dve.wait_ge(chain, it * CH + at)
                    V.scalar_tensor_tensor(out=t, in0=bank[USES[name][0]][0:rows, :], scalar=-0.5 / rows, in1=t,
                                           op0=ALU.mult, op1=ALU.mult).then_inc(taken[USES[name][0]], 1)
                    w_taken(dve, l, i, name)
                    V.scalar_tensor_tensor(out=y, in0=t, scalar=1.5, in1=y, op0=ALU.add, op1=ALU.mult).then_inc(chain, 1)
                    dve.wait_ge(chain, it * CH + (at + 1))

                for n, (b, y, name, hi_, lo_) in enumerate(((2, nq, "q_nope", nq_hi, nq_lo), (3, nk, "k_nope", nk_hi, nk_lo))):
                    refine(n, 3 + 3 * n, ("stat_q", "stat_k")[n], y[:, :])
                    V.scalar_tensor_tensor(out=y[:, :], in0=bank[b][:, :], scalar=gain(name), in1=y[:, :],
                                           op0=ALU.mult, op1=ALU.mult).then_inc(taken[b], 1)
                    w_taken(dve, l, i, name)
                    V.tensor_copy(hi_[:, :], y[:, :]).then_inc(chain, 1)
                    dve.wait_ge(chain, it * CH + (5 + 3 * n))
                    V.tensor_tensor(lo_[:, :], y[:, :], hi_[:, :].bitcast(f32), ALU.subtract).then_inc(nrm_s, 1)
                w_head_unit(5)
                V.tensor_tensor(cb[:, :], bank[1][:, :], rstd[:, :], ALU.mult).then_inc(taken[1], 1)
                refine(2, 9, "stat_r", nr[:, :])
                V.tensor_tensor(ksb[:, :], ksb[:, :], nr[:, :], ALU.mult).then_inc(chain, 1)
                dve.wait_ge(chain, it * CH + 11)
                V.tensor_copy(q_pe[0:ROPE, :], ksb[:, :]).then_inc(chain, 1)
                dve.wait_ge(chain, it * CH + 12)
                V.tensor_tensor(q_pe[ROPE:P, :], ksb[:, :], q_pe[0:ROPE, :].bitcast(f32), ALU.subtract).then_inc(qpe_s, 1)
                w_filled(dve, l, i, "num0")
                V.tensor_copy(sm[:, DEN, 0:2], bank[7][:, 128:258:129]).then_inc(fin_s, 1)
                w_filled(dve, l, i, "num1")
                V.tensor_copy(sm[:, DEN, 2:4], bank[6][:, 128:258:129]).then_inc(fin_s, 1)
                dve.wait_ge(fin_s, it * 8 + 2)
                V.scalar_tensor_tensor(out=sm[:, ADEN, :], in0=sm[:, DEN, :], scalar=-1.0, in1=sm[:, DEN, :],
                                       op0=ALU.mult, op1=ALU.max).then_inc(fin_s, 1)
                dve.wait_ge(fin_s, it * 8 + 3)
                V.tensor_tensor(sm[:, DD, :], sm[:, ADEN, :], emt[:, :, i], ALU.max).then_inc(fin_s, 1)
                dve.wait_ge(fin_s, it * 8 + 4)
                V.reciprocal(sm[:, RR, :], sm[:, DD, :]).then_inc(fin_s, 1)
                dve.wait_ge(fin_s, it * 8 + 5)
                V.tensor_tensor(sm[:, R2, :], sm[:, RR, :], sm[:, RR, :], ALU.mult).then_inc(fin_s, 1)
                dve.wait_ge(fin_s, it * 8 + 6)
                dve.wait_ge(ss_s, it * 4 + 4)
                V.tensor_tensor(sm[:, TT, :], sm[:, R2, :], sm[:, SS, :], ALU.mult).then_inc(fin_s, 1)
                w_head_unit(6)
                V.tensor_tensor(cc[:, :], bank[0][:, :], rstd[:, :], ALU.mult).then_inc(taken[0], 1)
                for qb in range(TC):
                    w_filled(dve, l, i, f"score{qb}")
                    V.reduce_max(sm[:, MX, qb:qb + 1], bank[2 + qb][:, 0:(qb + 1) * P], axis=AX.X).then_inc(mx_s, 1)
                dve.wait_ge(mx_s, it * 4 + 4)
                V.tensor_scalar(sm[:, NM, :], sm[:, MX, :], -(NOPE + ROPE) ** -0.5, None, ALU.mult).then_inc(nm_s, 1)
                for qb in range(TC):
                    w_taken(dve, l, i, f"score{qb}")
                V.reciprocal(sm[:, RINV, :], sm[:, SUM, :]).then_inc(rinv_s, 1)
                dve.wait_ge(rinv_s, it + 1)
                for qb in range(TC):
                    o = qb * (qb + 1) // 2 * P
                    V.tensor_scalar(prob[:, o:o + (qb + 1) * P], prob[:, o:o + (qb + 1) * P], sm[:, RINV, qb:qb + 1], None,
                                    ALU.mult).then_inc(p_s, 1)
                dve.wait_ge(hr_s, it * 2 + 2)
                V.tensor_tensor(sm[:, FF, :], sm[:, RR, :], sm[:, HR, :], ALU.mult).then_inc(fin_s, 1)
                dve.wait_ge(fin_s, it * 8 + 8)
                for c in range(TC):
                    b = 7 - c // 2
                    V.tensor_scalar(htok[:, c, :], bank[b][:, (c % 2) * 129:(c % 2) * 129 + DV], sm[:, FF, c:c + 1], None,
                                    ALU.mult).then_inc(taken[b] if c % 2 else h_s, 1)
                w_filled(dve, l, i, "pt1")
                V.tensor_copy(prob_t[:, 512:896], bank[3][:, 0:384]).then_inc(taken[3], 1)
                w_filled(dve, l, i, "pt2")
                V.tensor_copy(prob_t[:, 896:1280], bank[4][:, 0:384]).then_inc(taken[4], 1)
                w_filled(dve, l, i, "h_tr")
                dve.wait_ge(so_s, it + 1)
                V.scalar_tensor_tensor(out=ysB[:, i, :], in0=bank[7][:, :], scalar=par[:, bass.ds(i + PAR["head"], 1)],
                                       in1=so[:, :], op0=ALU.mult, op1=ALU.mult).then_inc(taken[7], 1)
                w_head_unit(7)
                V.tensor_tensor(zp[:, 2:SEQ + 2], bank[1][:, :], rstd[:, :], ALU.mult).then_inc(taken[1], 1)
                w_acc(dve, 1, A + 2)
                w_acc(dve, 0, A + 2)
                V.tensor_tensor(zp[:, 2:SEQ + 2], zp[:, 2:SEQ + 2], cc[:, :], ALU.mult).then_inc(conv_s, 1)
                dve.wait_ge(conv_s, it * 5 + 1)
                for j in range(3):
                    w = par[:, bass.ds(i * 3 + (PAR["conv"] + j), 1)]
                    if j == 0:
                        V.tensor_scalar(cc[:, :], zp[:, 0:SEQ], w, None, ALU.mult).then_inc(conv_s, 1)
                    else:
                        V.scalar_tensor_tensor(out=cc[:, :], in0=zp[:, j:j + SEQ], scalar=w, in1=cc[:, :],
                                               op0=ALU.mult, op1=ALU.add).then_inc(conv_s, 1)
                    dve.wait_ge(conv_s, it * 5 + 2 + j)
                V.tensor_tensor(ysA[:, i, :], cb[:, :], cc[:, :], ALU.mult).then_inc(conv_s, 1)

            dve.wait_ge(conv_s, (l + 1) * HEADS * 5)
            dve.wait_ge(taken[5], (l + 1) * _layer(5) + 1)
            for n, ys in enumerate((ysA, ysB, ysC)):
                if n:
                    w_unit(dve, unit(l, B_MERGE + n * U_MERGE - 1))
                for k in range(KT):
                    V.tensor_copy(act_hi[:, k, :], ys[:, k, :]).then_inc(act_h, 1)
                    dve.wait_ge(act_h, (l * 7 + n) * KT + k + 1)
                    V.tensor_tensor(act_lo[:, k, :], ys[:, k, :], act_hi[:, k, :].bitcast(f32), ALU.subtract).then_inc(act_s, 1)
                with dve.Fori(0, 4) as i:
                    dve.wait_ge(act_s, (l * 7 + n + 1) * KT)
                    for j in range(2):
                        a = l * ACC_L + i * 2 + (A_MERGE + n * 8 + j)
                        m = l * 3 * KT + i * 2 + (n * KT + j)
                        g = gsig[j]
                        mk = merged[:, i * 2 + j, :]
                        w_unit(dve, unit(l, B_MERGE + n * U_MERGE, i, 4, 2 * j))
                        V.tensor_tensor(g[:, :], bank[0][:, :], rstd[:, :], ALU.mult).then_inc(taken[0], 1)
                        w_unit(dve, unit(l, B_MERGE + n * U_MERGE, i, 4, 2 * j + 1))
                        dve.wait_ge(g_s, m + 1)
                        V.tensor_tensor(mk if n == 0 else ev_n[:, :], bank[1][:, :], g[:, :], ALU.mult).then_inc(taken[1], 1)
                        if n:
                            w_acc(dve, 1, a)
                            V.tensor_tensor(mk, mk, ev_n[:, :], ALU.add).then_inc(mg_a, 1)
                        if n == 2:
                            dve.wait_ge(mg_a, l * 2 * KT + i * 2 + (KT + j + 1))
                            V.tensor_copy(mg_hi[:, i * 2 + j, :], mk).then_inc(mg_h, 1)
                            dve.wait_ge(mg_h, l * KT + i * 2 + (j + 1))
                            V.tensor_tensor(mg_lo[:, i * 2 + j, :], mk, mg_hi[:, i * 2 + j, :].bitcast(f32), ALU.subtract)\
                                .then_inc(mg_s, 1)
            for k in range(KT):
                w_unit(dve, unit(l, B_OUT, j=k))
                V.tensor_tensor(xT[:, k, :], xT[:, k, :], bank[k % 2][:, :], ALU.add).then_inc(taken[k % 2], 1)
                w_acc(dve, k % 2, l * ACC_L + (A_OUT + k // 2))
                split_x(l * 2 + 1, k, gain("mlp", k))
            newton(l, 1)
            def up(g):
                dve.wait_ge(nw, l * 8 + 8)
                for k in range(KT):
                    a = l * ACC_L + g * 8 + (A_MLP + k // 2)
                    m = l * 4 * KT + g * KT + (k + 1)
                    w_unit(dve, unit(l, B_MLP, g, U_MLP, k))
                    V.tensor_tensor(ev_t[:, :], bank[k % 2][:, :], rstd[:, :], ALU.mult).then_inc(taken[k % 2], 1)
                    w_acc(dve, k % 2, a)
                    V.scalar_tensor_tensor(out=ev_r[:, :], in0=ev_t[:, :], scalar=0.0, in1=ev_t[:, :],
                                           op0=ALU.max, op1=ALU.mult).then_inc(act_a, 1)
                    dve.wait_ge(act_a, m)
                    V.tensor_copy(act_hi[:, k, :], ev_r[:, :]).then_inc(act_h, 1)
                    dve.wait_ge(act_h, l * 7 * KT + g * KT + (3 * KT + k + 1))
                    V.tensor_tensor(act_lo[:, k, :], ev_r[:, :], act_hi[:, k, :].bitcast(f32), ALU.subtract).then_inc(act_s, 1)

            with dve.Fori(0, FG - 1) as g:
                up(g)
                for k in range(KT):
                    w_unit(dve, unit(l, B_MLP, g, U_MLP, KT + k))
                    V.tensor_tensor(xT[:, k, :], xT[:, k, :], bank[k % 2][:, :], ALU.add).then_inc(taken[k % 2], 1)
            up(FG - 1)
            for k in range(KT):
                w_unit(dve, unit(l, B_MLP, FG - 1, U_MLP, KT + k))
                V.tensor_tensor(xT[:, k, :], xT[:, k, :], bank[k % 2][:, :], ALU.add).then_inc(taken[k % 2], 1)
                w_acc(dve, k % 2, l * ACC_L + (ACC_L - KT // 2 + k // 2))
                split_x(l * 2 + 2, k, gain("mix_next", k))

        for k in range(KT):
            dve.wait_ge(xt_filled, KT + k + 1)
            V.tensor_copy(out_tok[:, :, k * P:(k + 1) * P], bank[k % 2][:, :].rearrange("p (c d) -> p c d", d=P))\
                .then_inc(xt_taken, 1)

    ctx.close()


def unit_columns(w, c0, width=P):
    rows = w.shape[0]
    return w[:, c0:c0 + width].reshape(rows // P, P, width).transpose(1, 0, 2).reshape(P, rows // P * width)


def weight_stream(w_in, w_uq, w_ukv, w_branch, w_out, w_up, w_down):
    stream = np.zeros((DEPTH * UNITS, P, 1024), np.float32)
    at = 0

    def put(*blocks):
        nonlocal at
        o = 0
        for b in blocks:
            stream[at, :, o:o + b.shape[1]] = b
            o += b.shape[1]
        at += 1

    for l in range(DEPTH):
        kif = np.concatenate([w_in[l][:, C_KR:C_KR + 64], w_in[l][:, C_MI:C_MI + 32], w_in[l][:, C_MF:C_MF + 32]], axis=1)
        put(unit_columns(kif, 0))
        put(unit_columns(w_in[l], C_CKV))
        for k in range(2):
            put(unit_columns(w_in[l], C_CQ + k * P))
        for h in range(HEADS):
            qk = np.concatenate([w_in[l][:, C_MQ + h * DK:C_MQ + (h + 1) * DK], w_in[l][:, C_MK + h * DK:C_MK + (h + 1) * DK]],
                                axis=1)
            put(unit_columns(qk, 0))
            put(unit_columns(w_in[l], C_MV + h * P))
            q0 = h * (NOPE + ROPE)
            r0 = q0 + NOPE
            rows = [w_uq[l][k * P:(k + 1) * P] for k in range(2)]
            put(*[np.concatenate([r[:, q0:r0 + ROPE], r[:, r0 + ROPE // 2:r0 + ROPE], r[:, r0:r0 + ROPE // 2]], axis=1)
                  for r in rows])
            put(w_ukv[l][:, h * 2 * P:(h + 1) * 2 * P])
            put(unit_columns(w_in[l], C_MO + h * P))
            for c in (C_CB, C_CC, C_CU):
                put(unit_columns(w_in[l], c + h * P))
        for n in range(3):
            for d in range(KT):
                put(unit_columns(w_in[l], C_GATE + n * D_MODEL + d * P))
                put(unit_columns(w_branch[l, n], d * P))
        for d in range(KT):
            put(unit_columns(w_out[l], d * P))
        for g in range(FG):
            for j in range(KT):
                put(unit_columns(w_up[l], (g * KT + j) * P))
            for d in range(KT):
                put(unit_columns(w_down[l][g * D_MODEL:(g + 1) * D_MODEL], d * P))
    assert at == DEPTH * UNITS
    return stream


def tiles(v):
    return v.reshape(-1, P).T


def kernel(x, positions, mix_norm, w_in, conv_w, mlstm_igate_bias, mlstm_fgate_bias, mlstm_head_norm,
           mla_q_a_norm, mla_w_uq, mla_kv_a_norm, mla_w_ukv, mla_q_norm, mla_k_norm, w_branch, w_out,
           mlp_norm, w_up, w_down):
    import concourse.bacc as bacc
    from concourse.bass_utils import run_bass_kernel_spmd

    par = np.zeros((DEPTH, P, NPAR), np.float32)
    for l in range(DEPTH):
        def put(name, block, row=0):
            par[l, row:row + block.shape[0], PAR[name]:PAR[name] + block.shape[1]] = block

        put("mix_next", tiles(mix_norm[min(l + 1, DEPTH - 1)]))
        put("mlp", tiles(mlp_norm[l]))
        put("conv", conv_w[l].reshape(3, KT, P).transpose(2, 1, 0).reshape(P, KT * 3))
        put("head", tiles(mlstm_head_norm[l]))
        put("qa", tiles(mla_q_a_norm[l]))
        put("kva", tiles(mla_kv_a_norm[l]))
        put("q_nope", mla_q_norm[l][:NOPE, None])
        put("k_nope", mla_k_norm[l][:NOPE, None])
        put("q_rope", mla_q_norm[l][NOPE:, None])
        put("q_rope", mla_q_norm[l][NOPE + ROPE // 2:, None], 64)
        put("q_rope", mla_q_norm[l][NOPE:NOPE + ROPE // 2, None], 96)
        put("k_rope", mla_k_norm[l][NOPE:, None])
        put("b_i", mlstm_igate_bias[l][:, None])
        put("b_f", mlstm_fgate_bias[l][:, None])

    cst = np.zeros((P, NCST), np.float32)
    r = np.arange(P)
    cst[:, CST["ident"]:CST["ident"] + P] = np.eye(P)
    masks = np.zeros((P, 2, P), np.float32)
    masks[:, 0] = np.where(r[:, None] > r[None, :], BIG, 0)
    masks[:, 1] = np.where(r[None, :] > r[:, None], -BIG, 0)
    for d in range(ROPE):
        cst[(d + ROPE // 2) % ROPE, CST["swap"] + ROPE + d] = 1
    for h in range(HEADS):
        cst[h::32, CST["onehot"] + h] = 1
    freq = (10000.0 ** (-np.arange(0, ROPE, 2) / ROPE)).astype(np.float32)
    cst[:, CST["freq"]] = freq[r % (ROPE // 2)]
    cst[:, CST["sign"]] = np.where(r % ROPE < ROPE // 2, -1, 1)
    cst[:, CST["mix0"]:CST["mix0"] + KT] = tiles(mix_norm[0])

    arrays = {
        "x": np.ascontiguousarray(x[0]),
        "positions": np.ascontiguousarray(positions[0]),
        "wstream": weight_stream(w_in, mla_w_uq, mla_w_ukv, w_branch, w_out, w_up, w_down),
        "par": par,
        "cst": cst,
        "masks": masks,
    }
    nc = bacc.Bacc("TRN2", target_bir_lowering=False, num_devices=1)
    args = [nc.dram_tensor(n, a.shape, mybir.dt.from_np(a.dtype), kind="ExternalInput").ap() for n, a in arrays.items()]
    out = nc.dram_tensor("out", (SEQ, D_MODEL), mybir.dt.float32, kind="ExternalOutput").ap()
    build_trunk(nc, *args, out)
    result = run_bass_kernel_spmd(nc, [arrays], core_ids=[0])
    return result.results[0]["out"].reshape(1, SEQ, D_MODEL)
```

```python
import math
from contextlib import ExitStack

import numpy as np
import concourse.bass as bass
from concourse import mybir

D_MODEL, SEQ, DEPTH = 1024, 512, 2
P = 128
KT = D_MODEL // P
TC = SEQ // P
HEADS = 8
DK, DV = 64, 128
NOPE, ROPE = 128, 64
Q_LORA, KV_LORA = 256, 128
D_FF = 4096
FG = D_FF // D_MODEL
EPS = 1e-6
GATE_CAP = 15.0
BIG = 1e30

C_CB, C_CC, C_CU = 0, 1024, 2048
C_MQ, C_MK, C_MV, C_MO = 3072, 3584, 4096, 5120
C_MI, C_MF, C_CQ, C_CKV, C_KR, C_GATE = 6144, 6152, 6160, 6416, 6544, 6608

U_PRE, U_HEAD, U_MERGE, U_OUT, U_MLP = 4, 8, 16, 8, 16
UNITS = U_PRE + HEADS * U_HEAD + 3 * U_MERGE + U_OUT + FG * U_MLP
B_HEAD = U_PRE
B_MERGE = B_HEAD + HEADS * U_HEAD
B_OUT = B_MERGE + 3 * U_MERGE
B_MLP = B_OUT + U_OUT
STAGES, WSLOTS = 2, 4

PAR = {}
_at = 0
for _n, _w in (("mix_next", KT), ("mlp", KT), ("conv", KT * 3), ("head", KT), ("qa", 2), ("kva", 1),
               ("q_nope", 1), ("k_nope", 1), ("q_rope", 1), ("k_rope", 1), ("b_i", 1), ("b_f", 1)):
    PAR[_n] = _at
    _at += _w
NPAR = _at
CST = {}
_at = 0
for _n, _w in (("ident", P), ("swap", P), ("onehot", HEADS + 1), ("freq", 1),
               ("sign", 1), ("mix0", KT)):
    CST[_n] = _at
    _at += _w
NCST = _at

USES = {
    "q_nope": (2, 0), "score0": (2, 1), "pt0": (2, 2),
    "k_nope": (3, 0), "score1": (3, 1), "pt1": (3, 2),
    "q_rope": (4, 0), "stat_r": (4, 1), "score2": (4, 2), "pt2": (4, 3),
    "v_t": (5, 0), "stat_q": (5, 1), "score3": (5, 2), "v_tr": (5, 3), "pv": (5, 4),
    "m_bc": (6, 0), "k_tr": (6, 1), "vm_tr": (6, 2), "stat_k": (6, 3), "num1": (6, 4),
    "i_bc": (7, 0), "s_t": (7, 1), "c_loc": (7, 2), "num0": (7, 3), "h_tr": (7, 4),
}
BY_UNIT = ("q_rope", "v_t")
PRE_USE = {"stat_x": 2, "stat_kv": 3, "rot_kr": 4, "stat_kr": 5, "stat_cq": 6, "rows_tr": 7}
POST_USE = {"stat_h": 2}


def _per(bank, fills=False):
    return sum(1 for n, (b, _) in USES.items() if b == bank and not (fills and n in BY_UNIT))


def _nth(name, fills=False):
    b, k = USES[name]
    return k - (sum(1 for n in BY_UNIT if USES[n][0] == b and USES[n][1] < k) if fills else 0)


def _layer(bank, fills=False):
    return (HEADS * _per(bank, fills) + (bank in PRE_USE.values()) + (bank in POST_USE.values()))


def build_trunk(nc, x_in, pos_in, wstream, par_in, cst_in, masks_in, out):
    f32, f32r, bf16, i32 = mybir.dt.float32, mybir.dt.float32r, mybir.dt.bfloat16, mybir.dt.int32
    ALU, ACT, AX = mybir.AluOpType, mybir.ActivationFunctionType, mybir.AxisListType
    ctx = ExitStack()
    V, S, T, G = nc.vector, nc.scalar, nc.tensor, nc.gpsimd

    top = [16512]
    names = {}

    def place(name, shape, dt=f32, at=None):
        size = (2 if dt == bf16 else 4) * int(np.prod(shape[1:]))
        if at is None:
            at = top[0]
            top[0] += (size + 31) // 32 * 32
        names[name] = at
        return nc.alloc_sbuf_tensor_at(name, shape, dt, offset=at)

    xT = place("xT", [P, KT, SEQ])
    xg_hi = place("xg_hi", [P, KT, SEQ], f32r)
    xg_lo = place("xg_lo", [P, KT, SEQ], f32r)
    ysA = place("ysA", [P, KT, SEQ])
    ysB = place("ysB", [P, KT, SEQ])
    ysC = place("ysC", [P, KT, SEQ])
    merged = place("merged", [P, KT, SEQ], at=names["ysA"])
    mg_hi = place("mg_hi", [P, KT, SEQ], f32r, at=names["ysB"])
    mg_lo = place("mg_lo", [P, KT, SEQ], f32r, at=names["ysC"])
    x_tok = place("x_tok", [P, TC, D_MODEL], at=names["ysA"])
    out_tok = place("out_tok", [P, TC, D_MODEL], at=names["ysB"])
    stage = place("stage", [P, STAGES, 1024])
    whi = place("whi", [P, WSLOTS, 1024], f32r)
    wlo = place("wlo", [P, WSLOTS, 1024], f32r)

    cst = place("cst", [P, NCST])
    par = place("par", [P, NPAR])
    after_b = place("after_b", [P, SEQ], bf16)
    ones_r = place("ones_r", [P, P], f32r)
    ones = ones_r[:, :].bitcast(f32)
    ident_b = place("ident_b", [P, P], bf16)
    future_b = place("future_b", [P, P], bf16)
    cs = place("cs", [P, SEQ])
    gcs = place("gcs", [P, SEQ])
    eps = place("eps", [P, 1])
    halfpi = place("halfpi", [P, 1])
    cq_hi = place("cq_hi", [P, 2, SEQ], f32r)
    cq_lo = place("cq_lo", [P, 2, SEQ], f32r)
    ckv_hi = place("ckv_hi", [P, SEQ], f32r)
    ckv_lo = place("ckv_lo", [P, SEQ], f32r)
    kpe_h = place("kpe_h", [P, SEQ], f32r)
    kpe_l = place("kpe_l", [P, SEQ], f32r)
    rows_mi = place("rows_mi", [P, SEQ], f32r)
    acol = place("acol", [P, TC, HEADS])
    emt = place("emt", [P, TC, HEADS])
    rstd = place("rstd", [P, SEQ])
    ssum = place("ssum", [P, SEQ])
    tmp0 = top[0]
    sqx = place("sqx", [P, SEQ])
    ev_t = place("ev_t", [P, SEQ])
    ev_r = place("ev_r", [P, SEQ])
    ev_n = place("ev_n", [P, SEQ])
    gsig = [ev_t, ev_r]
    tmp_end = top[0]
    act_hi = place("act_hi", [P, KT, SEQ], f32r)
    act_lo = place("act_lo", [P, KT, SEQ], f32r)
    act0 = names["act_hi"]
    end = top[0]

    top[0] = tmp0
    prob = place("prob", [P, 1280])
    so = place("so", [P, SEQ])
    kw = place("kw", [P, TC, DK])
    assert top[0] <= tmp_end
    top[0] = act0
    nq = place("nq", [P, SEQ])
    nk = place("nk", [P, SEQ])
    nr = place("nr", [ROPE, SEQ])
    q_pe = place("q_pe", [P, SEQ], f32r)
    prob_t = place("prob_t", [P, 1280], at=names["nq"])
    qsb = place("qsb", [DK, SEQ])
    ksb = place("ksb", [DK, SEQ])
    v_ch = place("v_ch", [P, SEQ])
    vm_ch = place("vm_ch", [P, SEQ])
    htok = place("htok", [P, TC, DV], at=names["vm_ch"])
    mi = place("mi", [P, SEQ], f32r)
    tmp_n = place("tmp_n", [P, SEQ], at=names["mi"])
    qs = place("qs", [DK, SEQ])
    dec = place("dec", [P, TC, P])
    cb = place("cb", [P, SEQ])
    cc = place("cc", [P, SEQ])
    vmt = place("vmt", [P, TC, DV + 1])
    v_tok = place("v_tok", [P, TC, DV])
    sq_hi = [place("sqq_hi", [P, SEQ], f32r, at=names["cb"]), place("sqk_hi", [P, SEQ], f32r, at=names["vm_ch"])]
    sq_lo = [place("sqq_lo", [P, SEQ], f32r, at=names["cc"]), place("sqk_lo", [P, SEQ], f32r, at=names["prob"] + 2048)]
    nq_hi = place("nq_hi", [P, SEQ], f32r, at=names["prob"])
    nq_lo = place("nq_lo", [P, SEQ], f32r, at=names["v_tok"])
    nk_hi = place("nk_hi", [P, SEQ], f32r, at=names["vm_ch"])
    nk_lo = place("nk_lo", [P, SEQ], f32r, at=names["prob"] + 2048)
    yy = [place("yy_q", [P, SEQ], at=names["cb"]), place("yy_k", [P, SEQ], at=names["vm_ch"]), tmp_n]
    assert top[0] <= end, (top[0], end)
    top[0] = end
    zp = place("zp", [P, SEQ + 2])
    csb = place("csb", [DK, TC - 1, DV + 1], at=names["ssum"])
    sold = place("sold", [DK, TC], at=names["ssum"] + 1568)
    sm = place("sm", [P, 16, TC], at=names["ssum"] + 1600)
    end = top[0]
    assert end <= 229368, end
    MX, NM, SUM, RINV, SS, DEN, ADEN, DD, RR, R2, TT, LN, HR, FF = range(14)

    top[0] = act0
    cq_raw = place("cq_raw", [P, 2, SEQ])
    ckv_raw = place("ckv_raw", [P, SEQ])
    kr_raw = place("kr_raw", [ROPE, SEQ])
    sq_cq = place("sq_cq", [P, 2, SEQ])
    sq_ckv = place("sq_ckv", [P, SEQ])
    sq_kr = place("sq_kr", [ROPE, SEQ])
    r_i = place("r_i", [HEADS, SEQ])
    r_f = place("r_f", [HEADS, SEQ])
    r_nb = place("r_nb", [HEADS, SEQ])
    r_a = place("r_a", [HEADS, SEQ])
    r_d = place("r_d", [HEADS, SEQ])
    r_m = place("r_m", [HEADS, SEQ])
    r_e = place("r_e", [HEADS, SEQ])
    unit0 = place("unit0", [104, SEQ], at=names["sq_cq"])
    kpe = place("kpe", [ROPE, SEQ], at=names["sq_ckv"])
    m_prev = place("m_prev", [HEADS, TC + 1])
    masks = place("masks", [P, 2, P])
    assert top[0] <= act0 + 2 * KT * SEQ * 4
    top[0] = names["ysB"]
    pos_i = place("pos_i", [P, SEQ], i32)
    ang = place("ang", [P, SEQ])
    turns = place("turns", [P, SEQ])
    red = place("red", [P, SEQ])

    bank = [ctx.enter_context(nc.psum_tensor(f"bank{b}", [P, 512], f32)) for b in range(8)]

    def col(name, k=0, w=1):
        return cst[:, CST[name] + k:CST[name] + k + w]

    def gain(name, k=0, rows=slice(0, P)):
        return par[rows, PAR[name] + k:PAR[name] + k + 1]

    ident = cst[:, CST["ident"]:CST["ident"] + P]

    def sem(name):
        return ctx.enter_context(nc.semaphore(name))

    stage_in = [sem(f"stage_in{s}") for s in range(STAGES)]
    hi_ready = sem("hi_ready")
    w_ready = sem("w_ready")
    unit_done = sem("unit_done")
    taken = [sem(f"bank{b}_taken") for b in range(8)]
    filled = [sem(f"bank{b}_filled") for b in range(8)]
    cst_in_s, masks_in_s, pos_in_s, par_in_s = sem("cst_in"), sem("masks_in"), sem("pos_in"), sem("par_in")
    x_in_s = [sem(f"x_in{g}") for g in range(4)]
    out_s = sem("out_stored")
    consts = sem("consts_ready")
    trig = sem("trig_step")
    trig_done = sem("trig_done")
    xt_filled, xt_taken = sem("x_transposed"), sem("x_transpose_taken")
    ot = [sem("out_even_taken"), sem("out_odd_taken")]
    x_sq = sem("x_squared")
    ss_add = sem("ssum_added")
    xg_hi_s = sem("xg_hi_ready")
    xg_ready = sem("xg_ready")
    rs_step = sem("rstd_step")
    nw = sem("newton_step")
    pre_raw = sem("pre_raw")
    pre_sq = sem("pre_squared")
    pre_rs = sem("pre_rstd")
    pre_n = sem("pre_normed")
    row_v, row_s = sem("rows_vector"), sem("rows_scalar")
    head_in = sem("head_inputs")
    mi_s = sem("mi_ready")
    q_s = sem("mlstm_q_ready")
    qs_s = sem("qs_ready")
    kw_s = sem("kw_step")
    dec_s = sem("dec_step")
    sq_s = sem("mla_squared")
    rs_s = sem("mla_rstd")
    c_s = sem("c_state_step")
    qpe_s = sem("rotary_query_ready")
    nh_s = sem("query_key_rounded")
    nrm_s = sem("query_key_split")
    sql_s = sem("squares_split")
    chain = sem("head_step")
    mx_s, nm_s, rinv_s, p_s = sem("score_max"), sem("neg_max"), sem("prob_sum_inv"), sem("prob_ready")
    ss_s, fin_s, hr_s = sem("num_squared"), sem("num_step"), sem("head_rstd")
    h_s = sem("htok_step")
    so_s = sem("o_gate_ready")
    conv_s = sem("conv_step")
    act_a = sem("act_value")
    act_h = sem("act_hi_ready")
    act_s = sem("act_ready")
    g_s = sem("gate_ready")
    mg_a = sem("merge_sum")
    mg_h = sem("mg_hi_ready")
    mg_s = sem("merged_ready")

    block = ctx.enter_context(nc.Block())

    CH = 7
    N_CONSTS = 4 + 3 + TC
    N_TRIG = 14
    PRE_N, ROW_V, ROWS_AT = 16, 24, 20

    ACC_L = (U_PRE + HEADS * 6 + 3 * U_MERGE + U_OUT + FG * U_MLP) // 2
    A_HEAD = U_PRE // 2
    A_MERGE = A_HEAD + HEADS * 3
    A_OUT = A_MERGE + 3 * U_MERGE // 2
    A_MLP = A_OUT + U_OUT // 2

    def unit(l, base, i=0, per=0, j=0):
        return l * UNITS + i * per + (base + j)

    def used(l, i, name):
        b, _ = USES[name]
        return l * _layer(b) + i * _per(b) + (1 + _nth(name))

    def w_filled(e, l, i, name):
        b, _ = USES[name]
        e.wait_ge(filled[b], l * _layer(b, True) + i * _per(b, True) + (1 + _nth(name, True)) + 1)

    def w_taken(e, l, i, name):
        e.wait_ge(taken[USES[name][0]], used(l, i, name) + 2)

    def w_free(e, l, i, name):
        e.wait_ge(taken[USES[name][0]], used(l, i, name) + 1)

    def w_unit(e, u):
        e.wait_ge(unit_done, u + (1 + WSLOTS))

    def w_acc(e, b, n):
        e.wait_ge(taken[b], n + 2)

    @block.sync
    def _(sp):
        sp.dma_start(cst[:, :], cst_in).then_inc(cst_in_s, 16)
        for g in range(4):
            sp.dma_start(x_tok[:, :, g * 256:(g + 1) * 256], x_in.rearrange("(c p) d -> p c d", p=P)[:, :, g * 256:(g + 1) * 256])\
                .then_inc(x_in_s[g], 16)
        sp.dma_start(masks[:, :, :], masks_in).then_inc(masks_in_s, 16)
        with sp.Fori(0, DEPTH * UNITS // STAGES) as i:
            for s in range(STAGES):
                sp.wait_ge(w_ready, i * STAGES + (s + 1))
                sp.dma_start(stage[:, s, :], wstream[i * STAGES + s, :, :]).then_inc(stage_in[s], 16)
        for g in range(4):
            for odd in range(2):
                sp.wait_ge(ot[odd], g + 1)
            sp.dma_start(out.rearrange("(c p) d -> p c d", p=P)[:, :, g * 256:(g + 1) * 256],
                         out_tok[:, :, g * 256:(g + 1) * 256]).then_inc(out_s, 16)
        sp.wait_ge(out_s, 4 * 16)

    @block.gpsimd
    def _(pool):
        pool.sem_inc(w_ready, STAGES)
        pool.sem_inc(unit_done, WSLOTS)
        for b in range(8):
            pool.sem_inc(taken[b], 1)
        G.memset(eps[:, :], EPS).then_inc(consts, 1)
        G.memset(halfpi[:, :], math.pi / 2).then_inc(consts, 1)
        G.memset(rows_mi[:, :].bitcast(f32), 0.0).then_inc(consts, 1)
        G.memset(zp[:, 0:2], 0.0).then_inc(consts, 1)

        def lo(i, j):
            pool.wait_ge(hi_ready, i * WSLOTS + (j + 1))
            G.tensor_tensor(wlo[:, j, :], stage[:, j % STAGES, :], whi[:, j, :].bitcast(f32), ALU.subtract).then_inc(w_ready, 1)

        pool.wait_ge(cst_in_s, 16)
        pool.wait_ge(pos_in_s, 16)
        step = 0

        def link(ins):
            nonlocal step
            step += 1
            ins.then_inc(trig, 1)
            pool.wait_ge(trig, step)

        link(G.tensor_copy(ang[:, :], pos_i[:, :]))
        link(G.tensor_scalar(ang[:, :], ang[:, :], col("freq"), None, ALU.mult))
        link(G.tensor_scalar(turns[:, :], ang[:, :], 1.0 / (2 * math.pi), None, ALU.mult))
        lo(0, 0)
        link(G.tensor_scalar(turns[:, :], turns[:, :], 12582912.0, None, ALU.add))
        lo(0, 1)
        link(G.tensor_scalar(turns[:, :], turns[:, :], 12582912.0, None, ALU.subtract))
        lo(0, 2)
        lo(0, 3)
        left, parts = 2 * math.pi, []
        for bits in (5, 13, 21):
            parts.append(math.floor(left * 2 ** bits) / 2 ** bits)
            left -= parts[-1]
        for part in (*parts, left):
            link(G.tensor_scalar(red[:, :], turns[:, :], -part, None, ALU.mult))
            link(G.tensor_tensor(ang[:, :], ang[:, :], red[:, :], ALU.add))
        link(G.tensor_scalar(red[:, :], ang[:, :], 3.1415925, -3.1415925, ALU.min, ALU.max))
        assert step == N_TRIG

        with pool.Fori(1, DEPTH * UNITS // WSLOTS) as i:
            for j in range(WSLOTS):
                lo(i, j)

    @block.tensor
    def _(pe):
        def split_mm(acc, w, hi, lo, first, last):
            T.matmul(acc, w[0], hi, start=first, stop=False)
            T.matmul(acc, w[0], lo, start=False, stop=False)
            return T.matmul(acc, w[1], hi, start=False, stop=last)

        def project(u, slot, b, n, hi, lo, tile_ready=None):
            pe.wait_ge(w_ready, u + (1 + STAGES))
            pe.wait_ge(taken[b], n + 1)
            for k in range(KT):
                if tile_ready is not None:
                    pe.wait_ge(tile_ready[0], tile_ready[1] + (k + 1))
                w = (whi[:, slot, k * P:(k + 1) * P], wlo[:, slot, k * P:(k + 1) * P])
                last = split_mm(bank[b][:, :], w, hi[:, k, :], lo[:, k, :], k == 0, k == KT - 1)
            last.then_inc(unit_done, 1)

        pe.wait_ge(cst_in_s, 16)
        for k in range(KT):
            pe.wait_ge(x_in_s[k // 2], 16)
            if k >= 6:
                pe.wait_ge(xt_taken, k - 5)
            for c in range(TC):
                last = T.transpose(bank[2 + k % 6][:, c * P:(c + 1) * P], x_tok[:, c, k * P:(k + 1) * P], ident)
            last.then_inc(xt_filled, 1)

        with pe.Fori(0, DEPTH) as l:
            for j in range(U_PRE):
                project(unit(l, 0, j=j), j % WSLOTS, j % 2, l * ACC_L + j // 2, xg_hi, xg_lo,
                        (xg_ready, l * 2 * KT) if j == 0 else None)
                if j == 0:
                    pe.wait_ge(ss_add, l * 2 * (KT - 1) + (KT - 1))
                    pe.wait_ge(consts, N_CONSTS)
                    pe.wait_ge(taken[2], l * _layer(2) + 1)
                    T.matmul(bank[2][:, :], ones[:, :], ssum[:, :], start=True, stop=True).then_inc(filled[2], 1)
            pe.wait_ge(pre_sq, l * 4 + 1)
            pe.wait_ge(taken[5], l * _layer(5) + 1)
            T.matmul(bank[5][:, :], ones[0:ROPE, :], sq_kr[:, :], start=True, stop=True).then_inc(filled[5], 1)
            pe.wait_ge(pre_sq, l * 4 + 2)
            pe.wait_ge(taken[3], l * _layer(3) + 1)
            T.matmul(bank[3][:, :], ones[:, :], sq_ckv[:, :], start=True, stop=True).then_inc(filled[3], 1)
            pe.wait_ge(pre_sq, l * 4 + 3)
            pe.wait_ge(taken[6], l * _layer(6) + 1)
            T.matmul(bank[6][:, :], ones[:, :], sq_cq[:, 0, :], start=True, stop=False)
            pe.wait_ge(pre_sq, l * 4 + 4)
            T.matmul(bank[6][:, :], ones[:, :], sq_cq[:, 1, :], start=False, stop=True).then_inc(filled[6], 1)
            pe.wait_ge(row_v, l * ROW_V + ROWS_AT)
            pe.wait_ge(taken[7], l * _layer(7) + 1)
            pe.wait_ge(pre_n, l * PRE_N + 1)
            pe.wait_ge(taken[4], l * _layer(4) + 1)
            T.matmul(bank[4][:, :], col("swap", 0, P)[0:ROPE, :], kr_raw[:, :], start=True, stop=True).then_inc(filled[4], 1)
            for c in range(TC):
                T.transpose(bank[7][:, c * 8:c * 8 + 8], r_a[:, c * P:(c + 1) * P], ident[0:8, 0:8])
            for c in range(TC):
                last = T.transpose(bank[7][:, 32 + c * 8:40 + c * 8], r_d[:, c * P:(c + 1) * P], ident[0:8, 0:8])
            last.then_inc(filled[7], 1)

            with pe.Fori(0, HEADS) as i:
                def free(name):
                    w_free(pe, l, i, name)

                def fill(name, ins):
                    ins.then_inc(filled[USES[name][0]], 1)

                def head_unit(j, slot, b, n):
                    project(unit(l, B_HEAD, i, U_HEAD, j), slot, b, l * ACC_L + i * 3 + (A_HEAD + n), xg_hi, xg_lo)

                head_unit(0, 0, 0, 0)
                pe.wait_ge(mi_s, l * (HEADS + 1) + i + 1)
                free("m_bc")
                T.matmul(bank[6][:, :], ones_r[0:64, :], mi[0:64, :], start=True, stop=False)
                fill("m_bc", T.matmul(bank[6][:, :], ident_b[:, :], after_b[:, :], start=False, stop=True))
                free("i_bc")
                fill("i_bc", T.matmul(bank[7][:, :], ones_r[64:P, :], mi[64:P, :], start=True, stop=True))
                head_unit(1, 1, 1, 0)
                w_acc(pe, 0, l * ACC_L + i * 3 + A_HEAD)
                free("k_tr")
                free("s_t")
                for c in range(TC):
                    last = T.matmul(bank[7][:, c * P:(c + 1) * P], ksb[:, c * P:(c + 1) * P], qsb[:, c * P:(c + 1) * P],
                                    start=True, stop=True)
                fill("s_t", last)
                for c in range(TC):
                    last = T.transpose(bank[6][:, c * DK:(c + 1) * DK], ksb[:, c * P:(c + 1) * P], ident[0:DK, 0:DK])
                fill("k_tr", last)
                pe.wait_ge(w_ready, unit(l, B_HEAD, i, U_HEAD, 2) + (1 + STAGES))
                pe.wait_ge(pre_n, l * PRE_N + PRE_N)
                free("q_nope")
                for name, b, off in (("q_nope", 2, 0), ("q_rope", 4, P)):
                    if b == 4:
                        free("q_rope")
                    for k in range(2):
                        o = k * 2 * P + off
                        last = split_mm(bank[b][:, :], (whi[:, 2, o:o + P], wlo[:, 2, o:o + P]),
                                        cq_hi[:, k, :], cq_lo[:, k, :], k == 0, k == 1)
                    if b == 2:
                        fill("q_nope", last)
                last.then_inc(unit_done, 1)
                pe.wait_ge(w_ready, unit(l, B_HEAD, i, U_HEAD, 3) + (1 + STAGES))
                free("k_nope")
                fill("k_nope", split_mm(bank[3][:, :], (whi[:, 3, 0:P], wlo[:, 3, 0:P]), ckv_hi[:, :], ckv_lo[:, :], True, True))
                free("v_t")
                split_mm(bank[5][:, :], (whi[:, 3, P:2 * P], wlo[:, 3, P:2 * P]), ckv_hi[:, :], ckv_lo[:, :], True, True)\
                    .then_inc(unit_done, 1)
                w_acc(pe, 1, l * ACC_L + i * 3 + A_HEAD)
                free("vm_tr")
                for c in range(TC):
                    last = T.transpose(bank[6][:, c * P:(c + 1) * P], vm_ch[:, c * P:(c + 1) * P], ident)
                fill("vm_tr", last)
                head_unit(4, 0, 0, 1)
                w_taken(pe, l, i, "k_tr")
                w_taken(pe, l, i, "vm_tr")
                free("c_loc")
                for c in range(TC - 1):
                    last = T.matmul(bank[7][0:DK, c * 129:(c + 1) * 129], kw[:, c, :], vmt[:, c, :], start=True, stop=True)
                fill("c_loc", last)
                for n, name in enumerate(("stat_q", "stat_k", "stat_r")):
                    pe.wait_ge(sql_s, (l * HEADS + i) * 3 + (n + 1))
                    free(name)
                    b = bank[USES[name][0]]
                    if n < 2:
                        T.matmul(b[:, :], ones_r[:, :], sq_hi[n][:, :], start=True, stop=False)
                        fill(name, T.matmul(b[:, :], ones_r[:, :], sq_lo[n][:, :], start=False, stop=True))
                    else:
                        fill(name, T.matmul(b[:, :], ones_r[:, :], q_pe[:, :], start=True, stop=True))
                head_unit(5, 1, 1, 1)
                w_taken(pe, l, i, "s_t")
                pe.wait_ge(qs_s, l * HEADS + i + 1)
                for half, name in ((0, "num0"), (1, "num1")):
                    free(name)
                    for c in (2 * half, 2 * half + 1):
                        o = bank[7 - half][:, (c % 2) * 129:(c % 2) * 129 + 129]
                        last = T.matmul(o, dec[:, c, :], vmt[:, c, :], start=True, stop=(c == 0))
                        if c:
                            last = T.matmul(o, qs[:, c * P:(c + 1) * P], csb[:, c - 1, :], start=False, stop=True)
                    fill(name, last)
                head_unit(6, 2, 0, 2)
                pe.wait_ge(nrm_s, (l * HEADS + i) * 2 + 2)
                pe.wait_ge(qpe_s, l * HEADS + i + 1)
                for qb in range(TC):
                    b, w = bank[2 + qb], max(256, (qb + 1) * P)
                    q = slice(qb * P, (qb + 1) * P)
                    free(f"score{qb}")
                    split_mm(b[:, 0:w], (nq_hi[:, q], nq_lo[:, q]), nk_hi[:, 0:w], nk_lo[:, 0:w], True, False)
                    T.matmul(b[:, 0:w], q_pe[:, q], kpe_h[:, 0:w], start=False, stop=False)
                    T.matmul(b[:, 0:w], q_pe[:, q], kpe_l[:, 0:w], start=False, stop=False)
                    fill(f"score{qb}", T.matmul(b[:, q], ident_b[:, :], future_b[:, :], start=False, stop=True))
                head_unit(7, 3, 1, 2)
                free("v_tr")
                for c in range(TC):
                    last = T.transpose(bank[5][:, c * P:(c + 1) * P], v_ch[:, c * P:(c + 1) * P], ident)
                fill("v_tr", last)
                pe.wait_ge(p_s, (l * HEADS + i) * TC + TC)
                for kb, (b, o) in enumerate(((2, 0), (3, 0), (4, 0), (4, 2 * P))):
                    if kb < 3:
                        free(f"pt{kb}")
                    for qb in range(kb, TC):
                        src = (qb * (qb + 1) // 2 + kb) * P
                        last = T.transpose(bank[b][:, o + (qb - kb) * P:o + (qb - kb + 1) * P], prob[:, src:src + P], ident)
                    if kb != 2:
                        fill(f"pt{min(kb, 2)}", last)
                w_taken(pe, l, i, "num1")
                free("h_tr")
                for c in range(TC):
                    last = T.transpose(bank[7][:, c * P:(c + 1) * P], htok[:, c, :], ident)
                fill("h_tr", last)
                w_taken(pe, l, i, "v_tr")
                free("pv")
                at = 0
                for kb in range(TC):
                    if kb < 3:
                        w_taken(pe, l, i, f"pt{kb}")
                    w = (TC - kb) * P
                    last = T.matmul(bank[5][:, kb * P:SEQ], v_tok[:, kb, :], prob_t[:, at:at + w],
                                    start=(kb == 0), stop=(kb == TC - 1))
                    at += w
                fill("pv", last)

            for n in range(3):
                with pe.Fori(0, 4) as i:
                    for j in range(4):
                        u = unit(l, B_MERGE + n * U_MERGE, i, 4, j)
                        a = l * ACC_L + i * 2 + (A_MERGE + n * 8 + j // 2)
                        if j % 2 == 0:
                            project(u, j, 0, a, xg_hi, xg_lo)
                        else:
                            project(u, j, 1, a, act_hi, act_lo, (act_s, (l * 7 + n) * KT) if j == 1 else None)
            with pe.Fori(0, 2) as i:
                for j in range(4):
                    project(unit(l, B_OUT, i, 4, j), j, j % 2, l * ACC_L + i * 2 + (A_OUT + j // 2), mg_hi, mg_lo,
                            (mg_s, l * KT) if j == 0 else None)
            def mlp_quad(g, i, down, stat=False):
                for j in range(4):
                    base = B_MLP + (8 if down else 0)
                    hi, lo = (act_hi, act_lo) if down else (xg_hi, xg_lo)
                    ready = (act_s, l * 7 * KT + g * KT + 3 * KT) if down else (xg_ready, l * 2 * KT + KT)
                    project(unit(l, base, g, U_MLP, j) + i * 4, j, j % 2,
                            l * ACC_L + g * 8 + i * 2 + (A_MLP + (4 if down else 0) + j // 2), hi, lo,
                            ready if j == 0 else None)
                    if stat and j == 0:
                        pe.wait_ge(ss_add, l * 2 * (KT - 1) + 2 * (KT - 1))
                        pe.wait_ge(taken[2], l * _layer(2) + _layer(2))
                        T.matmul(bank[2][:, :], ones[:, :], ssum[:, :], start=True, stop=True).then_inc(filled[2], 1)

            mlp_quad(0, 0, False, stat=True)
            mlp_quad(0, 1, False)
            with pe.Fori(0, 2) as i:
                mlp_quad(0, i, True)
            with pe.Fori(1, FG) as g:
                with pe.Fori(0, 2) as i:
                    mlp_quad(g, i, False)
                with pe.Fori(0, 2) as i:
                    mlp_quad(g, i, True)

        for k in range(KT):
            pe.wait_ge(taken[k % 2], DEPTH * ACC_L + 1 - (KT - 1 - k) // 2)
            if k >= 6:
                pe.wait_ge(ot[k % 2], (k - 6) // 2 + 1)
            for c in range(TC):
                last = T.transpose(bank[2 + k % 6][:, c * P:(c + 1) * P], xT[:, k, c * P:(c + 1) * P], ident)
            last.then_inc(xt_filled, 1)

    @block.scalar
    def _(act):
        def hi(l, base, i, per, j):
            slot = (base + j) % WSLOTS
            act.wait_ge(stage_in[slot % STAGES], (l * (UNITS // 2) + i * (per // 2) + (base + j) // 2) * 16 + 16)
            act.wait_ge(unit_done, unit(l, base, i, per, j) + 1)
            S.activation(whi[:, slot, :], stage[:, slot % STAGES, :], ACT.Copy).then_inc(hi_ready, 1)

        def main_rstd(l, norm):
            act.wait_ge(filled[2], l * _layer(2, True) + (_layer(2, True) if norm else 1))
            S.activation(rstd[:, :], bank[2][:, :], ACT.Ln, scale=1.0 / D_MODEL, bias=eps[:, :]).then_inc(rs_step, 1)
            act.wait_ge(rs_step, l * 4 + (norm * 2 + 1))
            S.activation(rstd[:, :], rstd[:, :], ACT.Exp, scale=-0.5).then_inc(rs_step, 1)

        def squares(norm, k):
            if k >= 2:
                act.wait_ge(ss_add, norm * (KT - 1) + (k - 1))
            S.activation(ssum[:, :] if k == 0 else sqx[:, :], xT[:, k, :], ACT.Square).then_inc(x_sq, 1)

        act.dma_start(pos_i[:, :], pos_in.partition_broadcast(P)).then_inc(pos_in_s, 16)
        S.preload_act_table_set("natural_log_exp_and_others")
        for k in range(KT):
            act.wait_ge(xt_filled, k + 1)
            S.activation(xT[:, k, :], bank[2 + k % 6][:, :], ACT.Copy).then_inc(xt_taken, 1)
            act.wait_ge(xt_taken, k + 1)
            squares(0, k)
            for j in {2: (0,), 5: (1,), 7: (2, 3)}.get(k, ()):
                hi(0, 0, 0, 0, j)
        act.wait_ge(consts, N_CONSTS)

        with act.Fori(0, DEPTH) as l:
            S.preload_act_table_set("natural_log_exp_and_others")
            act.wait_ge(xg_ready, l * 2 * KT + KT)
            act.dma_start(par[:, :], par_in[l, :, :]).then_inc(par_in_s, 16)
            main_rstd(l, 0)
            hi(l, 0, 0, 0, 4)
            act.wait_ge(pre_raw, l * 3 + 1)
            S.activation(sq_kr[:, :], kr_raw[:, :], ACT.Square).then_inc(pre_sq, 1)
            act.wait_ge(row_v, l * ROW_V + 2)
            S.activation(r_i[:, :], r_i[:, :], ACT.Tanh).then_inc(row_s, 1)
            S.activation(r_f[:, :], r_f[:, :], ACT.Tanh).then_inc(row_s, 1)
            S.preload_act_table_set("natural_log_exp_and_others")
            act.wait_ge(row_s, l * 8 + 2)
            S.activation(r_f[:, :], r_f[:, :], ACT.Exp, scale=-GATE_CAP).then_inc(row_s, 1)
            act.wait_ge(row_s, l * 8 + 3)
            S.activation(r_f[:, :], r_f[:, :], ACT.Ln, bias=ones[0:HEADS, 0:1]).then_inc(row_s, 1)
            hi(l, 0, 0, 0, 5)
            w_acc(act, 1, l * ACC_L)
            S.activation(sq_ckv[:, :], ckv_raw[:, :], ACT.Square).then_inc(pre_sq, 1)
            w_acc(act, 0, l * ACC_L + 1)
            S.activation(sq_cq[:, 0, :], cq_raw[:, 0, :], ACT.Square).then_inc(pre_sq, 1)
            for c in range(TC):
                act.wait_ge(row_v, l * ROW_V + (9 + 3 * c))
                S.activation(r_e[:, c * P:(c + 1) * P], r_m[:, c * P:(c + 1) * P], ACT.Exp,
                             scale=-1.0, bias=m_prev[:, c:c + 1]).then_inc(row_s, 1)
                if c == 2:
                    w_acc(act, 1, l * ACC_L + 1)
                    S.activation(sq_cq[:, 1, :], cq_raw[:, 1, :], ACT.Square).then_inc(pre_sq, 1)
            for n, (b, dst, width, rows) in enumerate(((5, sq_kr[:, :], ROPE, ROPE), (3, sq_ckv[:, :], KV_LORA, P),
                                                       (6, sq_cq[:, 0, :], Q_LORA, P))):
                act.wait_ge(filled[b], l * _layer(b, True) + 1)
                S.activation(dst, bank[b][0:rows, :], ACT.Ln, scale=1.0 / width, bias=eps[0:rows, :]).then_inc(taken[b], 1)
                act.wait_ge(taken[b], l * _layer(b) + 2)
                S.activation(dst, dst, ACT.Exp, scale=-0.5).then_inc(pre_rs, 1)
            with act.If(l < 1):
                act.wait_ge(trig, N_TRIG)
                S.activation(ang[0:64, :], red[0:64, :], ACT.Abs).then_inc(trig_done, 1)
                act.wait_ge(trig_done, 1)
                S.activation(cs[0:64, :], ang[0:64, :], ACT.Sin, scale=-1.0, bias=halfpi[0:64, :]).then_inc(trig_done, 1)
                S.activation(cs[64:P, :], red[64:P, :], ACT.Sin, scale=col("sign")[64:P, :]).then_inc(trig_done, 1)
                S.preload_act_table_set("natural_log_exp_and_others")
            act.wait_ge(filled[7], l * _layer(7, True) + 1)
            S.activation(acol[:, :, :], bank[7][:, 0:32].rearrange("p (c h) -> p c h", h=8), ACT.Copy).then_inc(head_in, 1)
            S.activation(emt[:, :, :], bank[7][:, 32:64].rearrange("p (c h) -> p c h", h=8), ACT.Exp).then_inc(taken[7], 1)

            with act.Fori(0, HEADS) as i:
                def head_hi(j):
                    hi(l, B_HEAD, i, U_HEAD, j)

                it = l * HEADS + i
                head_hi(2)
                act.wait_ge(head_in, l + 1)
                w_filled(act, l, i, "m_bc")
                for c in range(TC):
                    ins = S.activation(dec[:, c, :], bank[6][:, c * P:(c + 1) * P], ACT.Exp, scale=-1.0,
                                       bias=acol[:, c, bass.ds(i, 1)])
                    ins.then_inc(taken[6] if c == TC - 1 else dec_s, 1)
                head_hi(3)
                head_hi(4)
                head_hi(5)
                w_filled(act, l, i, "q_nope")
                S.activation(sq_hi[0][:, :], bank[2][:, :], ACT.Square).then_inc(sq_s, 1)
                S.activation(nq[:, :], bank[2][:, :], ACT.Square).then_inc(sq_s, 1)
                head_hi(6)
                w_filled(act, l, i, "k_nope")
                w_filled(act, l, i, "vm_tr")
                S.activation(sq_hi[1][:, :], bank[3][:, :], ACT.Square).then_inc(sq_s, 1)
                S.activation(nk[:, :], bank[3][:, :], ACT.Square).then_inc(sq_s, 1)
                w_unit(act, unit(l, B_HEAD, i, U_HEAD, 2))
                S.activation(q_pe[0:ROPE, :], bank[4][0:ROPE, :], ACT.Square).then_inc(sq_s, 1)
                S.activation(nr[:, :], bank[4][0:ROPE, :], ACT.Square).then_inc(sq_s, 1)
                head_hi(7)
                for n, (name, dst, rows) in enumerate((("stat_q", nq, P), ("stat_k", nk, P), ("stat_r", nr, ROPE))):
                    w_filled(act, l, i, name)
                    b = USES[name][0]
                    S.activation(dst[:, :], bank[b][0:rows, :], ACT.Ln, scale=1.0 / rows).then_inc(rs_s, 1)
                    act.wait_ge(rs_s, it * 9 + (3 * n + 1))
                    S.activation(dst[:, :], dst[:, :], ACT.Exp, scale=-0.5).then_inc(rs_s, 1)
                    act.wait_ge(rs_s, it * 9 + (3 * n + 2))
                    S.activation(yy[n][0:rows, :], dst[:, :], ACT.Square).then_inc(rs_s, 1)
                for name, y, hi_ in (("q_nope", nq, nq_hi), ("k_nope", nk, nk_hi)):
                    w_taken(act, l, i, name)
                    S.activation(hi_[:, :], y[:, :], ACT.Copy).then_inc(nh_s, 1)
                w_acc(act, 0, l * ACC_L + i * 3 + (A_HEAD + 1))
                S.activation(so[:, :], so[:, :], ACT.Sigmoid).then_inc(so_s, 1)
                S.preload_act_table_set("natural_log_exp_and_others")
                head_hi(8)
                for c in range(TC):
                    if c % 2 == 0:
                        act.wait_ge(fin_s, it * 8 + c // 2 + 1)
                    S.activation(tmp_n[:, c * DV:(c + 1) * DV], bank[7 - c // 2][:, (c % 2) * 129:(c % 2) * 129 + DV], ACT.Square,
                                 accum_out=sm[:, SS, c:c + 1]).then_inc(ss_s, 1)
                head_hi(9)
                act.wait_ge(nm_s, it + 1)
                for qb in range(TC):
                    o = qb * (qb + 1) // 2 * P
                    S.activation(prob[:, o:o + (qb + 1) * P], bank[2 + qb][:, 0:(qb + 1) * P], ACT.Exp,
                                 scale=(NOPE + ROPE) ** -0.5, bias=sm[:, NM, qb:qb + 1],
                                 accum_out=sm[:, SUM, qb:qb + 1]).then_inc(taken[2 + qb], 1)
                act.wait_ge(fin_s, it * 8 + 7)
                S.activation(sm[:, LN, :], sm[:, TT, :], ACT.Ln, scale=1.0 / DV, bias=eps[:, :]).then_inc(hr_s, 1)
                act.wait_ge(hr_s, it * 2 + 1)
                S.activation(sm[:, HR, :], sm[:, LN, :], ACT.Exp, scale=-0.5).then_inc(hr_s, 1)
                w_filled(act, l, i, "v_tr")
                S.activation(v_tok[:, :, :], bank[5][:, :].rearrange("p (c d) -> p c d", d=DV), ACT.Copy)\
                    .then_inc(taken[5], 1)
                w_filled(act, l, i, "pt0")
                S.activation(prob_t[:, 0:512], bank[2][:, :], ACT.Copy).then_inc(taken[2], 1)
                w_filled(act, l, i, "pt1")
                S.activation(prob_t[:, 512:896], bank[3][:, 0:384], ACT.Copy).then_inc(taken[3], 1)
                w_filled(act, l, i, "pv")
                S.activation(ysC[:, i, :], bank[5][:, :], ACT.Copy).then_inc(taken[5], 1)

            S.preload_act_table_set("sigmoid_and_others")
            for n, ys in enumerate((ysA, ysB, ysC)):
                if n == 0:
                    act.wait_ge(conv_s, (l + 1) * HEADS * 5 - 5)
                    act.wait_ge(taken[5], (l + 1) * _layer(5) + 1)
                else:
                    w_unit(act, unit(l, B_MERGE + n * U_MERGE - 1))
                for k in range(KT):
                    if n == 0 and k == KT - 1:
                        act.wait_ge(conv_s, (l + 1) * HEADS * 5)
                    S.activation(act_hi[:, k, :], ys[:, k, :], ACT.Copy).then_inc(act_h, 1)
                with act.Fori(0, 4) as i:
                    for j in range(4):
                        hi(l, B_MERGE + n * U_MERGE, i, 4, j + 2)
                        if j % 2 == 0:
                            w_acc(act, 0, l * ACC_L + i * 2 + (A_MERGE + n * 8 + j // 2))
                            g = gsig[j // 2]
                            S.activation(g[:, :], g[:, :], ACT.Sigmoid).then_inc(g_s, 1)
            S.preload_act_table_set("natural_log_exp_and_others")
            for k in range(KT):
                hi(l, B_OUT, 0, 0, k + 2)
                w_acc(act, k % 2, l * ACC_L + (A_OUT + k // 2))
                squares(l * 2 + 1, k)
            main_rstd(l, 1)
            with act.Fori(0, FG * U_MLP // 4 - 2) as i:
                for j in range(4):
                    hi(l, B_MLP, i, 4, j + 2)
            for k in range(KT):
                if k < KT - 2:
                    hi(l, B_MLP + FG * U_MLP - KT, 0, 0, k + 2)
                else:
                    with act.If(l < DEPTH - 1):
                        hi(l, UNITS - KT, 0, 0, k + 2)
                with act.If(l < DEPTH - 1):
                    w_acc(act, k % 2, l * ACC_L + (ACC_L - KT // 2 + k // 2))
                    squares(l * 2 + 2, k)
            with act.If(l < DEPTH - 1):
                for k in range(2):
                    hi(l, UNITS, 0, 0, k + 2)

        for k in range(1, KT, 2):
            act.wait_ge(xt_filled, KT + k + 1)
            S.activation(out_tok[:, :, k * P:(k + 1) * P], bank[2 + k % 6][:, :].rearrange("p (c d) -> p c d", d=P), ACT.Copy)\
                .then_inc(ot[1], 1)

    @block.vector
    def _(dve):
        def split_x(norm, k, g):
            V.tensor_scalar(xg_hi[:, k, :], xT[:, k, :], g, None, ALU.mult).then_inc(xg_hi_s, 1)
            dve.wait_ge(xg_hi_s, norm * KT + (k + 1))
            V.scalar_tensor_tensor(out=xg_lo[:, k, :], in0=xT[:, k, :], scalar=g, in1=xg_hi[:, k, :].bitcast(f32),
                                   op0=ALU.mult, op1=ALU.subtract).then_inc(xg_ready, 1)
            if k:
                dve.wait_ge(x_sq, norm * KT + (k + 1))
                if k > 1:
                    dve.wait_ge(ss_add, norm * (KT - 1) + (k - 1))
                V.tensor_tensor(ssum[:, :], ssum[:, :], sqx[:, :], ALU.add).then_inc(ss_add, 1)

        def newton(l, norm):
            base = norm * 4
            dve.wait_ge(filled[2], l * _layer(2, True) + (_layer(2, True) if norm else 1))
            dve.wait_ge(rs_step, l * 4 + (norm * 2 + 1))
            V.tensor_scalar(ev_n[:, :], bank[2][:, :], 1.0 / D_MODEL, EPS, ALU.mult, ALU.add).then_inc(taken[2], 1)
            dve.wait_ge(rs_step, l * 4 + (norm * 2 + 2))
            V.tensor_tensor(ev_t[:, :], rstd[:, :], rstd[:, :], ALU.mult).then_inc(nw, 1)
            dve.wait_ge(nw, l * 8 + (base + 1))
            dve.wait_ge(taken[2], l * _layer(2) + ((_layer(2) if norm else 1) + 1))
            V.tensor_tensor(ev_t[:, :], ev_t[:, :], ev_n[:, :], ALU.mult).then_inc(nw, 1)
            dve.wait_ge(nw, l * 8 + (base + 2))
            V.tensor_scalar(ev_t[:, :], ev_t[:, :], -0.5, 1.5, ALU.mult, ALU.add).then_inc(nw, 1)
            dve.wait_ge(nw, l * 8 + (base + 3))
            V.tensor_tensor(rstd[:, :], rstd[:, :], ev_t[:, :], ALU.mult).then_inc(nw, 1)

        V.memset(ones[:, :], 1.0).then_inc(consts, 1)
        dve.wait_ge(cst_in_s, 16)
        V.tensor_copy(ident_b[:, :], ident).then_inc(consts, 1)
        for k in range(KT):
            dve.wait_ge(xt_taken, k + 1)
            split_x(0, k, col("mix0", k))
        dve.wait_ge(masks_in_s, 16)
        V.tensor_copy(future_b[:, :], masks[:, 1, :]).then_inc(consts, 1)
        for c in range(TC):
            V.tensor_copy(after_b[:, c * P:(c + 1) * P], masks[:, 0, :]).then_inc(consts, 1)
        dve.wait_ge(consts, N_CONSTS)

        def head_rows(h):
            V.tensor_scalar(mi[:, :], rows_mi[:, :].bitcast(f32), cst[:, bass.ds(h + CST["onehot"], 1)], None, ALU.mult)\
                .then_inc(mi_s, 1)

        with dve.Fori(0, DEPTH) as l:
            w_unit(dve, unit(l, 0))
            V.tensor_copy(unit0[:, :], bank[0][0:104, :]).then_inc(taken[0], 1)
            w_acc(dve, 0, l * ACC_L)
            newton(l, 0)
            dve.wait_ge(nw, l * 8 + 4)
            V.tensor_tensor(kr_raw[:, :], unit0[0:64, :], rstd[0:64, :], ALU.mult).then_inc(pre_raw, 1)
            V.tensor_tensor(r_i[:, :], unit0[64:72, :], rstd[64:72, :], ALU.mult).then_inc(pre_raw, 1)
            V.tensor_tensor(r_f[:, :], unit0[96:104, :], rstd[96:104, :], ALU.mult).then_inc(pre_raw, 1)
            w_unit(dve, unit(l, 0, j=1))
            V.tensor_tensor(ckv_raw[:, :], bank[1][:, :], rstd[:, :], ALU.mult).then_inc(taken[1], 1)
            dve.wait_ge(par_in_s, l * 16 + 16)
            dve.wait_ge(pre_raw, l * 3 + 3)
            V.tensor_scalar(r_i[:, :], r_i[:, :], gain("b_i", 0, slice(0, 8)), 1.0 / GATE_CAP, ALU.add, ALU.mult).then_inc(row_v, 1)
            V.tensor_scalar(r_f[:, :], r_f[:, :], gain("b_f", 0, slice(0, 8)), 1.0 / GATE_CAP, ALU.add, ALU.mult).then_inc(row_v, 1)
            dve.wait_ge(row_s, l * 8 + 4)
            for c in range(TC):
                V.tensor_tensor_scan(r_nb[:, c * P:(c + 1) * P], ones[0:HEADS, :], r_f[:, c * P:(c + 1) * P], 0.0,
                                     ALU.mult, ALU.add).then_inc(row_v, 1)
            dve.wait_ge(row_v, l * ROW_V + 6)
            V.scalar_tensor_tensor(out=r_a[:, :], in0=r_i[:, :], scalar=GATE_CAP, in1=r_nb[:, :], op0=ALU.mult,
                                   op1=ALU.add).then_inc(row_v, 1)
            V.memset(m_prev[:, 0:1], 0.0).then_inc(row_v, 1)
            w_unit(dve, unit(l, 0, j=2))
            V.tensor_tensor(cq_raw[:, 0, :], bank[0][:, :], rstd[:, :], ALU.mult).then_inc(taken[0], 1)
            dve.wait_ge(row_v, l * ROW_V + 8)
            for c in range(TC):
                s = slice(c * P, (c + 1) * P)
                V.tensor_tensor_scan(r_m[:, s], r_a[:, s], r_a[:, s], m_prev[:, c:c + 1], ALU.max, ALU.max)\
                    .then_inc(row_v, 1)
                dve.wait_ge(row_v, l * ROW_V + (9 + 3 * c))
                V.tensor_tensor(m_prev[:, c + 1:c + 2], r_m[:, (c + 1) * P - 1:(c + 1) * P],
                                r_nb[:, (c + 1) * P - 1:(c + 1) * P], ALU.subtract).then_inc(row_v, 1)
                V.tensor_tensor(r_d[:, s], r_nb[:, s], r_m[:, s], ALU.subtract).then_inc(row_v, 1)
                if c == 2:
                    w_unit(dve, unit(l, 0, j=3))
                    V.tensor_tensor(cq_raw[:, 1, :], bank[1][:, :], rstd[:, :], ALU.mult).then_inc(taken[1], 1)
                dve.wait_ge(row_v, l * ROW_V + (11 + 3 * c))
            V.tensor_copy(rows_mi[0:8, :], r_m[:, :]).then_inc(row_v, 1)
            dve.wait_ge(row_v, l * ROW_V + 21)
            V.tensor_tensor(rows_mi[32:40, :], r_m[:, :], rows_mi[0:8, :].bitcast(f32), ALU.subtract).then_inc(row_v, 1)
            dve.wait_ge(pre_rs, l * 3 + 1)
            V.scalar_tensor_tensor(out=kr_raw[:, :], in0=kr_raw[:, :], scalar=gain("k_rope", 0, slice(0, 64)), in1=sq_kr[:, :],
                                   op0=ALU.mult, op1=ALU.mult).then_inc(pre_n, 1)
            dve.wait_ge(row_s, l * 8 + 8)
            V.tensor_copy(rows_mi[64:72, :], r_e[:, :]).then_inc(row_v, 1)
            dve.wait_ge(row_v, l * ROW_V + 23)
            V.tensor_tensor(rows_mi[96:104, :], r_e[:, :], rows_mi[64:72, :].bitcast(f32), ALU.subtract).then_inc(row_v, 1)
            dve.wait_ge(row_v, l * ROW_V + ROW_V)
            head_rows(0)
            dve.wait_ge(pre_rs, l * 3 + 3)
            V.scalar_tensor_tensor(out=ckv_raw[:, :], in0=ckv_raw[:, :], scalar=gain("kva"), in1=sq_ckv[:, :],
                                   op0=ALU.mult, op1=ALU.mult).then_inc(pre_n, 1)
            for k in range(2):
                V.scalar_tensor_tensor(out=cq_raw[:, k, :], in0=cq_raw[:, k, :], scalar=gain("qa", k), in1=sq_cq[:, 0, :],
                                       op0=ALU.mult, op1=ALU.mult).then_inc(pre_n, 1)
            dve.wait_ge(pre_n, l * PRE_N + 4)
            V.tensor_copy(ckv_hi[:, :], ckv_raw[:, :]).then_inc(pre_n, 1)
            V.tensor_copy(cq_hi[:, :, :], cq_raw[:, :, :]).then_inc(pre_n, 1)
            dve.wait_ge(pre_n, l * PRE_N + 6)
            V.tensor_tensor(ckv_lo[:, :], ckv_raw[:, :], ckv_hi[:, :].bitcast(f32), ALU.subtract).then_inc(pre_n, 1)
            V.tensor_tensor(cq_lo[:, :, :], cq_raw[:, :, :], cq_hi[:, :, :].bitcast(f32), ALU.subtract).then_inc(pre_n, 1)
            dve.wait_ge(trig_done, 3)
            V.tensor_scalar(gcs[:, :], cs[:, :], gain("q_rope"), None, ALU.mult).then_inc(pre_n, 1)
            dve.wait_ge(filled[4], l * _layer(4, True) + 1)
            V.tensor_tensor(kpe[:, :], bank[4][64:P, :], cs[64:P, :], ALU.mult).then_inc(taken[4], 1)
            V.tensor_tensor(sq_kr[:, :], kr_raw[:, :], cs[0:64, :], ALU.mult).then_inc(pre_n, 1)
            dve.wait_ge(taken[4], l * _layer(4) + 2)
            dve.wait_ge(pre_n, l * PRE_N + 10)
            V.tensor_tensor(kpe[:, :], kpe[:, :], sq_kr[:, :], ALU.add).then_inc(pre_n, 1)
            dve.wait_ge(pre_n, l * PRE_N + 11)
            for r0 in (0, 64):
                V.tensor_copy(kpe_h[r0:r0 + ROPE, :], kpe[:, :]).then_inc(pre_n, 1)
            dve.wait_ge(pre_n, l * PRE_N + 13)
            for r0 in (0, 64):
                V.tensor_tensor(kpe_l[r0:r0 + ROPE, :], kpe[:, :], kpe_h[0:ROPE, :].bitcast(f32), ALU.subtract).then_inc(
                    pre_n, 1)
            dve.wait_ge(taken[7], l * _layer(7) + 2)
            V.memset(vmt[:, :, DV:DV + 1], 1.0).then_inc(pre_n, 1)

            with dve.Fori(0, HEADS) as i:
                dve.wait_ge(pre_n, l * PRE_N + PRE_N)
                it = l * HEADS + i
                A = l * ACC_L + i * 3 + A_HEAD

                def w_head_unit(j):
                    w_unit(dve, unit(l, B_HEAD, i, U_HEAD, j))

                w_head_unit(0)
                V.scalar_tensor_tensor(out=qsb[:, :], in0=bank[0][0:DK, :], scalar=DK ** -0.5, in1=rstd[0:DK, :],
                                       op0=ALU.mult, op1=ALU.mult).then_inc(q_s, 1)
                V.tensor_tensor(ksb[:, :], bank[0][DK:P, :], rstd[DK:P, :], ALU.mult).then_inc(taken[0], 1)
                w_filled(dve, l, i, "i_bc")
                dve.wait_ge(q_s, it + 1)
                V.tensor_tensor(qs[:, :], bank[7][0:DK, :], qsb[:, :], ALU.mult).then_inc(qs_s, 1)
                V.tensor_copy(sold[:, :], bank[7][0:DK, P - 1:SEQ:P]).then_inc(taken[7], 1)
                w_head_unit(1)
                V.tensor_tensor(vm_ch[:, :], bank[1][:, :], rstd[:, :], ALU.mult).then_inc(taken[1], 1)
                w_filled(dve, l, i, "k_tr")
                w_taken(dve, l, i, "m_bc")
                for c in range(TC):
                    V.tensor_scalar(kw[:, c, :], bank[6][:, c * DK:(c + 1) * DK], dec[:, c, P - 1:P], None, ALU.mult)\
                        .then_inc(taken[6] if c == TC - 1 else kw_s, 1)
                w_filled(dve, l, i, "s_t")
                w_taken(dve, l, i, "k_tr")
                V.tensor_tensor(dec[:, :, :], bank[7][:, :].rearrange("p (c t) -> p c t", t=P), dec[:, :, :], ALU.mult)\
                    .then_inc(taken[7], 1)
                w_head_unit(3)
                V.tensor_copy(v_ch[:, :], bank[5][:, :]).then_inc(taken[5], 1)
                w_filled(dve, l, i, "vm_tr")
                V.tensor_copy(vmt[:, :, 0:DV], bank[6][:, :].rearrange("p (c d) -> p c d", d=DV)).then_inc(taken[6], 1)
                for n, (sq, hi_, lo_) in enumerate(((nq[:, :], sq_hi[0][:, :], sq_lo[0][:, :]),
                                                    (nk[:, :], sq_hi[1][:, :], sq_lo[1][:, :]),
                                                    (nr[:, :], q_pe[0:ROPE, :], q_pe[ROPE:P, :]))):
                    dve.wait_ge(sq_s, it * 6 + (2 * n + 2))
                    V.scalar_tensor_tensor(out=lo_, in0=sq, scalar=EPS, in1=hi_.bitcast(f32), op0=ALU.add,
                                           op1=ALU.subtract).then_inc(sql_s, 1)
                V.tensor_tensor(ksb[:, :], bank[4][0:ROPE, :], gcs[0:ROPE, :], ALU.mult).then_inc(chain, 1)
                V.tensor_tensor(qsb[:, :], bank[4][ROPE:P, :], gcs[ROPE:P, :], ALU.mult).then_inc(taken[4], 1)
                dve.wait_ge(chain, it * CH + 1)
                w_taken(dve, l, i, "q_rope")
                V.tensor_tensor(ksb[:, :], ksb[:, :], qsb[:, :], ALU.add).then_inc(chain, 1)
                w_head_unit(4)
                V.tensor_tensor(so[:, :], bank[0][:, :], rstd[:, :], ALU.mult).then_inc(taken[0], 1)
                w_filled(dve, l, i, "c_loc")
                V.tensor_copy(csb[:, 0, :], bank[7][0:DK, 0:129]).then_inc(c_s, 1)
                for c in (1, 2):
                    dve.wait_ge(c_s, it * 2 + c)
                    V.scalar_tensor_tensor(out=csb[:, c, :], in0=csb[:, c - 1, :], scalar=sold[:, c:c + 1],
                                           in1=bank[7][0:DK, c * 129:(c + 1) * 129], op0=ALU.mult, op1=ALU.add)\
                        .then_inc(c_s if c == 1 else taken[7], 1)

                def refine(n, name, y):
                    rows = y.shape[0]
                    t = yy[n][0:rows, :]
                    dve.wait_ge(rs_s, it * 9 + (3 * n + 3))
                    V.scalar_tensor_tensor(out=t, in0=bank[USES[name][0]][0:rows, :], scalar=-0.5 / rows, in1=t,
                                           op0=ALU.mult, op1=ALU.mult).then_inc(taken[USES[name][0]], 1)
                    w_taken(dve, l, i, name)
                    V.scalar_tensor_tensor(out=y, in0=t, scalar=1.5, in1=y, op0=ALU.add, op1=ALU.mult).then_inc(chain, 1)
                    dve.wait_ge(chain, it * CH + (3 + n))

                for n, (b, y, name) in enumerate(((2, nq, "q_nope"), (3, nk, "k_nope"))):
                    refine(n, ("stat_q", "stat_k")[n], y[:, :])
                    V.scalar_tensor_tensor(out=y[:, :], in0=bank[b][:, :], scalar=gain(name), in1=y[:, :],
                                           op0=ALU.mult, op1=ALU.mult).then_inc(taken[b], 1)
                refine(2, "stat_r", nr[:, :])
                V.tensor_tensor(ksb[:, :], ksb[:, :], nr[:, :], ALU.mult).then_inc(chain, 1)
                dve.wait_ge(chain, it * CH + 6)
                V.tensor_copy(q_pe[0:ROPE, :], ksb[:, :]).then_inc(chain, 1)
                dve.wait_ge(chain, it * CH + 7)
                V.tensor_tensor(q_pe[ROPE:P, :], ksb[:, :], q_pe[0:ROPE, :].bitcast(f32), ALU.subtract).then_inc(qpe_s, 1)
                for n, (y, hi_, lo_) in enumerate(((nq, nq_hi, nq_lo), (nk, nk_hi, nk_lo))):
                    dve.wait_ge(nh_s, it * 2 + (n + 1))
                    V.tensor_tensor(lo_[:, :], y[:, :], hi_[:, :].bitcast(f32), ALU.subtract).then_inc(nrm_s, 1)
                w_head_unit(5)
                V.tensor_tensor(cb[:, :], bank[1][:, :], rstd[:, :], ALU.mult).then_inc(taken[1], 1)
                w_filled(dve, l, i, "num0")
                V.tensor_copy(sm[:, DEN, 0:2], bank[7][:, 128:258:129]).then_inc(fin_s, 1)
                w_filled(dve, l, i, "num1")
                V.tensor_copy(sm[:, DEN, 2:4], bank[6][:, 128:258:129]).then_inc(fin_s, 1)
                dve.wait_ge(fin_s, it * 8 + 2)
                V.scalar_tensor_tensor(out=sm[:, ADEN, :], in0=sm[:, DEN, :], scalar=-1.0, in1=sm[:, DEN, :],
                                       op0=ALU.mult, op1=ALU.max).then_inc(fin_s, 1)
                dve.wait_ge(fin_s, it * 8 + 3)
                V.tensor_tensor(sm[:, DD, :], sm[:, ADEN, :], emt[:, :, i], ALU.max).then_inc(fin_s, 1)
                dve.wait_ge(fin_s, it * 8 + 4)
                V.reciprocal(sm[:, RR, :], sm[:, DD, :]).then_inc(fin_s, 1)
                dve.wait_ge(fin_s, it * 8 + 5)
                V.tensor_tensor(sm[:, R2, :], sm[:, RR, :], sm[:, RR, :], ALU.mult).then_inc(fin_s, 1)
                dve.wait_ge(fin_s, it * 8 + 6)
                dve.wait_ge(ss_s, it * 4 + 4)
                V.tensor_tensor(sm[:, TT, :], sm[:, R2, :], sm[:, SS, :], ALU.mult).then_inc(fin_s, 1)
                w_head_unit(6)
                V.tensor_tensor(cc[:, :], bank[0][:, :], rstd[:, :], ALU.mult).then_inc(taken[0], 1)
                for qb in range(TC):
                    w_filled(dve, l, i, f"score{qb}")
                    V.reduce_max(sm[:, MX, qb:qb + 1], bank[2 + qb][:, 0:(qb + 1) * P], axis=AX.X).then_inc(mx_s, 1)
                dve.wait_ge(mx_s, it * 4 + 4)
                V.tensor_scalar(sm[:, NM, :], sm[:, MX, :], -(NOPE + ROPE) ** -0.5, None, ALU.mult).then_inc(nm_s, 1)
                for qb in range(TC):
                    w_taken(dve, l, i, f"score{qb}")
                V.reciprocal(sm[:, RINV, :], sm[:, SUM, :]).then_inc(rinv_s, 1)
                dve.wait_ge(rinv_s, it + 1)
                for qb in range(TC):
                    o = qb * (qb + 1) // 2 * P
                    V.tensor_scalar(prob[:, o:o + (qb + 1) * P], prob[:, o:o + (qb + 1) * P], sm[:, RINV, qb:qb + 1], None,
                                    ALU.mult).then_inc(p_s, 1)
                dve.wait_ge(hr_s, it * 2 + 2)
                V.tensor_tensor(sm[:, FF, :], sm[:, RR, :], sm[:, HR, :], ALU.mult).then_inc(fin_s, 1)
                dve.wait_ge(fin_s, it * 8 + 8)
                for c in range(TC):
                    b = 7 - c // 2
                    V.tensor_scalar(htok[:, c, :], bank[b][:, (c % 2) * 129:(c % 2) * 129 + DV], sm[:, FF, c:c + 1], None,
                                    ALU.mult).then_inc(taken[b] if c % 2 else h_s, 1)
                w_filled(dve, l, i, "pt2")
                V.tensor_copy(prob_t[:, 896:1280], bank[4][:, 0:384]).then_inc(taken[4], 1)
                head_rows(i + 1)
                w_filled(dve, l, i, "h_tr")
                dve.wait_ge(so_s, it + 1)
                V.scalar_tensor_tensor(out=ysB[:, i, :], in0=bank[7][:, :], scalar=par[:, bass.ds(i + PAR["head"], 1)],
                                       in1=so[:, :], op0=ALU.mult, op1=ALU.mult).then_inc(taken[7], 1)
                w_head_unit(7)
                V.tensor_tensor(zp[:, 2:SEQ + 2], bank[1][:, :], rstd[:, :], ALU.mult).then_inc(taken[1], 1)
                w_acc(dve, 1, A + 2)
                w_acc(dve, 0, A + 2)
                V.tensor_tensor(zp[:, 2:SEQ + 2], zp[:, 2:SEQ + 2], cc[:, :], ALU.mult).then_inc(conv_s, 1)
                dve.wait_ge(conv_s, it * 5 + 1)
                for j in range(3):
                    w = par[:, bass.ds(i * 3 + (PAR["conv"] + j), 1)]
                    if j == 0:
                        V.tensor_scalar(cc[:, :], zp[:, 0:SEQ], w, None, ALU.mult).then_inc(conv_s, 1)
                    else:
                        V.scalar_tensor_tensor(out=cc[:, :], in0=zp[:, j:j + SEQ], scalar=w, in1=cc[:, :],
                                               op0=ALU.mult, op1=ALU.add).then_inc(conv_s, 1)
                    dve.wait_ge(conv_s, it * 5 + 2 + j)
                V.tensor_tensor(ysA[:, i, :], cb[:, :], cc[:, :], ALU.mult).then_inc(conv_s, 1)

            dve.wait_ge(conv_s, (l + 1) * HEADS * 5)
            dve.wait_ge(taken[5], (l + 1) * _layer(5) + 1)
            for n, ys in enumerate((ysA, ysB, ysC)):
                if n:
                    w_unit(dve, unit(l, B_MERGE + n * U_MERGE - 1))
                for k in range(KT):
                    dve.wait_ge(act_h, (l * 7 + n) * KT + k + 1)
                    V.tensor_tensor(act_lo[:, k, :], ys[:, k, :], act_hi[:, k, :].bitcast(f32), ALU.subtract).then_inc(act_s, 1)
                with dve.Fori(0, 4) as i:
                    dve.wait_ge(act_s, (l * 7 + n + 1) * KT)
                    for j in range(2):
                        a = l * ACC_L + i * 2 + (A_MERGE + n * 8 + j)
                        m = l * 3 * KT + i * 2 + (n * KT + j)
                        g = gsig[j]
                        mk = merged[:, i * 2 + j, :]
                        w_unit(dve, unit(l, B_MERGE + n * U_MERGE, i, 4, 2 * j))
                        V.tensor_tensor(g[:, :], bank[0][:, :], rstd[:, :], ALU.mult).then_inc(taken[0], 1)
                        w_unit(dve, unit(l, B_MERGE + n * U_MERGE, i, 4, 2 * j + 1))
                        dve.wait_ge(g_s, m + 1)
                        V.tensor_tensor(mk if n == 0 else ev_n[:, :], bank[1][:, :], g[:, :], ALU.mult).then_inc(taken[1], 1)
                        if n:
                            w_acc(dve, 1, a)
                            V.tensor_tensor(mk, mk, ev_n[:, :], ALU.add).then_inc(mg_a, 1)
                        if n == 2:
                            dve.wait_ge(mg_a, l * 2 * KT + i * 2 + (KT + j + 1))
                            V.tensor_copy(mg_hi[:, i * 2 + j, :], mk).then_inc(mg_h, 1)
                            dve.wait_ge(mg_h, l * KT + i * 2 + (j + 1))
                            V.tensor_tensor(mg_lo[:, i * 2 + j, :], mk, mg_hi[:, i * 2 + j, :].bitcast(f32), ALU.subtract)\
                                .then_inc(mg_s, 1)
            for k in range(KT):
                w_unit(dve, unit(l, B_OUT, j=k))
                V.tensor_tensor(xT[:, k, :], xT[:, k, :], bank[k % 2][:, :], ALU.add).then_inc(taken[k % 2], 1)
                w_acc(dve, k % 2, l * ACC_L + (A_OUT + k // 2))
                split_x(l * 2 + 1, k, gain("mlp", k))
            newton(l, 1)
            def up(g):
                dve.wait_ge(nw, l * 8 + 8)
                for k in range(KT):
                    a = l * ACC_L + g * 8 + (A_MLP + k // 2)
                    m = l * 4 * KT + g * KT + (k + 1)
                    w_unit(dve, unit(l, B_MLP, g, U_MLP, k))
                    V.tensor_tensor(ev_t[:, :], bank[k % 2][:, :], rstd[:, :], ALU.mult).then_inc(taken[k % 2], 1)
                    w_acc(dve, k % 2, a)
                    V.scalar_tensor_tensor(out=ev_r[:, :], in0=ev_t[:, :], scalar=0.0, in1=ev_t[:, :],
                                           op0=ALU.max, op1=ALU.mult).then_inc(act_a, 1)
                    dve.wait_ge(act_a, m)
                    V.tensor_copy(act_hi[:, k, :], ev_r[:, :]).then_inc(act_h, 1)
                    dve.wait_ge(act_h, l * 7 * KT + g * KT + (3 * KT + k + 1))
                    V.tensor_tensor(act_lo[:, k, :], ev_r[:, :], act_hi[:, k, :].bitcast(f32), ALU.subtract).then_inc(act_s, 1)

            with dve.Fori(0, FG - 1) as g:
                up(g)
                for k in range(KT):
                    w_unit(dve, unit(l, B_MLP, g, U_MLP, KT + k))
                    V.tensor_tensor(xT[:, k, :], xT[:, k, :], bank[k % 2][:, :], ALU.add).then_inc(taken[k % 2], 1)
            up(FG - 1)
            for k in range(KT):
                w_unit(dve, unit(l, B_MLP, FG - 1, U_MLP, KT + k))
                V.tensor_tensor(xT[:, k, :], xT[:, k, :], bank[k % 2][:, :], ALU.add).then_inc(taken[k % 2], 1)
                with dve.If(l < DEPTH - 1):
                    w_acc(dve, k % 2, l * ACC_L + (ACC_L - KT // 2 + k // 2))
                    split_x(l * 2 + 2, k, gain("mix_next", k))

        for k in range(0, KT, 2):
            dve.wait_ge(xt_filled, KT + k + 1)
            V.tensor_copy(out_tok[:, :, k * P:(k + 1) * P], bank[2 + k % 6][:, :].rearrange("p (c d) -> p c d", d=P))\
                .then_inc(ot[0], 1)

    ctx.close()


def unit_columns(w, c0, width=P):
    rows = w.shape[0]
    return w[:, c0:c0 + width].reshape(rows // P, P, width).transpose(1, 0, 2).reshape(P, rows // P * width)


def weight_stream(w_in, w_uq, w_ukv, w_branch, w_out, w_up, w_down):
    stream = np.zeros((DEPTH * UNITS, P, 1024), np.float32)
    at = 0

    def put(*blocks):
        nonlocal at
        o = 0
        for b in blocks:
            stream[at, :, o:o + b.shape[1]] = b
            o += b.shape[1]
        at += 1

    for l in range(DEPTH):
        kif = np.concatenate([w_in[l][:, C_KR:C_KR + 64], w_in[l][:, C_MI:C_MI + 32], w_in[l][:, C_MF:C_MF + 32]], axis=1)
        put(unit_columns(kif, 0))
        put(unit_columns(w_in[l], C_CKV))
        for k in range(2):
            put(unit_columns(w_in[l], C_CQ + k * P))
        for h in range(HEADS):
            qk = np.concatenate([w_in[l][:, C_MQ + h * DK:C_MQ + (h + 1) * DK], w_in[l][:, C_MK + h * DK:C_MK + (h + 1) * DK]],
                                axis=1)
            put(unit_columns(qk, 0))
            put(unit_columns(w_in[l], C_MV + h * P))
            q0 = h * (NOPE + ROPE)
            r0 = q0 + NOPE
            rows = [w_uq[l][k * P:(k + 1) * P] for k in range(2)]
            put(*[np.concatenate([r[:, q0:r0 + ROPE], r[:, r0 + ROPE // 2:r0 + ROPE], r[:, r0:r0 + ROPE // 2]], axis=1)
                  for r in rows])
            put(w_ukv[l][:, h * 2 * P:(h + 1) * 2 * P])
            put(unit_columns(w_in[l], C_MO + h * P))
            for c in (C_CB, C_CC, C_CU):
                put(unit_columns(w_in[l], c + h * P))
        for n in range(3):
            for d in range(KT):
                put(unit_columns(w_in[l], C_GATE + n * D_MODEL + d * P))
                put(unit_columns(w_branch[l, n], d * P))
        for d in range(KT):
            put(unit_columns(w_out[l], d * P))
        for g in range(FG):
            for j in range(KT):
                put(unit_columns(w_up[l], (g * KT + j) * P))
            for d in range(KT):
                put(unit_columns(w_down[l][g * D_MODEL:(g + 1) * D_MODEL], d * P))
    assert at == DEPTH * UNITS
    return stream


def tiles(v):
    return v.reshape(-1, P).T


def kernel(x, positions, mix_norm, w_in, conv_w, mlstm_igate_bias, mlstm_fgate_bias, mlstm_head_norm,
           mla_q_a_norm, mla_w_uq, mla_kv_a_norm, mla_w_ukv, mla_q_norm, mla_k_norm, w_branch, w_out,
           mlp_norm, w_up, w_down):
    import concourse.bacc as bacc
    from concourse.bass_utils import run_bass_kernel_spmd

    par = np.zeros((DEPTH, P, NPAR), np.float32)
    for l in range(DEPTH):
        def put(name, block, row=0):
            par[l, row:row + block.shape[0], PAR[name]:PAR[name] + block.shape[1]] = block

        put("mix_next", tiles(mix_norm[min(l + 1, DEPTH - 1)]))
        put("mlp", tiles(mlp_norm[l]))
        put("conv", conv_w[l].reshape(3, KT, P).transpose(2, 1, 0).reshape(P, KT * 3))
        put("head", tiles(mlstm_head_norm[l]))
        put("qa", tiles(mla_q_a_norm[l]))
        put("kva", tiles(mla_kv_a_norm[l]))
        put("q_nope", mla_q_norm[l][:NOPE, None])
        put("k_nope", mla_k_norm[l][:NOPE, None])
        put("q_rope", mla_q_norm[l][NOPE:, None])
        put("q_rope", mla_q_norm[l][NOPE + ROPE // 2:, None], 64)
        put("q_rope", mla_q_norm[l][NOPE:NOPE + ROPE // 2, None], 96)
        put("k_rope", mla_k_norm[l][NOPE:, None])
        put("b_i", mlstm_igate_bias[l][:, None])
        put("b_f", mlstm_fgate_bias[l][:, None])

    cst = np.zeros((P, NCST), np.float32)
    r = np.arange(P)
    cst[:, CST["ident"]:CST["ident"] + P] = np.eye(P)
    masks = np.zeros((P, 2, P), np.float32)
    masks[:, 0] = np.where(r[:, None] > r[None, :], BIG, 0)
    masks[:, 1] = np.where(r[None, :] > r[:, None], -BIG, 0)
    for d in range(ROPE):
        cst[(d + ROPE // 2) % ROPE, CST["swap"] + ROPE + d] = 1
    for h in range(HEADS):
        cst[h::32, CST["onehot"] + h] = 1
    freq = (10000.0 ** (-np.arange(0, ROPE, 2) / ROPE)).astype(np.float32)
    cst[:, CST["freq"]] = freq[r % (ROPE // 2)]
    cst[:, CST["sign"]] = np.where(r % ROPE < ROPE // 2, -1, 1)
    cst[:, CST["mix0"]:CST["mix0"] + KT] = tiles(mix_norm[0])

    arrays = {
        "x": np.ascontiguousarray(x[0]),
        "positions": np.ascontiguousarray(positions[0]),
        "wstream": weight_stream(w_in, mla_w_uq, mla_w_ukv, w_branch, w_out, w_up, w_down),
        "par": par,
        "cst": cst,
        "masks": masks,
    }
    nc = bacc.Bacc("TRN2", target_bir_lowering=False, num_devices=1)
    args = [nc.dram_tensor(n, a.shape, mybir.dt.from_np(a.dtype), kind="ExternalInput").ap() for n, a in arrays.items()]
    out = nc.dram_tensor("out", (SEQ, D_MODEL), mybir.dt.float32, kind="ExternalOutput").ap()
    build_trunk(nc, *args, out)
    result = run_bass_kernel_spmd(nc, [arrays], core_ids=[0])
    return result.results[0]["out"].reshape(1, SEQ, D_MODEL)
```
